# Optimizing a Trainium2 kernel written in Bass

```python
import jax, jax.numpy as jnp
from jax import lax
import numpy as np
import math

D_MODEL = 1024
BATCH = 1
SEQ = 512
DEPTH = 1

GRID_W = 64
CTX_LEN = 256
GLA_HEADS = 4
GLA_DK = 64
GLA_DV = 128
GLA_WIDTH = GLA_HEADS * GLA_DV
GATE_RANK = 16
GATE_NORMALIZER = 16.0
CHUNK = 64
POOL_WINDOWS = (2, 4, 8, 16)
POOL_GROUP = 128
POOL_WIDTH = POOL_GROUP * len(POOL_WINDOWS)
MIX_WIDTH = GLA_WIDTH + POOL_WIDTH
Q_COLS = GLA_HEADS * GLA_DK
K_COLS = GLA_HEADS * GLA_DK
V_COLS = GLA_WIDTH
G_COLS = GLA_WIDTH
A_COLS = 2 * GATE_RANK
P_COLS = POOL_WIDTH
OFF_K = Q_COLS
OFF_V = OFF_K + K_COLS
OFF_G = OFF_V + V_COLS
OFF_A = OFF_G + G_COLS
OFF_P = OFF_A + A_COLS
IN_COLS = OFF_P + P_COLS
N_GROUPS = 4
EXPERTS_PER_GROUP = 8
N_EXPERTS = N_GROUPS * EXPERTS_PER_GROUP
TOP_K_INNER = 2
D_EXPERT = 256
EPS = 1e-6


def rmsnorm(x, g):
    xf = x.astype(jnp.float32)
    y = xf * lax.rsqrt(jnp.mean(xf * xf, axis=-1, keepdims=True) + EPS)
    return (y * g).astype(x.dtype)

def modulate(h, shift, scale):
    return h * (1.0 + scale) + shift

def flip(t):
    return jnp.flip(t, axis=1)

def split_heads_qkv(q, k, v):
    B, L, _ = q.shape
    q = q.reshape(B, L, GLA_HEADS, GLA_DK) * (GLA_DK ** -0.5)
    k = k.reshape(B, L, GLA_HEADS, GLA_DK)
    v = v.reshape(B, L, GLA_HEADS, GLA_DV)
    return q, k, v

def log_decay(a_low, w_dec, b_dec):
    B, L, _ = a_low.shape
    a = a_low.reshape(B, L, 2, GATE_RANK).astype(jnp.float32)
    la = jax.nn.log_sigmoid(jnp.einsum('bldr,drk->bldk', a, w_dec) + b_dec) / GATE_NORMALIZER
    la = la.reshape(B, L, 2, GLA_HEADS, GLA_DK)
    return la[:, :, 0], la[:, :, 1]

def gla_state(k, v, la, s0):
    B, L, H, dk = k.shape
    dv = v.shape[-1]
    N = L // CHUNK
    kc = k.reshape(B, N, CHUNK, H, dk).astype(jnp.float32)
    vc = v.reshape(B, N, CHUNK, H, dv)
    b = jnp.cumsum(la.reshape(B, N, CHUNK, H, dk), axis=2)
    b_last = b[:, :, -1]
    k_st = kc * jnp.exp(b_last[:, :, None] - b)
    d_state = jnp.einsum('bnchd,bnche->nbhde', k_st, vc)
    decay = jnp.exp(b_last).transpose(1, 0, 2, 3)

    def step(S, inp):
        d, ds = inp
        return d[..., None] * S + ds, S

    s_fin, s_prev = lax.scan(step, s0, (decay, d_state))
    return s_prev, s_fin, b

def gla_chunked(q, k, v, la, s0):
    s_prev, s_fin, b = gla_state(k, v, la, s0)
    B, L, H, dk = q.shape
    dv = v.shape[-1]
    N = L // CHUNK
    qb = q.reshape(B, N, CHUNK, H, dk).astype(jnp.float32) * jnp.exp(b)
    kb = k.reshape(B, N, CHUNK, H, dk).astype(jnp.float32) * jnp.exp(-b)
    vc = v.reshape(B, N, CHUNK, H, dv)
    mask = jnp.tril(jnp.ones((CHUNK, CHUNK), dtype=bool))
    scores = jnp.where(mask, jnp.einsum('bnihd,bnjhd->bnhij', qb, kb), 0.0)
    o = jnp.einsum('bnhij,bnjhe->bnihe', scores, vc) + jnp.einsum('bnihd,nbhde->bnihe', qb, s_prev)
    return o.reshape(B, L, H, dv), s_fin

def gla_bidirectional(q, k, v, la_f, la_b, s0_f, s0_b):
    o_f, s_f = gla_chunked(q, k, v, la_f, s0_f)
    o_b, s_b = gla_chunked(flip(q), flip(k), flip(v), flip(la_b), s0_b)
    return o_f + flip(o_b), s_f, s_b

def window_mean(x, w, axis):
    n = x.shape[axis]
    lo = w // 2
    hi = w - 1 - lo
    cs = jnp.cumsum(x.astype(jnp.float32), axis=axis)
    pad = [(0, 0)] * x.ndim
    pad[axis] = (1, 0)
    cs = jnp.pad(cs, pad)
    idx = np.arange(n)
    start = np.clip(idx - lo, 0, n)
    end = np.clip(idx + hi + 1, 0, n)
    s = jnp.take(cs, jnp.asarray(end), axis=axis) - jnp.take(cs, jnp.asarray(start), axis=axis)
    cshape = [1] * x.ndim
    cshape[axis] = n
    cnt = jnp.asarray((end - start).astype(np.float32).reshape(cshape))
    return s / cnt

def pool_mixer(p, w_pool, pool_scale, rows):
    B, L, _ = p.shape
    groups = p.reshape(B, L, len(POOL_WINDOWS), POOL_GROUP)
    outs = []
    for gi, w in enumerate(POOL_WINDOWS):
        xg = groups[:, :, gi]
        if rows is None:
            m = window_mean(xg, w, 1)
        else:
            xg2 = xg.reshape(B, rows, GRID_W, POOL_GROUP)
            m = window_mean(window_mean(xg2, w, 2), w, 1).reshape(B, L, POOL_GROUP)
        outs.append(m - xg)
    y = jnp.stack(outs, axis=2)
    y = jnp.einsum('blgc,gcd->blgd', y, w_pool).reshape(B, L, POOL_WIDTH)
    return y * pool_scale

def token_mixer(h, w_in, w_dec, b_dec, gla_norm_g, w_pool, pool_scale, w_out, s0_f, s0_b, rows):
    B, L, _ = h.shape
    proj = h @ w_in
    q, k, v, g, a_low, p = jnp.split(proj, [OFF_K, OFF_V, OFF_G, OFF_A, OFF_P], axis=-1)
    q, k, v = split_heads_qkv(q, k, v)
    la_f, la_b = log_decay(a_low, w_dec, b_dec)
    o, s_f, s_b = gla_bidirectional(q, k, v, la_f, la_b, s0_f, s0_b)
    o = rmsnorm(o, gla_norm_g).reshape(B, L, GLA_WIDTH) * jax.nn.silu(g)
    pooled = pool_mixer(p, w_pool, pool_scale, rows)
    out = jnp.concatenate([o, pooled.astype(o.dtype)], axis=-1) @ w_out
    return out, s_f, s_b

def context_states(h, w_in, w_dec, b_dec):
    B, L, _ = h.shape
    kv = h @ w_in[:, OFF_K:OFF_G]
    a_low = h @ w_in[:, OFF_A:OFF_P]
    k = kv[..., :K_COLS].reshape(B, L, GLA_HEADS, GLA_DK)
    v = kv[..., K_COLS:].reshape(B, L, GLA_HEADS, GLA_DV)
    la_f, la_b = log_decay(a_low, w_dec, b_dec)
    s0 = jnp.zeros((B, GLA_HEADS, GLA_DK, GLA_DV), jnp.float32)
    _, s_f, _ = gla_state(k, v, la_f, s0)
    _, s_b, _ = gla_state(flip(k), flip(v), flip(la_b), s0)
    return s_f, s_b

def hier_moe(h, w_rg, w_re, w_e_in, w_e_out):
    B, L, D = h.shape
    t = h.reshape(-1, D)
    pg = jax.nn.softmax((t @ w_rg).astype(jnp.float32), axis=-1)
    gp, gi = lax.top_k(pg, 1)
    le = (t @ w_re).astype(jnp.float32).reshape(-1, N_GROUPS, EXPERTS_PER_GROUP)
    le = jnp.take_along_axis(le, gi[:, :, None], axis=1)[:, 0]
    ew, ei = lax.top_k(jax.nn.softmax(le, axis=-1), TOP_K_INNER)
    ew = ew / jnp.sum(ew, axis=-1, keepdims=True)
    weights = gp * ew
    eid = gi * EXPERTS_PER_GROUP + ei
    gates = jnp.einsum('tk,tke->et', weights, jax.nn.one_hot(eid, N_EXPERTS, dtype=jnp.float32))

    def body(acc, inp):
        wi, wo, ge = inp
        a, u = jnp.split(t @ wi, 2, axis=-1)
        return acc + ((jax.nn.silu(a) * u) @ wo) * ge[:, None], None

    y, _ = lax.scan(body, jnp.zeros(t.shape, jnp.float32), (w_e_in, w_e_out, gates))
    return y.reshape(B, L, D).astype(h.dtype)

def first_inputs(seed: int = 0) -> dict:
    key = jax.random.key(seed)
    ks = jax.random.split(key, 24)
    f32 = jnp.float32

    def nrm(k, shape, s):
        return jax.random.normal(k, shape, f32) * s

    D = D_MODEL
    return {
        "x": nrm(ks[0], (BATCH, SEQ, D), 1.0),
        "c": nrm(ks[1], (BATCH, D), 1.0),
        "ctx": nrm(ks[2], (BATCH, CTX_LEN, D), 1.0),
        "c_ctx": nrm(ks[3], (D,), 1.0),
        "w_ada": nrm(ks[4], (DEPTH, D, 6 * D), D ** -0.5),
        "b_ada": nrm(ks[5], (DEPTH, 6 * D), 0.02),
        "norm1_g": 1.0 + nrm(ks[6], (DEPTH, D), 0.02),
        "w_in": nrm(ks[7], (DEPTH, D, IN_COLS), D ** -0.5),
        "w_decay": nrm(ks[8], (DEPTH, 2, GATE_RANK, GLA_HEADS * GLA_DK), GATE_RANK ** -0.5),
        "b_decay": nrm(ks[9], (DEPTH, 2, GLA_HEADS * GLA_DK), 0.1),
        "gla_norm_g": 1.0 + nrm(ks[10], (DEPTH, GLA_DV), 0.02),
        "w_pool": nrm(ks[11], (DEPTH, len(POOL_WINDOWS), POOL_GROUP, POOL_GROUP), POOL_GROUP ** -0.5),
        "pool_scale": 1.0 + nrm(ks[12], (DEPTH, POOL_WIDTH), 0.02),
        "w_out": nrm(ks[13], (DEPTH, MIX_WIDTH, D), MIX_WIDTH ** -0.5),
        "norm2_g": 1.0 + nrm(ks[14], (DEPTH, D), 0.02),
        "w_router_group": nrm(ks[15], (DEPTH, D, N_GROUPS), D ** -0.5),
        "w_router_expert": nrm(ks[16], (DEPTH, D, N_EXPERTS), D ** -0.5),
        "w_expert_in": nrm(ks[17], (DEPTH, N_EXPERTS, D, 2 * D_EXPERT), D ** -0.5),
        "w_expert_out": nrm(ks[18], (DEPTH, N_EXPERTS, D_EXPERT, D), D_EXPERT ** -0.5),
        "final_norm_g": 1.0 + nrm(ks[19], (D,), 0.02),
    }

def first_block(x, c, ctx, c_ctx, w_ada, b_ada, norm1_g, w_in, w_decay, b_decay, gla_norm_g, w_pool,
              pool_scale, w_out, norm2_g, w_router_group, w_router_expert, w_expert_in, w_expert_out,
              final_norm_g):
    rows = x.shape[1] // GRID_W
    xc = ctx
    for i in range(DEPTH):
        mod = jax.nn.silu(c) @ w_ada[i] + b_ada[i]
        sh_a, sc_a, gt_a, sh_m, sc_m, gt_m = jnp.split(mod[:, None, :], 6, axis=-1)
        mod_c = jax.nn.silu(c_ctx) @ w_ada[i] + b_ada[i]
        csh_a, csc_a, cgt_a, csh_m, csc_m, cgt_m = jnp.split(mod_c, 6, axis=-1)

        hc = modulate(rmsnorm(xc, norm1_g[i]), csh_a, csc_a)
        if i + 1 < DEPTH:
            zero_s = jnp.zeros((xc.shape[0], GLA_HEADS, GLA_DK, GLA_DV), jnp.float32)
            out_c, s_f, s_b = token_mixer(hc, w_in[i], w_decay[i], b_decay[i], gla_norm_g[i], w_pool[i],
                                          pool_scale[i], w_out[i], zero_s, zero_s, None)
            xc_next = xc + (cgt_a * out_c).astype(xc.dtype)
            hc2 = modulate(rmsnorm(xc_next, norm2_g[i]), csh_m, csc_m)
            xc_next = xc_next + (cgt_m * hier_moe(hc2, w_router_group[i], w_router_expert[i],
                                                  w_expert_in[i], w_expert_out[i])).astype(xc.dtype)
        else:
            s_f, s_b = context_states(hc, w_in[i], w_decay[i], b_decay[i])
            xc_next = xc

        h = modulate(rmsnorm(x, norm1_g[i]), sh_a, sc_a)
        out, _, _ = token_mixer(h, w_in[i], w_decay[i], b_decay[i], gla_norm_g[i], w_pool[i],
                                pool_scale[i], w_out[i], s_f, s_b, rows)
        x = x + (gt_a * out).astype(x.dtype)
        h2 = modulate(rmsnorm(x, norm2_g[i]), sh_m, sc_m)
        x = x + (gt_m * hier_moe(h2, w_router_group[i], w_router_expert[i],
                                 w_expert_in[i], w_expert_out[i])).astype(x.dtype)
        xc = xc_next
    return rmsnorm(x, final_norm_g)


DEPTH_2 = 2

N_A_LAYERS = DEPTH_2 // 2
N_B_LAYERS = DEPTH_2 - N_A_LAYERS

GDN_HEADS = 8
GDN_DK = 128
GDN_DV = 128
GDN_KDIM = GDN_HEADS * GDN_DK
GDN_VDIM = GDN_HEADS * GDN_DV
QKV_DIM = 2 * GDN_KDIM + GDN_VDIM
GDN_PROJ_DIM = QKV_DIM + GDN_VDIM + 2 * GDN_HEADS
CONV_WIDTH = 4

SB_HEADS = 8
SB_DH = D_MODEL // SB_HEADS
SB_DIM = SB_HEADS * SB_DH
Q_BLOCK = 128

D_FF = -(-8 * D_MODEL // (3 * 256)) * 256


def rms_norm(x, gain):
    xf = x.astype(jnp.float32)
    y = xf * lax.rsqrt(jnp.mean(xf * xf, axis=-1, keepdims=True) + EPS)
    return (y * gain.astype(jnp.float32)).astype(x.dtype)

def l2_norm(x):
    xf = x.astype(jnp.float32)
    return xf * lax.rsqrt(jnp.sum(xf * xf, axis=-1, keepdims=True) + EPS)

def causal_depthwise_conv(x, w):
    c = x.shape[-1]
    return lax.conv_general_dilated(
        x, w[:, None, :].astype(x.dtype), window_strides=(1,),
        padding=[(CONV_WIDTH - 1, 0)], dimension_numbers=('NWC', 'WIO', 'NWC'),
        feature_group_count=c)

def swiglu(x, w_gu, w_down):
    g, u = jnp.split(x @ w_gu, 2, axis=-1)
    return (jax.nn.silu(g) * u) @ w_down

def gated_delta_rule(q, k, v, beta, g):
    b_, h_, s_, dk = q.shape
    dv = v.shape[-1]
    n = s_ // CHUNK
    q = (q * dk ** -0.5).reshape(b_, h_, n, CHUNK, dk)
    k = k.reshape(b_, h_, n, CHUNK, dk)
    v = v.reshape(b_, h_, n, CHUNK, dv)
    beta = beta.reshape(b_, h_, n, CHUNK)
    g_cum = jnp.cumsum(g.reshape(b_, h_, n, CHUNK), axis=-1)

    idx = jnp.arange(CHUNK)
    incl = idx[:, None] >= idx[None, :]
    strict = idx[:, None] > idx[None, :]
    decay = jnp.exp(jnp.where(incl, g_cum[..., :, None] - g_cum[..., None, :], -jnp.inf))

    k_beta = k * beta[..., None]
    a_low = jnp.where(strict, jnp.einsum('bhncd,bhnsd->bhncs', k_beta, k) * decay, 0.0)
    eye = jnp.eye(CHUNK, dtype=q.dtype)
    rhs = jnp.concatenate([v * beta[..., None], k_beta * jnp.exp(g_cum)[..., None]], axis=-1)
    sol = lax.linalg.triangular_solve(eye + a_low, rhs, left_side=True, lower=True,
                                      unit_diagonal=True)
    u, w = sol[..., :dv], sol[..., dv:]

    attn_intra = jnp.einsum('bhncd,bhnsd->bhncs', q, k) * decay
    g_last = g_cum[..., -1]
    k_decay = k * jnp.exp(g_last[..., None] - g_cum)[..., None]
    q_decay = q * jnp.exp(g_cum)[..., None]

    def step(state, inp):
        qd, kd, ui, wi, ai, gl = inp
        v_new = ui - jnp.einsum('bhck,bhkv->bhcv', wi, state)
        o = (jnp.einsum('bhck,bhkv->bhcv', qd, state)
             + jnp.einsum('bhcs,bhsv->bhcv', ai, v_new))
        state = state * jnp.exp(gl)[..., None, None] + jnp.einsum('bhck,bhcv->bhkv', kd, v_new)
        return state, o

    xs = tuple(jnp.moveaxis(t, 2, 0) for t in (q_decay, k_decay, u, w, attn_intra, g_last))
    state0 = jnp.zeros((b_, h_, dk, dv), q.dtype)
    _, o = lax.scan(step, state0, xs)
    return jnp.moveaxis(o, 0, 2).reshape(b_, h_, s_, dv)

def gdn_mixer(hn, w_in, conv_w, a_log, dt_bias, o_gain, w_out):
    b_, s_, _ = hn.shape
    f32 = jnp.float32
    proj = hn @ w_in
    qkv, z, b_raw, a_raw = jnp.split(
        proj, [QKV_DIM, QKV_DIM + GDN_VDIM, QKV_DIM + GDN_VDIM + GDN_HEADS], axis=-1)
    qkv = jax.nn.silu(causal_depthwise_conv(qkv, conv_w))
    q, k, v = jnp.split(qkv, [GDN_KDIM, 2 * GDN_KDIM], axis=-1)

    def heads(t, d):
        return t.reshape(b_, s_, GDN_HEADS, d).transpose(0, 2, 1, 3)

    q = l2_norm(heads(q, GDN_DK))
    k = l2_norm(heads(k, GDN_DK))
    v = heads(v, GDN_DV).astype(f32)
    beta = jax.nn.sigmoid(b_raw.astype(f32)).transpose(0, 2, 1)
    g = (-jnp.exp(a_log.astype(f32))
         * jax.nn.softplus(a_raw.astype(f32) + dt_bias.astype(f32))).transpose(0, 2, 1)
    o = gated_delta_rule(q, k, v, beta, g).transpose(0, 2, 1, 3)
    zf = z.reshape(b_, s_, GDN_HEADS, GDN_DV).astype(f32)
    o = rms_norm(o, o_gain) * jax.nn.silu(zf)
    return o.reshape(b_, s_, GDN_VDIM).astype(hn.dtype) @ w_out

def shared_kv(h, kv_norm, w_kv, k_gain):
    b_, s_, _ = h.shape
    k, v = jnp.split(rms_norm(h, kv_norm) @ w_kv, 2, axis=-1)
    k = rms_norm(k.reshape(b_, s_, SB_HEADS, SB_DH), k_gain).transpose(0, 2, 1, 3)
    v = v.reshape(b_, s_, SB_HEADS, SB_DH).transpose(0, 2, 1, 3)
    return k, v

def stick_breaking_attention(q, k, v):
    _, _, s_, dh = q.shape
    f32 = jnp.float32
    scale = dh ** -0.5
    outs = []
    for blk in range(s_ // Q_BLOCK):
        t0 = blk * Q_BLOCK
        end = t0 + Q_BLOCK
        qb = q[:, :, t0:end].astype(f32)
        kb = k[:, :, :end].astype(f32)
        vb = v[:, :, :end].astype(f32)
        z = jnp.einsum('bhtd,bhsd->bhts', qb, kb) * scale
        t_idx = t0 + jnp.arange(Q_BLOCK)
        s_idx = jnp.arange(end)
        causal = s_idx[None, :] < t_idx[:, None]
        ls_neg = jax.nn.log_sigmoid(-z)
        log_fail = jnp.where(causal, ls_neg, 0.0)
        log_rest = lax.cumsum(log_fail, axis=3, reverse=True) - log_fail
        log_a = z + ls_neg + log_rest
        att = jnp.where(causal, jnp.exp(log_a), 0.0)
        outs.append(jnp.einsum('bhts,bhsd->bhtd', att, vb))
    return jnp.concatenate(outs, axis=2).astype(q.dtype)

def sb_mixer(hn, k_sh, v_sh, w_q, q_gain, w_out):
    b_, s_, _ = hn.shape
    q = rms_norm((hn @ w_q).reshape(b_, s_, SB_HEADS, SB_DH), q_gain).transpose(0, 2, 1, 3)
    o = stick_breaking_attention(q, k_sh, v_sh)
    return o.transpose(0, 2, 1, 3).reshape(b_, s_, SB_DIM).astype(hn.dtype) @ w_out

def second_inputs(seed: int = 0) -> dict:
    key = jax.random.key(seed)
    ks = jax.random.split(key, 17)
    f32 = jnp.float32

    def dense(k, shape, fan_in, scale=1.0):
        return jax.random.normal(k, shape, f32) * (scale * fan_in ** -0.5)

    def gain(k, shape):
        return 1.0 + 0.02 * jax.random.normal(k, shape, f32)

    out_scale = (2 * DEPTH_2) ** -0.5
    x = jax.random.normal(ks[0], (BATCH, SEQ, D_MODEL), f32)
    attn_norm = gain(ks[1], (DEPTH_2, D_MODEL))
    ffn_norm = gain(ks[2], (DEPTH_2, D_MODEL))
    gdn_w_in = dense(ks[3], (N_A_LAYERS, D_MODEL, GDN_PROJ_DIM), D_MODEL)
    gdn_conv_w = jax.random.normal(ks[4], (N_A_LAYERS, CONV_WIDTH, QKV_DIM), f32) * CONV_WIDTH ** -0.5
    gdn_a_log = jnp.log(jax.random.uniform(ks[5], (N_A_LAYERS, GDN_HEADS), f32, 1.0, 16.0))
    dt = jnp.exp(jax.random.uniform(ks[6], (N_A_LAYERS, GDN_HEADS), f32,
                                    math.log(1e-3), math.log(1e-1)))
    gdn_dt_bias = dt + jnp.log(-jnp.expm1(-dt))
    gdn_o_gain = gain(ks[7], (N_A_LAYERS, GDN_DV))
    gdn_w_out = dense(ks[8], (N_A_LAYERS, GDN_VDIM, D_MODEL), GDN_VDIM, out_scale)
    kv_norm = gain(ks[9], (D_MODEL,))
    w_kv = dense(ks[10], (D_MODEL, 2 * SB_DIM), D_MODEL)
    k_gain = gain(ks[11], (SB_DH,))
    sb_w_q = dense(ks[12], (N_B_LAYERS, D_MODEL, SB_DIM), D_MODEL)
    sb_q_gain = gain(ks[13], (N_B_LAYERS, SB_DH))
    sb_w_out = dense(ks[14], (N_B_LAYERS, SB_DIM, D_MODEL), SB_DIM, out_scale)
    ffn_w_gu = dense(ks[15], (DEPTH_2, D_MODEL, 2 * D_FF), D_MODEL)
    ffn_w_down = dense(ks[16], (DEPTH_2, D_FF, D_MODEL), D_FF, out_scale)
    return {"x": x, "attn_norm": attn_norm, "ffn_norm": ffn_norm,
            "gdn_w_in": gdn_w_in, "gdn_conv_w": gdn_conv_w, "gdn_a_log": gdn_a_log,
            "gdn_dt_bias": gdn_dt_bias, "gdn_o_gain": gdn_o_gain, "gdn_w_out": gdn_w_out,
            "kv_norm": kv_norm, "w_kv": w_kv, "k_gain": k_gain,
            "sb_w_q": sb_w_q, "sb_q_gain": sb_q_gain, "sb_w_out": sb_w_out,
            "ffn_w_gu": ffn_w_gu, "ffn_w_down": ffn_w_down}

def second_block(x, attn_norm, ffn_norm, gdn_w_in, gdn_conv_w, gdn_a_log, gdn_dt_bias,
              gdn_o_gain, gdn_w_out, kv_norm, w_kv, k_gain, sb_w_q, sb_q_gain, sb_w_out,
              ffn_w_gu, ffn_w_down):
    h = x
    k_sh = None
    v_sh = None
    for layer in range(DEPTH_2):
        hn = rms_norm(h, attn_norm[layer])
        if layer < N_A_LAYERS:
            i = layer
            h = h + gdn_mixer(hn, gdn_w_in[i], gdn_conv_w[i], gdn_a_log[i], gdn_dt_bias[i],
                              gdn_o_gain[i], gdn_w_out[i])
        else:
            if layer == N_A_LAYERS:
                k_sh, v_sh = shared_kv(h, kv_norm, w_kv, k_gain)
            j = layer - N_A_LAYERS
            h = h + sb_mixer(hn, k_sh, v_sh, sb_w_q[j], sb_q_gain[j], sb_w_out[j])
        h = h + swiglu(rms_norm(h, ffn_norm[layer]), ffn_w_gu[layer], ffn_w_down[layer])
    return h


def setup_inputs(seed=0):
    out = dict(first_inputs(seed))
    for name, value in second_inputs(seed + 1).items():
        if name != "x":
            out[name + "_2"] = value
    return out


def reference(
    x, c, ctx, c_ctx, w_ada, b_ada, norm1_g, w_in, w_decay, b_decay, gla_norm_g, w_pool,
    pool_scale, w_out, norm2_g, w_router_group, w_router_expert, w_expert_in, w_expert_out,
    final_norm_g, attn_norm_2, ffn_norm_2, gdn_w_in_2, gdn_conv_w_2, gdn_a_log_2, gdn_dt_bias_2,
    gdn_o_gain_2, gdn_w_out_2, kv_norm_2, w_kv_2, k_gain_2, sb_w_q_2, sb_q_gain_2, sb_w_out_2,
    ffn_w_gu_2, ffn_w_down_2,
):
    x = first_block(
        x, c, ctx, c_ctx, w_ada, b_ada, norm1_g, w_in, w_decay, b_decay, gla_norm_g, w_pool,
        pool_scale, w_out, norm2_g, w_router_group, w_router_expert, w_expert_in, w_expert_out,
        final_norm_g,
    )
    return second_block(
        x, attn_norm_2, ffn_norm_2, gdn_w_in_2, gdn_conv_w_2, gdn_a_log_2, gdn_dt_bias_2,
        gdn_o_gain_2, gdn_w_out_2, kv_norm_2, w_kv_2, k_gain_2, sb_w_q_2, sb_q_gain_2,
        sb_w_out_2, ffn_w_gu_2, ffn_w_down_2,
    )


_drawn_inputs = setup_inputs


def setup_inputs(seed=0):
    import zlib

    import numpy as np

    out = dict(_drawn_inputs(seed))
    spreads = {}
    factors = {'attn_norm_2': 5.377,
     'ffn_norm_2': 5.193,
     'gdn_o_gain_2': 8.0,
     'kv_norm_2': 23.134,
     'k_gain_2': 22.888,
     'sb_q_gain_2': 26.708}
    for name, (base, spread) in spreads.items():
        noise = np.random.default_rng([zlib.crc32(name.encode()), seed]).standard_normal(out[name].shape)
        drawn = base * np.exp(spread * noise) if base else spread * noise
        out[name] = __import__('jax').numpy.asarray(drawn.astype(out[name].dtype))
    for name, factor in factors.items():
        out[name] = (out[name] * factor).astype(out[name].dtype)
    return out
```

```python
from contextlib import ExitStack

import numpy as np
import concourse.bass as bass
from concourse import mybir

F32 = mybir.dt.float32
U8 = mybir.dt.uint8
ALU = mybir.AluOpType
ACT = mybir.ActivationFunctionType
AX = mybir.AxisListType
P = 128
D = 1024
KT = D // P
T = 512
TT = T // P
CTX = 256
TA = T + CTX
EPS = 1e-6
SLOTS = 8
NEXP = 32
FF = 2816
FT = FF // P
HEADS = 8
GRID_W = 64
ROWS = T // GRID_W
WINDOWS = (2, 4, 8, 16)
LEVELS = 6
MASKED_LOW = -3.0e38


class Cols:

    def __init__(self, parts):
        self.at, n = {}, 0
        for name, width in parts:
            self.at[name] = (n, n + width)
            n += width
        self.n = n

    def __getitem__(self, name):
        return slice(*self.at[name])


PARAMS = Cols([("b_ada", 48), ("norm1", 8), ("norm2", 8), ("final", 8), ("attn", 16), ("ffn", 16), ("kvn", 8),
               ("gla", 1), ("pscale", 4), ("bdec", 4), ("conv", 96), ("ogain", 1), ("kgain", 1), ("qgain", 1),
               ("cvec", 16)])
TABLES = Cols([("ident", P), ("ones", P), ("incl", P), ("strict", P), ("after", P),
               ("glaf", P), ("glab", P), ("level", P * (LEVELS + 1)), ("rank", 8), ("resetg", TA), ("resetd", T),
               ("rcount", 4 * T)])
STREAM = Cols([("ada", 48), ("k", 2), ("v", 4), ("q", 2), ("g", 4), ("p", 4), ("out", 8), ("experts", 6 * NEXP),
               ("gdn", 32), ("gdnout", 8), ("gu0", 2 * FT), ("down0", FT), ("sbk", 8), ("sbv", 8), ("sbq", 8),
               ("sbout", 8), ("gu1", 2 * FT), ("down1", FT)])
SMALL = Cols([("wa", 8 * 32), ("wab", 8 * 16), ("router", 8 * 36), ("pool", 4 * P)])


def tables():
    t = np.zeros((P, TABLES.n), np.float32)
    j, i = np.arange(P)[:, None], np.arange(P)[None, :]
    t[:, TABLES["ident"]] = j == i
    t[:, TABLES["ones"]] = 1
    t[:, TABLES["incl"]] = j <= i
    t[:, TABLES["strict"]] = j < i
    t[:, TABLES["after"]] = j > i
    same = j // 64 == i // 64
    t[:, TABLES["glaf"]] = same & (j <= i)
    t[:, TABLES["glab"]] = same & (j >= i)
    lv = t[:, TABLES["level"]].reshape(P, LEVELS + 1, P)
    for n in range(LEVELS + 1):
        s = 1 << n
        lv[:, n] = (j // (2 * s) == i // (2 * s)) & (j % (2 * s) < s) & (i % (2 * s) >= s)
    t[:, TABLES["level"]] = lv.reshape(P, -1)
    t[:, TABLES["rank"]] = 8 - np.arange(8)
    t[:, TABLES["resetg"]] = np.arange(TA) % 64 != 0
    t[:, TABLES["resetd"]] = np.arange(T) % P != 0
    rc = np.zeros((4, ROWS, GRID_W), np.float32)
    for g, w in enumerate(WINDOWS):
        lo, hi = w // 2, w - 1 - w // 2
        count = [np.clip(np.arange(n) + hi + 1, 0, n) - np.clip(np.arange(n) - lo, 0, n) for n in (ROWS, GRID_W)]
        rc[g] = 1.0 / (count[0][:, None] * count[1][None, :])
    t[:, TABLES["rcount"]] = rc.reshape(1, -1)
    return t


def flat(ap):
    return ap.rearrange("p a n -> p (a n)")


def program(nc, xT, ctxT, stream, small, params, heads8, wdec, table, outT):
    with ExitStack() as ctx:
        def sb(name, shape, dt=F32, on=None):
            return (on or ctx).enter_context(nc.sbuf_tensor(name, shape, dt))

        live = []

        def sem(name):
            live.append(nc.alloc_semaphore(name))
            return live[-1]

        def kept_sem(name):
            return ctx.enter_context(nc.semaphore(name))

        def retire():
            nc.clear_and_free_semaphores(list(live))
            live.clear()
            nc.all_engine_barrier()

        ring = sb("ring", [P, SLOTS, 1024])
        res = sb("res", [P, KT, T])
        hn = sb("hn", [P, KT, T])
        par = sb("par", [P, PARAMS.n])
        tab = sb("tab", [P, TABLES.n])
        sml = sb("sml", [P, SMALL.n])
        mod = sb("mod", [P, 48, 2])
        ab8 = sb("ab8", [8, 2])
        ps = ctx.enter_context(nc.psum_tensor("ps", [P, 8, 512], F32))

        ident = tab[:, TABLES["ident"]]
        ones = tab[:, TABLES["ones"]]

        def col(name, i=0):
            a = PARAMS.at[name][0] + i
            return par[:, a:a + 1]

        block_in = [kept_sem(f"block_in{s}") for s in range(SLOTS)]
        blocks_done = kept_sem("blocks_done")
        issued = [0]

        def load_blocks(sp, upto_block):
            upto_block = min(upto_block, STREAM.n)

            def one(b, i=None):
                s = b % SLOTS
                back = b - SLOTS + 1
                if i is None:
                    if back > 0:
                        sp.wait_ge(blocks_done, back)
                    src = stream[b]
                else:
                    sp.wait_ge(blocks_done, i * SLOTS + back)
                    src = flat(stream[bass.ds(i * SLOTS + b, 1)].rearrange("a p n -> p a n"))
                sp.dma_start(ring[:, s, :], src).then_inc(block_in[s], 16)

            while issued[0] < SLOTS and issued[0] < upto_block:
                one(issued[0])
                issued[0] += 1
            turns = (upto_block - issued[0]) // SLOTS
            if turns > 1:
                with sp.Fori(0, turns) as i:
                    for j in range(SLOTS):
                        one(issued[0] + j, i)
                issued[0] += turns * SLOTS
            while issued[0] < upto_block:
                one(issued[0])
                issued[0] += 1

        def block_here(pe, b, later=None):
            v = 16 * (b // SLOTS + 1)
            pe.wait_ge(block_in[b % SLOTS], v if later is None else later * 16 + v)
            return ring[:, b % SLOTS, :]

        def dense_tile(pe, w, act, out):
            for k in range(KT):
                m = pe.matmul(out, w[:, k * P:(k + 1) * P], act[:, k, :], start=k == 0, stop=k == KT - 1)
            m.then_inc(blocks_done, 1)

        def credit(pool, sems):
            for pair in sems:
                for s in pair:
                    pool.sem_inc(s, 1)

        def apart(eng):
            eng.wait_ge(small_in, 64)

        small_in = kept_sem("small_in")
        x_in = sem("x_in")
        hctx = sb("hctx", [P, KT, CTX])
        hand = ExitStack()
        cs = sb("cs", [P, 8, 2], on=hand)
        cs_ready = sem("cs_ready")
        mod_ready = sem("mod_ready")
        with nc.Block() as block:
            @block.scalar
            def _(act):
                act.dma_start(par[:, :], params).then_inc(small_in, 16)
                act.dma_start(sml[:, :], small).then_inc(small_in, 16)
                act.dma_start(tab[:, :], table).then_inc(small_in, 16)
                act.dma_start(ab8[:, :], heads8).then_inc(small_in, 16)
                act.dma_start(res[:, :, :], xT.rearrange("(k p) t -> p k t", p=P)).then_inc(x_in, 16)
                act.dma_start(hctx[:, :, :], ctxT.rearrange("(k p) t -> p k t", p=P)).then_inc(x_in, 16)
                act.wait_ge(small_in, 64)
                act.activation(cs[:, :, :], par[:, PARAMS["cvec"]].rearrange("p (k c) -> p k c", c=2),
                               ACT.Silu).then_inc(cs_ready, 1)

            @block.sync
            def _(sp):
                load_blocks(sp, STREAM["k"].start + SLOTS)

            @block.tensor
            def _(pe):
                pe.wait_ge(cs_ready, 1)
                with pe.Fori(0, 6) as i:
                    pe.wait_ge(mod_ready, i + 1)
                    for j in range(SLOTS):
                        w = block_here(pe, j, i)
                        for k in range(KT):
                            m = pe.matmul(ps[:, 0, 2 * j:2 * j + 2], w[:, k * P:(k + 1) * P], cs[:, k, :],
                                          start=k == 0, stop=k == KT - 1)
                        m.then_inc(blocks_done, 1)

            @block.vector
            def _(ve):
                ve.wait_ge(small_in, 64)
                ve.sem_inc(mod_ready, 1)
                with ve.Fori(0, 6) as i:
                    ve.wait_ge(blocks_done, i * SLOTS + SLOTS)
                    ve.tensor_tensor(mod[:, bass.ds(i * 8, 8), :],
                                     ps[:, 0, 0:16].rearrange("p (n c) -> p n c", c=2),
                                     par[:, bass.ds(i * 8, 8)].unsqueeze(2).to_broadcast([P, 8, 2]),
                                     ALU.add).then_inc(mod_ready, 1)
        hand.close()

        def norm(name, src, dst, gain, shift=None, n=T, first_wait=None):
            with ExitStack() as st:
                sq = sb(name + "_sq", [P, KT, n], on=st)
                rs = sb(name + "_rs", [P, n], on=st)
                squared, summed, root, scaled = (sem(name + s) for s in ("_squared", "_summed", "_root", "_scaled"))
                with nc.Block() as block:
                    @block.scalar
                    def _(act):
                        if first_wait:
                            act.wait_ge(*first_wait)
                        for k in range(KT):
                            act.activation(sq[:, k, :], src[:, k, :], ACT.Square).then_inc(squared, 1)
                        act.wait_ge(root, 1)
                        act.activation(rs[:, :], rs[:, :], ACT.Sqrt).then_inc(root, 1)
                        if shift is not None:
                            for k in range(KT):
                                act.wait_ge(scaled, k + 1)
                                act.activation(dst[:, k, :], dst[:, k, :], ACT.Identity, bias=shift(k))

                    @block.tensor
                    def _(pe):
                        for k in range(KT):
                            pe.wait_ge(squared, k + 1)
                            m = pe.matmul(ps[:, 0, 0:n], ones, sq[:, k, :], start=k == 0, stop=k == KT - 1)
                        m.then_inc(summed, 1)

                    @block.vector
                    def _(ve):
                        ve.wait_ge(summed, 1)
                        ve.tensor_scalar(rs[:, :], ps[:, 0, 0:n], 1.0 / D, EPS, ALU.mult, ALU.add).then_inc(root, 1)
                        ve.wait_ge(root, 2)
                        ve.reciprocal(rs[:, :], rs[:, :]).then_inc(root, 1)
                        ve.wait_ge(root, 3)
                        ve.wait_ge(squared, KT)
                        for k in range(KT):
                            ve.scalar_tensor_tensor(dst[:, k, :], src[:, k, :], gain(k), rs[:, :],
                                                    ALU.mult, ALU.mult).then_inc(scaled, 1)

        gscale = sb("gscale", [P, 3, KT])
        gready = sem("gready")
        with nc.Block() as block:
            @block.vector
            def _(ve):
                for n, (part, c, g) in enumerate(((8, 0, "norm1"), (8, 1, "norm1"), (32, 0, "norm2"))):
                    ve.scalar_tensor_tensor(gscale[:, n, :], mod[:, part:part + 8, c], 1.0, par[:, PARAMS[g]],
                                            ALU.add, ALU.mult).then_inc(gready, 1)
                ve.wait_ge(x_in, 32)
        norm("n1", res, hn, lambda k: gscale[:, 0, k:k + 1], lambda k: mod[:, k, 0:1])
        norm("n1c", hctx, hctx, lambda k: gscale[:, 1, k:k + 1], lambda k: mod[:, k, 1:2], n=CTX)

        mix = sb("mix", [P, KT, T])
        gla = ctx.enter_context(ExitStack())
        gs = mix[:, 4:8, :]
        kT = sb("kT", [P, 2, TA], on=gla)
        qT = sb("qT", [P, 2, T], on=gla)
        vtok = sb("vtok", [P, 6, 512], on=gla)
        pT = sb("pT", [P, 4, T], on=gla)
        aT = sb("aT", [32, TA], on=gla)
        wd = sb("wd", [32, 512], on=gla)
        wd_zero, wd_in = sem("wd_zero"), sem("wd_in")
        evac_k, evac_v, evac_n, a_sum = sem("evac_k"), sem("evac_v"), sem("evac_n"), sem("a_sum")
        BK, BV, BQ = STREAM["k"].start, STREAM["v"].start, STREAM["q"].start
        with nc.Block() as block:
            @block.sync
            def _(sp):
                load_blocks(sp, STREAM["out"].start + SLOTS)

            @block.gpsimd
            def _(pool):
                pool.memset(wd[:, :], 0.0).then_inc(wd_zero, 1)
                pool.wait_ge(wd_zero, 1)
                pool.dma_start(wd[0:16, 0:256], wdec[0]).then_inc(wd_in, 16)
                pool.dma_start(wd[16:32, 256:512], wdec[1]).then_inc(wd_in, 16)

            @block.tensor
            def _(pe):
                for n in range(2):
                    w = block_here(pe, BK + n)
                    for k in range(KT):
                        pe.matmul(ps[:, 2 * n, :], w[:, k * P:(k + 1) * P], hn[:, k, :], start=k == 0, stop=k == KT - 1)
                    for k in range(KT):
                        m = pe.matmul(ps[:, 2 * n + 1, 0:CTX], w[:, k * P:(k + 1) * P], hctx[:, k, :],
                                      start=k == 0, stop=k == KT - 1)
                    m.then_inc(blocks_done, 1)
                wa = sml[:, SMALL["wa"]].rearrange("p (k n) -> p k n", k=KT)
                for k in range(KT):
                    pe.matmul(ps[0:32, 6, :], wa[:, k, :], hn[:, k, :], start=k == 0, stop=k == KT - 1)
                for k in range(KT):
                    m = pe.matmul(ps[0:32, 7, 0:CTX], wa[:, k, :], hctx[:, k, :], start=k == 0, stop=k == KT - 1)
                m.then_inc(a_sum, 1)
                pe.wait_ge(evac_k, 4)
                for b in range(4):
                    w = block_here(pe, BV + b)
                    for kk in range(2):
                        k = 2 * b + kk
                        for t in range(6):
                            h = hn[:, k, t * P:(t + 1) * P] if t < 4 else hctx[:, k, (t - 4) * P:(t - 3) * P]
                            m = pe.matmul(ps[:, t, :], h, w[:, kk * 512:(kk + 1) * 512], start=k == 0, stop=k == KT - 1)
                    m.then_inc(blocks_done, 1)
                for n in range(10):
                    w = block_here(pe, BQ + n)
                    bank = (6 + n) % 8
                    if n < 2:
                        pe.wait_ge(evac_k, 5 + n)
                    elif n < 8:
                        pe.wait_ge(evac_v, n - 1)
                    else:
                        pe.wait_ge(evac_n, n - 7)
                    dense_tile(pe, w, hn, ps[:, bank, :])

            @block.scalar
            def _(act):
                for n in range(2):
                    act.wait_ge(blocks_done, BK + n + 1)
                    act.activation(kT[:, n, 0:T], ps[:, 2 * n, :], ACT.Copy).then_inc(evac_k, 1)
                    act.activation(kT[:, n, T:TA], ps[:, 2 * n + 1, 0:CTX], ACT.Copy).then_inc(evac_k, 1)
                act.wait_ge(a_sum, 1)
                act.activation(aT[:, 0:T], ps[0:32, 6, :], ACT.Copy).then_inc(evac_k, 1)
                act.activation(aT[:, T:TA], ps[0:32, 7, 0:CTX], ACT.Copy).then_inc(evac_k, 1)
                act.wait_ge(blocks_done, BV + 4)
                for t in range(6):
                    act.activation(vtok[:, t, :], ps[:, t, :], ACT.Copy).then_inc(evac_v, 1)
                for n in range(10):
                    act.wait_ge(blocks_done, BQ + n + 1)
                    out = qT[:, n, :] if n < 2 else gs[:, n - 2, :] if n < 6 else pT[:, n - 6, :]
                    act.activation(out, ps[:, (6 + n) % 8, :], ACT.Silu if 2 <= n < 6 else ACT.Copy,
                                   scale=0.125 if n < 2 else 1.0).then_inc(evac_n, 1)

        st = gla.enter_context(ExitStack())
        qbm = hn[:, :, :].rearrange("p (a b) t -> p a b t", b=2)
        kb = hctx[:, :, :].rearrange("p (a b) t -> p a (b t)", b=2)
        tot = sb("tot", [P, 4, 12], on=gla)
        SS = sb("SS", [P, 4, 12, P], on=gla)
        kstT = sb("kstT", [P, 2, 4, 2, P], on=gla)
        kst = sb("kst", [P, 4, TA], on=st)
        cum = sb("cum", [P, TA], on=st)
        la = sb("la", [P, TA], on=st)
        lg = sb("lg", [P, TA], on=st)
        bb = sb("bb", [P, TA], on=st)
        dl = mix[:, 2:4, :].rearrange("p a t -> p (a t)")[:, 0:TA]
        e1, e2 = mix[:, 0, :], mix[:, 1, :]
        z_sum, z_log, z_dve, z_exp, z_zero = sem("z_sum"), sem("z_log"), sem("z_dve"), sem("z_exp"), sem("z_zero")
        with nc.Block() as block:
            @block.gpsimd
            def _(pool):
                pool.memset(qbm[:, :, :, :], 0.0).then_inc(z_zero, 1)
                pool.memset(kstT[:, :, :, :, :], 0.0).then_inc(z_zero, 1)
                pool.memset(SS[:, :, 0, :], 0.0).then_inc(z_zero, 1)

            @block.tensor
            def _(pe):
                pe.wait_ge(wd_in, 32)
                for dp in range(4):
                    pe.matmul(ps[:, 2 * dp, :], wd[:, dp * P:(dp + 1) * P], aT[:, 0:T], start=True, stop=True)
                    pe.matmul(ps[:, 2 * dp + 1, 0:CTX], wd[:, dp * P:(dp + 1) * P], aT[:, T:TA],
                              start=True, stop=True).then_inc(z_sum, 1)

            @block.scalar
            def _(act):
                n = [0]

                def step(ins):
                    n[0] += 1
                    ins.then_inc(z_log, 1)
                    act.wait_ge(z_log, n[0])
                for dp in range(4):
                    bias = col("bdec", dp)
                    act.wait_ge(z_dve, 11 * dp + 2)
                    act.activation(lg[:, 0:T], ps[:, 2 * dp, :], ACT.Abs, bias=bias).then_inc(z_log, 1)
                    n[0] += 1
                    step(act.activation(lg[:, T:TA], ps[:, 2 * dp + 1, 0:CTX], ACT.Abs, bias=bias))
                    step(act.activation(lg[:, :], lg[:, :], ACT.Exp, scale=-1.0))
                    step(act.activation(lg[:, :], lg[:, :], ACT.Ln, bias=1.0))
                    act.wait_ge(z_dve, 11 * dp + 7)
                    act.activation(e1, bb[:, 0:T], ACT.Exp, scale=1.0 / 16).then_inc(z_exp, 1)
                    act.activation(e2, bb[:, 0:T], ACT.Exp, scale=-1.0 / 16).then_inc(z_exp, 1)
                    act.activation(lg[:, :], dl, ACT.Exp, scale=1.0 / 16).then_inc(z_exp, 1)
                    act.activation(tot[:, dp, :], tot[:, dp, :], ACT.Exp, scale=1.0 / 16).then_inc(z_exp, 1)

            @block.vector
            def _(ve):
                n = [0]

                def step(ins):
                    n[0] += 1
                    ins.then_inc(z_dve, 1)
                    ve.wait_ge(z_dve, n[0])
                ve.wait_ge(z_zero, 3)
                for dp in range(4):
                    pair, back = dp % 2, dp // 2
                    bias = col("bdec", dp)
                    ve.wait_ge(z_sum, dp + 1)
                    step(ve.tensor_scalar(la[:, 0:T], ps[:, 2 * dp, :], bias, 0.0, ALU.add, ALU.min))
                    step(ve.tensor_scalar(la[:, T:TA], ps[:, 2 * dp + 1, 0:CTX], bias, 0.0, ALU.add, ALU.min))
                    ve.wait_ge(z_log, 4 * dp + 4)
                    step(ve.tensor_tensor(la[:, :], la[:, :], lg[:, :], ALU.subtract))
                    step(ve.tensor_tensor_scan(cum[:, :], tab[:, TABLES["resetg"]], la[:, :], 0.0, ALU.mult, ALU.add))
                    chunks = [x.rearrange("p (c j) -> p c j", j=64) for x in (cum[:, :], bb[:, :], dl)]
                    t3 = tot[:, dp, :].unsqueeze(2).to_broadcast([P, 12, 64])
                    step(ve.tensor_copy(tot[:, dp, :].unsqueeze(2), chunks[0][:, :, 63:64]))
                    if back:
                        step(ve.tensor_tensor(dl, cum[:, :], la[:, :], ALU.subtract))
                        step(ve.tensor_tensor(chunks[1], t3, chunks[2], ALU.subtract))
                    else:
                        step(ve.tensor_copy(bb[:, :], cum[:, :]))
                        step(ve.tensor_tensor(chunks[2], t3, chunks[1], ALU.subtract))
                    ve.wait_ge(z_exp, 4 * dp + 4)
                    for h in range(2):
                        r = slice(64 * h, 64 * h + 64)
                        step(ve.tensor_tensor(qbm[r, dp, h, :], qT[r, pair, :], e1[r, :], ALU.mult))
                    step(ve.tensor_tensor(kb[:, dp, :], kT[:, pair, 0:T], e2, ALU.mult))
                    step(ve.tensor_tensor(kst[:, dp, :], kT[:, pair, :], lg[:, :], ALU.mult))

        def chunk_of(d, s):
            return (8 + s if s < 4 else s - 4) if d == 0 else (11 - s if s < 4 else 11 - s)
        tr_done, tr_copied, ds_done, ds_used = sem("tr_done"), sem("tr_copied"), sem("ds_done"), sem("ds_used")
        STEPS = 11
        with nc.Block() as block:
            @block.tensor
            def _(pe):
                for s in range(STEPS):
                    u = s % 2
                    if s >= 2:
                        pe.wait_ge(tr_copied, 2 * (s - 1))
                    for dp in range(4):
                        c = chunk_of(dp // 2, s)
                        tile = c // 2
                        m = pe.transpose(ps[:, u, dp * P:(dp + 1) * P], kst[:, dp, tile * P:(tile + 1) * P], ident)
                    m.then_inc(tr_done, 1)
                    pe.wait_ge(tr_copied, 2 * (s + 1))
                    for pair in range(2):
                        if s >= 2:
                            pe.wait_ge(ds_used, 8 * (s - 2) + 4 * pair + 4)
                        for d in range(2):
                            c = chunk_of(d, s)
                            m = pe.matmul(ps[:, 2 + u + 2 * pair, d * 256:d * 256 + 256],
                                          kstT[:, u, 2 * d + pair, c % 2, :],
                                          vtok[:, c // 2, pair * 256:pair * 256 + 256], start=True, stop=True)
                        m.then_inc(ds_done, 1)

            @block.scalar
            def _(act):
                for s in range(STEPS):
                    act.wait_ge(tr_done, s + 1)
                    if s >= 2:
                        act.wait_ge(ds_done, 2 * (s - 1))
                    for d in range(2):
                        half = chunk_of(d, s) % 2
                        r = slice(64 * half, 64 * half + 64)
                        act.activation(kstT[r, s % 2, 2 * d:2 * d + 2, half, :],
                                       ps[r, s % 2, 256 * d:256 * d + 256].rearrange("p (a n) -> p a n", a=2),
                                       ACT.Copy).then_inc(tr_copied, 1)

            @block.vector
            def _(ve):
                for s in range(STEPS):
                    for pair in range(2):
                        ve.wait_ge(ds_done, 2 * s + pair + 1)
                        if s:
                            ve.wait_ge(ds_used, 8 * (s - 1) + 4 * pair + 4)
                        for d in range(2):
                            dp = 2 * d + pair
                            c = chunk_of(d, s)
                            for h in range(2):
                                r = slice(64 * h, 64 * h + 64)
                                o = d * 256 + h * P
                                ve.scalar_tensor_tensor(SS[r, dp, s + 1, :], SS[r, dp, s, :], tot[r, dp, c:c + 1],
                                                        ps[r, 2 + s % 2 + 2 * pair, o:o + P],
                                                        ALU.mult, ALU.add).then_inc(ds_used, 1)
        st.close()

        sc = sb("sc", [P, 2, 2, 512], on=gla)
        masks = sb("masks", [P, 2, P], U8, on=gla)
        oT = sb("oT", [P, 4, T], on=gla)
        sc_zero, sc_done, sc_kept, o_done, o_kept = (sem(n) for n in ("sc_zero", "sc_done", "sc_kept", "o_done", "o_kept"))
        with nc.Block() as block:
            @block.gpsimd
            def _(pool):
                pool.memset(sc[:, :, :, :], 0.0).then_inc(sc_zero, 1)

            @block.tensor
            def _(pe):
                for t in range(TT):
                    cols = slice(t * P, (t + 1) * P)
                    for d in range(2):
                        if t >= 2:
                            pe.wait_ge(sc_kept, 2 * (t - 2) + d + 1)
                        for h in range(4):
                            dp = 2 * d + h // 2
                            m = pe.matmul(ps[:, 2 * (t % 2) + d, h * P:(h + 1) * P], kb[:, dp, cols],
                                          qbm[:, dp, h % 2, cols], start=True, stop=True)
                        m.then_inc(sc_done, 1)
                    pe.wait_ge(sc_kept, 2 * t + 2)
                    if t >= 2:
                        pe.wait_ge(o_kept, t - 1)
                    for h in range(4):
                        out = ps[:, 4 + t % 2, h * P:(h + 1) * P]
                        pe.matmul(out, vtok[:, t, h * P:(h + 1) * P], sc[:, t % 2, 0, h * P:(h + 1) * P],
                                  start=True, stop=False)
                        for d in range(2):
                            dp = 2 * d + h // 2
                            for cc in range(2):
                                c = 2 * t + cc
                                s = 4 + c if d == 0 else 11 - c
                                pe.matmul(out[:, 64 * cc:64 * cc + 64], SS[:, dp, s, :],
                                          qbm[:, dp, h % 2, c * 64:(c + 1) * 64], start=False, stop=False,
                                          skip_group_check=True)
                        m = pe.matmul(out, vtok[:, t, h * P:(h + 1) * P], sc[:, t % 2, 1, h * P:(h + 1) * P],
                                      start=False, stop=True)
                    m.then_inc(o_done, 1)

            @block.vector
            def _(ve):
                ve.tensor_copy(masks[:, 0, :], tab[:, TABLES["glaf"]]).then_inc(sc_zero, 1)
                ve.tensor_copy(masks[:, 1, :], tab[:, TABLES["glab"]]).then_inc(sc_zero, 1)
                ve.wait_ge(sc_zero, 3)
                for t in range(TT):
                    if t >= 2:
                        ve.wait_ge(o_done, t - 1)
                    for d in range(2):
                        ve.wait_ge(sc_done, 2 * t + d + 1)
                        ve.copy_predicated(sc[:, t % 2, d, :].rearrange("p (h i) -> p h i", h=4),
                                           masks[:, d, :].unsqueeze(1).to_broadcast([P, 4, P]),
                                           ps[:, 2 * (t % 2) + d, :].rearrange("p (h i) -> p h i", h=4)
                                           ).then_inc(sc_kept, 1)

            @block.scalar
            def _(act):
                for t in range(TT):
                    act.wait_ge(o_done, t + 1)
                    act.activation(oT[:, :, t * P:(t + 1) * P],
                                   ps[:, 4 + t % 2, :].rearrange("p (h i) -> p h i", h=4), ACT.Copy).then_inc(o_kept, 1)

        sq, rs = hn[:, 0:4, :], hn[:, 4:8, :]
        grid = (ROWS + 16) * (GRID_W + 16)
        spare = SS[:, :, :, :].rearrange("p a b c -> p (a b c)")
        bufs = [spare[:, n * grid:(n + 1) * grid].rearrange("p (r c) -> p r c", c=GRID_W + 16) for n in range(3)]
        o_ms, o_pow = sem("o_ms"), sem("o_pow")
        o_sq, o_sum, o_root, o_mix = sem("o_sq"), sem("o_sum"), sem("o_root"), sem("o_mix")
        pool_step, pooled, pool_mm, pool_out = sem("pool_step"), sem("pooled"), sem("pool_mm"), sem("pool_out")
        with nc.Block() as block:
            @block.scalar
            def _(act):
                for h in range(4):
                    act.activation(sq[:, h, :], oT[:, h, :], ACT.Square).then_inc(o_sq, 1)
                for h in range(4):
                    act.wait_ge(o_ms, h + 1)
                    act.activation(rs[:, h, :], rs[:, h, :], ACT.Sqrt).then_inc(o_pow, 1)

            @block.tensor
            def _(pe):
                for h in range(4):
                    pe.wait_ge(o_sq, h + 1)
                    pe.matmul(ps[:, h, :], ones, sq[:, h, :], start=True, stop=True).then_inc(o_sum, 1)
                wp = sml[:, SMALL["pool"]].rearrange("p (g n) -> p g n", g=4)
                for g in range(4):
                    pe.wait_ge(pooled, g + 1)
                    pe.matmul(ps[:, 4 + g, :], wp[:, g, :], pT[:, g, :], start=True, stop=True).then_inc(pool_mm, 1)

            @block.gpsimd
            def _(pool):
                n = [0]

                def step(ins):
                    n[0] += 1
                    ins.then_inc(pool_step, 1)
                    pool.wait_ge(pool_step, n[0])
                for g, w in enumerate(WINDOWS):
                    lo = w // 2
                    a, b, c = bufs
                    if g:
                        pool.wait_ge(pooled, g)
                    pool.memset(a[:, :, :], 0.0).then_inc(pool_step, 1)
                    pool.memset(b[:, :, :], 0.0).then_inc(pool_step, 1)
                    n[0] += 2
                    pool.wait_ge(pool_step, n[0])
                    step(pool.tensor_copy(a[:, lo:lo + ROWS, lo:lo + GRID_W],
                                          pT[:, g, :].rearrange("p (r c) -> p r c", c=GRID_W)))
                    s = 1
                    width = GRID_W + 16
                    while s < w:
                        step(pool.tensor_tensor(b[:, 0:ROWS + 16, 0:width - s], a[:, 0:ROWS + 16, 0:width - s],
                                                a[:, 0:ROWS + 16, s:width], ALU.add))
                        a, b = b, a
                        s *= 2
                    s = 1
                    rows = ROWS + 16
                    while s < w:
                        step(pool.tensor_tensor(b[:, 0:rows - s, 0:GRID_W], a[:, 0:rows - s, 0:GRID_W],
                                                a[:, s:rows, 0:GRID_W], ALU.add))
                        a, b = b, a
                        s *= 2
                    rc = tab[:, TABLES["rcount"]].rearrange("p (g r c) -> p g r c", g=4, c=GRID_W)[:, g]
                    step(pool.tensor_tensor(c[:, 0:ROWS, 0:GRID_W], a[:, 0:ROWS, 0:GRID_W], rc, ALU.mult))
                    p3 = pT[:, g, :].rearrange("p (r c) -> p r c", c=GRID_W)
                    pool.tensor_tensor(p3, c[:, 0:ROWS, 0:GRID_W], p3, ALU.subtract).then_inc(pooled, 1)
                pool.wait_ge(pooled, 4)

            @block.vector
            def _(ve):
                n = [0]

                def step(ins):
                    n[0] += 1
                    ins.then_inc(o_root, 1)
                    ve.wait_ge(o_root, n[0])
                for h in range(4):
                    ve.wait_ge(o_sum, h + 1)
                    ve.tensor_scalar(rs[:, h, :], ps[:, h, :], 1.0 / P, EPS, ALU.mult, ALU.add).then_inc(o_ms, 1)
                for h in range(4):
                    ve.wait_ge(o_pow, h + 1)
                    step(ve.reciprocal(rs[:, h, :], rs[:, h, :]))
                    step(ve.scalar_tensor_tensor(rs[:, h, :], oT[:, h, :], col("gla"), rs[:, h, :], ALU.mult, ALU.mult))
                    ve.tensor_tensor(mix[:, h, :], rs[:, h, :], gs[:, h, :], ALU.mult).then_inc(o_mix, 1)
                ve.wait_ge(o_mix, 4)
                for g in range(4):
                    ve.wait_ge(pool_mm, g + 1)
                    ve.tensor_scalar(mix[:, 4 + g, :], ps[:, 4 + g, :], col("pscale", g), None, ALU.mult).then_inc(pool_out, 1)
        gla.close()

        def project_out(name, act_in, first_block, gate, next_block):
            added = sem(name + "_added")
            with nc.Block() as block:
                @block.sync
                def _(sp):
                    load_blocks(sp, next_block)

                @block.tensor
                def _(pe):
                    for n in range(KT):
                        dense_tile(pe, block_here(pe, first_block + n), act_in, ps[:, n, :])

                @block.vector
                def _(ve):
                    for n in range(KT):
                        ve.wait_ge(blocks_done, first_block + n + 1)
                        if gate is None:
                            ve.tensor_tensor(res[:, n, :], ps[:, n, :], res[:, n, :], ALU.add).then_inc(added, 1)
                        else:
                            ve.scalar_tensor_tensor(res[:, n, :], ps[:, n, :], gate(n), res[:, n, :],
                                                    ALU.mult, ALU.add).then_inc(added, 1)

        project_out("mixout", mix, STREAM["out"].start, lambda n: mod[:, 16 + n, 0:1], STREAM["experts"].start + SLOTS)
        norm("n2", res, hn, lambda k: gscale[:, 2, k:k + 1], lambda k: mod[:, 24 + k, 0:1])

        moe = ctx.enter_context(ExitStack())
        gates = sb("gates", [P, TT, NEXP], on=moe)
        lgt = sb("lgt", [P, TT, 36], on=moe)
        gt_ = sb("gt_", [P, 8, TT, 8], on=moe)
        prod = sb("prod", [P, TT, 4, 8], on=moe)
        one = sb("one", [P, 8, TT, 1], on=moe)
        logits_done, r_step, r_exp = sem("logits_done"), sem("r_step"), sem("r_exp")
        with nc.Block() as block:
            @block.tensor
            def _(pe):
                wr = sml[:, SMALL["router"]].rearrange("p (k n) -> p k n", k=KT)
                for t in range(TT):
                    for k in range(KT):
                        m = pe.matmul(ps[:, 0, t * 36:(t + 1) * 36], hn[:, k, t * P:(t + 1) * P], wr[:, k, :],
                                      start=k == 0, stop=k == KT - 1)
                m.then_inc(logits_done, 1)

            @block.scalar
            def _(act):
                act.wait_ge(r_step, 3)
                act.activation(gt_[:, 1, :, 0:4], gt_[:, 0, :, 0:4], ACT.Exp).then_inc(r_exp, 1)
                act.wait_ge(r_step, 21)
                act.activation(one[:, 5], one[:, 4], ACT.Exp).then_inc(r_exp, 1)

            @block.vector
            def _(ve):
                n = [0]

                def step(ins):
                    n[0] += 1
                    ins.then_inc(r_step, 1)
                    ve.wait_ge(r_step, n[0])

                def wide(x, width):
                    return x.to_broadcast([P, TT, width])
                rank = tab[:, TABLES["rank"]].unsqueeze(1)

                def first_of(eq, width, top, hot):
                    step(ve.tensor_tensor(hot, eq, rank[:, :, 8 - 8:width].to_broadcast([P, TT, width]), ALU.mult))
                    step(ve.tensor_reduce(top, hot, AX.X, ALU.max))
                    step(ve.tensor_tensor(hot, hot, wide(top, width), ALU.is_equal))
                ve.wait_ge(logits_done, 1)
                step(ve.tensor_copy(lgt[:, :, :], ps[:, 0, 0:144].rearrange("p (t n) -> p t n", t=TT)))
                group = lgt[:, :, 0:4]
                step(ve.tensor_reduce(one[:, 0], group, AX.X, ALU.max))
                step(ve.tensor_tensor(gt_[:, 0, :, 0:4], group, wide(one[:, 0], 4), ALU.subtract))
                ve.wait_ge(r_exp, 1)
                step(ve.tensor_reduce(one[:, 1], gt_[:, 1, :, 0:4], AX.X, ALU.add))
                step(ve.reciprocal(one[:, 1], one[:, 1]))
                step(ve.tensor_tensor(gt_[:, 2, :, 0:4], group, wide(one[:, 0], 4), ALU.is_equal))
                first_of(gt_[:, 2, :, 0:4], 4, one[:, 2], gt_[:, 3, :, 0:4])
                hot_g = gt_[:, 3, :, 0:4].unsqueeze(3).to_broadcast([P, TT, 4, 8])
                step(ve.tensor_tensor(prod[:, :, :, :], lgt[:, :, 4:36].rearrange("p t (g e) -> p t g e", g=4),
                                      hot_g, ALU.mult))
                le, eq, h1, h2, rest = (gt_[:, n, :, :] for n in (4, 5, 6, 7, 0))
                step(ve.tensor_reduce(le.unsqueeze(3), prod[:, :, :, :].rearrange("p t g e -> p t e g"), AX.X, ALU.add))
                step(ve.tensor_reduce(one[:, 2], le, AX.X, ALU.max))
                step(ve.tensor_tensor(eq, le, wide(one[:, 2], 8), ALU.is_equal))
                first_of(eq, 8, one[:, 3], h1)
                step(ve.scalar_tensor_tensor(rest, h1, MASKED_LOW, le, ALU.mult, ALU.add))
                step(ve.tensor_reduce(one[:, 3], rest, AX.X, ALU.max))
                step(ve.tensor_tensor(eq, rest, wide(one[:, 3], 8), ALU.is_equal))
                step(ve.tensor_tensor(one[:, 4], one[:, 3], one[:, 2], ALU.subtract))
                step(ve.memset(one[:, 6], 1.0))
                first_of(eq, 8, one[:, 7], h2)
                ve.wait_ge(r_exp, 2)
                step(ve.tensor_tensor(one[:, 6], one[:, 5], one[:, 6], ALU.add))
                step(ve.reciprocal(one[:, 6], one[:, 6]))
                step(ve.tensor_tensor(one[:, 6], one[:, 6], one[:, 1], ALU.mult))
                step(ve.tensor_tensor(one[:, 5], one[:, 5], one[:, 6], ALU.mult))
                step(ve.tensor_tensor(h1, h1, wide(one[:, 6], 8), ALU.mult))
                step(ve.tensor_tensor(h2, h2, wide(one[:, 5], 8), ALU.mult))
                step(ve.tensor_tensor(h1, h1, h2, ALU.add))
                step(ve.tensor_tensor(gates[:, :, :].rearrange("p t (g e) -> p t g e", g=4), hot_g,
                                      h1.unsqueeze(2).to_broadcast([P, TT, 4, 8]), ALU.mult))

        acc = mix[:, :, :].rearrange("p (t h) n -> p t h n", h=2)
        sg = sb("sg", [P, 2, T], on=moe)
        hid = sb("hid", [P, 2, T], on=moe)
        BE = STREAM["experts"].start
        silu_done, act_ready, out_done, acc_done, acc_zero = (
            sem(n) for n in ("silu_done", "act_ready", "out_done", "acc_done", "acc_zero"))
        with nc.Block() as block:
            @block.sync
            def _(sp):
                load_blocks(sp, STREAM["gdn"].start + SLOTS)

            @block.tensor
            def _(pe):
                with pe.Fori(0, NEXP // 4) as i:
                    for u in range(4):
                        e, b = i * 4 + u, BE + 6 * u
                        for j in range(4):
                            pe.wait_ge(act_ready, e * 2 + j // 2 + 1)
                            dense_tile(pe, block_here(pe, b + j, i * 3), hn, ps[:, j, :])
                        w = [block_here(pe, b + 4 + f, i * 3) for f in range(2)]
                        pe.wait_ge(act_ready, e * 2 + 4)
                        for n in range(8):
                            t, half = n // 2, n % 2
                            pe.wait_ge(acc_done, e * 8 + n + 1)
                            for f in range(2):
                                m = pe.matmul(ps[:, 4 + n % 4, :], hid[:, f, t * P:(t + 1) * P],
                                              w[f][:, half * 512:(half + 1) * 512], start=f == 0, stop=f == 1)
                                if n == 7:
                                    m.then_inc(blocks_done, 1)
                            if n < 7:
                                m.then_inc(out_done, 1)

            @block.scalar
            def _(act):
                with act.Fori(0, NEXP // 4) as i:
                    for u in range(4):
                        for f in range(2):
                            act.wait_ge(blocks_done, i * 24 + BE + 6 * u + 2 * f + 1)
                            act.wait_ge(act_ready, i * 8 + 2 * u + f + 1)
                            act.activation(sg[:, f, :], ps[:, 2 * f, :], ACT.Silu).then_inc(silu_done, 1)

            @block.vector
            def _(ve):
                ve.sem_inc(act_ready, 2)
                ve.sem_inc(acc_done, 4)
                ve.memset(acc, 0.0).then_inc(acc_zero, 1)
                ve.wait_ge(acc_zero, 1)
                with ve.Fori(0, NEXP // 4) as i:
                    for u in range(4):
                        for f in range(2):
                            ve.wait_ge(silu_done, i * 8 + 2 * u + f + 1)
                            ve.wait_ge(blocks_done, i * 24 + BE + 6 * u + 2 * f + 2)
                            ve.tensor_tensor(hid[:, f, :], sg[:, f, :], ps[:, 2 * f + 1, :], ALU.mult).then_inc(act_ready, 1)
                        for n in range(8):
                            t, half = n // 2, n % 2
                            if n < 7:
                                ve.wait_ge(out_done, i * 28 + 7 * u + n + 1)
                            else:
                                ve.wait_ge(blocks_done, i * 24 + BE + 6 * u + 6)
                            ve.wait_ge(acc_done, i * 32 + max(8 * u + n - 3, 1))
                            ve.scalar_tensor_tensor(acc[:, t, half, :], ps[:, 4 + n % 4, :],
                                                    flat(gates[:, t:t + 1, bass.ds(i * 4 + u, 1)].rearrange("p a n -> p n a")),
                                                    acc[:, t, half, :], ALU.mult, ALU.add).then_inc(acc_done, 1)
        y_done, y_added = sem("y_done"), sem("y_added")
        with nc.Block() as block:
            @block.tensor
            def _(pe):
                for k in range(KT):
                    for t in range(TT):
                        m = pe.transpose(ps[:, k, t * P:(t + 1) * P],
                                         acc[:, t, k // 4, (k % 4) * P:(k % 4 + 1) * P], ident)
                    m.then_inc(y_done, 1)

            @block.vector
            def _(ve):
                for k in range(KT):
                    ve.wait_ge(y_done, k + 1)
                    ve.scalar_tensor_tensor(res[:, k, :], ps[:, k, :], mod[:, 40 + k, 0:1], res[:, k, :],
                                            ALU.mult, ALU.add).then_inc(y_added, 1)
        moe.close()
        norm("fin", res, res, lambda k: col("final", k))

        retire()
        norm("gn", res, hn, lambda k: col("attn", k))
        V = mix
        gdn = ctx.enter_context(ExitStack())
        Q = sb("Q", [P, HEADS, T], on=gdn)
        K = sb("K", [P, HEADS, T], on=gdn)
        Z = sb("Z", [P, HEADS, T], on=gdn)
        gcols = sb("gcols", [P, 3, TT, HEADS], on=gdn)
        egl = sb("egl", [P, HEADS, TT], on=gdn)
        rows = tab[0:8, TABLES["rcount"]].rearrange("p (a t) -> p a t", a=4)
        ea = sb("ea", [8, 1], on=gdn)
        ab_done, ab_act, ab_dve, ab_tr, ab_cols = (sem(n) for n in ("ab_done", "ab_act", "ab_dve", "ab_tr", "ab_cols"))
        with nc.Block() as block:
            @block.tensor
            def _(pe):
                wab = sml[:, SMALL["wab"]].rearrange("p (k n) -> p k n", k=KT)
                for part in range(2):
                    for k in range(KT):
                        m = pe.matmul(ps[0:8, part, :], wab[:, k, 8 * part:8 * part + 8], hn[:, k, :],
                                      start=k == 0, stop=k == KT - 1)
                m.then_inc(ab_done, 1)
                pe.wait_ge(ab_dve, 6)
                for a in range(3):
                    for t in range(TT):
                        o = (a * TT + t) * 8
                        m = pe.transpose(ps[:, 2, o:o + 8], rows[:, a, t * P:(t + 1) * P], tab[0:8, 0:8])
                m.then_inc(ab_tr, 1)

            @block.scalar
            def _(act):
                n = [0]

                def step(ins):
                    n[0] += 1
                    ins.then_inc(ab_act, 1)
                    act.wait_ge(ab_act, n[0])
                act.wait_ge(ab_done, 1)
                step(act.activation(rows[:, 1, :], ps[0:8, 0, :], ACT.Sigmoid))
                step(act.activation(ea[:, :], ab8[:, 0:1], ACT.Exp))
                step(act.activation(rows[:, 3, :], ps[0:8, 1, :], ACT.Abs, bias=ab8[:, 1:2]))
                step(act.activation(rows[:, 3, :], rows[:, 3, :], ACT.Exp, scale=-1.0))
                step(act.activation(rows[:, 3, :], rows[:, 3, :], ACT.Ln, bias=1.0))
                act.wait_ge(ab_dve, 5)
                step(act.activation(rows[:, 3, :], rows[:, 0, :], ACT.Exp))

            @block.vector
            def _(ve):
                n = [0]

                def step(ins):
                    n[0] += 1
                    ins.then_inc(ab_dve, 1)
                    ve.wait_ge(ab_dve, n[0])
                ve.wait_ge(ab_act, 5)
                step(ve.tensor_scalar(rows[:, 0, :], ps[0:8, 1, :], ab8[:, 1:2], 0.0, ALU.add, ALU.max))
                step(ve.tensor_tensor(rows[:, 0, :], rows[:, 0, :], rows[:, 3, :], ALU.add))
                step(ve.tensor_scalar(rows[:, 3, :], rows[:, 0, :], ea[:, :], -1.0, ALU.mult, ALU.mult))
                step(ve.tensor_tensor_scan(rows[:, 0, :], tab[0:8, TABLES["resetd"]], rows[:, 3, :], 0.0,
                                           ALU.mult, ALU.add))
                step(ve.nop())
                ve.wait_ge(ab_act, 6)
                step(ve.tensor_tensor(rows[:, 2, :], rows[:, 1, :], rows[:, 3, :], ALU.mult))
                ve.wait_ge(ab_tr, 1)
                ve.tensor_copy(gcols[:, :, :, :].rearrange("p a t h -> p (a t h)"), ps[:, 2, 0:96]).then_inc(ab_cols, 1)

        st = gdn.enter_context(ExitStack())
        cin = sb("cin", [P, 2, 3, T + 3], on=st)
        cv = sb("cv", [P, 2, 3, T], on=st)
        sq = hctx[:, :, :].rearrange("p (u j b) t -> p u j (b t)", u=2, j=2)
        rs = sb("g_rs", [P, 2, 2, T], on=st)
        BG = STREAM["gdn"].start
        cin_zero = sem("cin_zero")
        (copied, gated_z, conv_step, conved, silued, squared, summed, mean_read, rooted, qk_step, qk_done) = (
            [sem(f"g_{n}{u}") for u in range(2)] for n in
            ("copied", "gated_z", "conv_step", "conved", "silued", "squared", "summed", "mean_read", "rooted",
             "qk_step", "qk_done"))
        with nc.Block() as block:
            @block.sync
            def _(sp):
                load_blocks(sp, STREAM["gdnout"].start + SLOTS)

            @block.gpsimd
            def _(pool):
                credit(pool, (copied, gated_z, conv_step, conved, silued, squared, summed, mean_read, rooted, qk_step,
                              qk_done))
                pool.memset(cin[:, :, :, 0:3], 0.0).then_inc(cin_zero, 1)

            @block.tensor
            def _(pe):
                with pe.Fori(0, HEADS // 2) as i:
                    for u in range(2):
                        for j in range(4):
                            if j < 2:
                                pe.wait_ge(mean_read[u], i * 2 + 1)
                            elif j == 2:
                                pe.wait_ge(copied[u], i * 3 + 1)
                            else:
                                pe.wait_ge(gated_z[u], i + 1)
                            dense_tile(pe, block_here(pe, BG + 4 * u + j, i), hn, ps[:, 4 * u + j, :])
                    for u in range(2):
                        for j in range(2):
                            pe.wait_ge(squared[u], i * 2 + j + 2)
                            pe.matmul(ps[:, 4 * u + j, :], ones, sq[:, u, j, :], start=True, stop=True).then_inc(summed[u], 1)

            @block.scalar
            def _(act):
                with act.Fori(0, HEADS // 2) as i:
                    for u in range(2):
                        for j in range(3):
                            act.wait_ge(blocks_done, i * 8 + BG + 4 * u + j + 1)
                            act.wait_ge(conved[u], i * 3 + 1)
                            act.activation(cin[:, u, j, 3:], ps[:, 4 * u + j, :], ACT.Copy).then_inc(copied[u], 1)
                        act.wait_ge(blocks_done, i * 8 + BG + 4 * u + 4)
                        apart(act)
                        act.activation(flat(Z[:, bass.ds(i * 2 + u, 1), :]), ps[:, 4 * u + 3, :], ACT.Silu).then_inc(gated_z[u], 1)
                    for u in range(2):
                        for j in range(3):
                            act.wait_ge(conved[u], i * 3 + j + 2)
                            apart(act)
                            out = cv[:, u, j, :] if j < 2 else flat(V[:, bass.ds(i * 2 + u, 1), :])
                            act.activation(out, cv[:, u, j, :], ACT.Silu).then_inc(silued[u], 1)
                        for j in range(2):
                            act.wait_ge(silued[u], i * 3 + j + 2)
                            act.wait_ge(summed[u], i * 2 + 1)
                            act.activation(sq[:, u, j, :], cv[:, u, j, :], ACT.Square).then_inc(squared[u], 1)
                    for u in range(2):
                        for j in range(2):
                            act.wait_ge(mean_read[u], i * 2 + j + 2)
                            act.activation(rs[:, u, j, :], rs[:, u, j, :], ACT.Sqrt).then_inc(rooted[u], 1)

            @block.vector
            def _(ve):
                ve.wait_ge(cin_zero, 1)
                with ve.Fori(0, HEADS // 2) as i:
                    for u in range(2):
                        for j in range(3):
                            ve.wait_ge(copied[u], i * 3 + j + 2)
                            if j == 2:
                                ve.wait_ge(silued[u], i * 3 + 1)
                            else:
                                ve.wait_ge(squared[u], i * 2 + 1)
                            for w in range(4):
                                tap = par[:, bass.ds((i * 2 + u) * 4 + PARAMS.at["conv"][0] + 32 * j + w, 1)]
                                if w == 0:
                                    ins = ve.tensor_scalar(cv[:, u, j, :], cin[:, u, j, 0:T], tap, None, ALU.mult)
                                else:
                                    ve.wait_ge(conv_step[u], i * 9 + 3 * j + w + 1)
                                    ins = ve.scalar_tensor_tensor(cv[:, u, j, :], cin[:, u, j, w:w + T], tap,
                                                                  cv[:, u, j, :], ALU.mult, ALU.add)
                                ins.then_inc(conv_step[u] if w < 3 else conved[u], 1)
                    for u in range(2):
                        for j in range(2):
                            ve.wait_ge(summed[u], i * 2 + j + 2)
                            ve.wait_ge(qk_done[u], i * 2 + 1)
                            ve.tensor_scalar(rs[:, u, j, :], ps[:, 4 * u + j, :], EPS, None, ALU.add).then_inc(mean_read[u], 1)
                    for u in range(2):
                        for j in range(2):
                            ve.wait_ge(rooted[u], i * 2 + j + 2)
                            ve.reciprocal(rs[:, u, j, :], rs[:, u, j, :]).then_inc(qk_step[u], 1)
                            ve.wait_ge(qk_step[u], i * 2 + j + 2)
                            ve.scalar_tensor_tensor(flat((Q, K)[j][:, bass.ds(i * 2 + u, 1), :]), cv[:, u, j, :],
                                                    (P ** -0.5, 1.0)[j], rs[:, u, j, :], ALU.mult, ALU.mult
                                                    ).then_inc(qk_done[u], 1)
        st.close()

        def tiles(x):
            return x.rearrange("p (n i) -> p n i", n=TT)

        def every_tile(mask):
            return mask.unsqueeze(1).to_broadcast([P, TT, P])
        KD = sb("KD", [P, HEADS, T], on=gdn)
        AT = hn
        st = gdn.enter_context(ExitStack())
        rowm = hctx[:, :, :].rearrange("p (u a b) t -> p u a (b t)", u=2, a=2)
        dm, aT_, bmT, mm_, tn, tT = (sb(f"inv_{n}", [P, 2, T], on=st) for n in ("dm", "aT", "bmT", "m", "t", "tT"))
        ks = sb("ks", [P, 2, T], on=st)
        vs = sml[:, 0:2 * T].rearrange("p (u t) -> p u t", u=2)
        names = ("staged", "rowed", "spread", "diff", "expd", "exprow", "paired", "dve", "qdec", "t_tr", "kv_tr",
                 "t_copy", "kv_ready", "masked", "m_done", "m_copy", "xy_done", "updated", "fin_done", "fin_kept")
        S = {n: [sem(f"i_{n}{u}") for u in range(2)] for n in names}
        with nc.Block() as block:
            @block.scalar
            def _(act):
                with act.Fori(0, HEADS // 2) as i:
                    heads = [bass.ds(i * 2 + u, 1) for u in range(2)]
                    for u in range(2):
                        act.wait_ge(S["fin_done"][u], i + 1)
                        apart(act)
                        act.activation(ks[:, u, :], flat(K[:, heads[u], :]), ACT.Copy).then_inc(S["staged"][u], 1)
                        act.activation(vs[:, u, :], flat(V[:, heads[u], :]), ACT.Copy).then_inc(S["staged"][u], 1)
                    for u in range(2):
                        act.wait_ge(S["diff"][u], i * 2 + 3)
                        act.activation(mm_[:, u, :], ps[:, 4 * u, :], ACT.Exp).then_inc(S["exprow"][u], 1)
                        act.activation(dm[:, u, :], dm[:, u, :], ACT.Exp).then_inc(S["expd"][u], 1)
                    for u in range(2):
                        act.wait_ge(S["t_tr"][u], i + 2)
                        act.activation(tn[:, u, :], ps[:, 4 * u + 2, :], ACT.Copy).then_inc(S["t_copy"][u], 1)
                    for lv in range(1, LEVELS + 1):
                        for u in range(2):
                            act.wait_ge(S["m_done"][u], i * LEVELS + lv + 1)
                            if lv == 1:
                                act.wait_ge(S["qdec"][u], i + 2)
                            act.activation(mm_[:, u, :], ps[:, 4 * u + 2, :], ACT.Copy).then_inc(S["m_copy"][u], 1)

            @block.gpsimd
            def _(pool):
                credit(pool, S.values())
                with pool.Fori(0, HEADS // 2) as i:
                    heads = [bass.ds(i * 2 + u, 1) for u in range(2)]
                    for u in range(2):
                        pool.wait_ge(S["exprow"][u], i + 2)
                        pool.wait_ge(S["paired"][u], i + 2)
                        apart(pool)
                        q = flat(Q[:, heads[u], :])
                        pool.tensor_tensor(q, q, mm_[:, u, :], ALU.mult).then_inc(S["qdec"][u], 1)
                    for lv in range(1, LEVELS + 1):
                        for u in range(2):
                            if lv == 1:
                                pool.wait_ge(S["dve"][u], i * 8 + 8 + 1)
                            pool.wait_ge(S["m_done"][u], i * LEVELS + lv - 1 + 1)
                            m0 = TABLES.at["level"][0] + lv * P
                            pool.tensor_tensor(tiles(bmT[:, u, :]), tiles(aT_[:, u, :]),
                                               every_tile(tab[:, m0:m0 + P]), ALU.mult).then_inc(S["masked"][u], 1)

            @block.vector
            def _(ve):
                with ve.Fori(0, HEADS // 2) as i:
                    heads = [bass.ds(i * 2 + u, 1) for u in range(2)]

                    def bycol(a, u):
                        return gcols[:, a, :, heads[u]].to_broadcast([P, TT, P])
                    for u in range(2):
                        for a in range(2):
                            ve.tensor_scalar(rowm[0:8, u, a, :], rows[:, a, :], tab[0:8, heads[u]], None,
                                             ALU.mult).then_inc(S["rowed"][u], 1)
                    for u in range(2):
                        ve.wait_ge(S["spread"][u], i + 2)
                        ve.tensor_tensor(tiles(dm[:, u, :]), tiles(ps[:, 4 * u, :]), bycol(0, u), ALU.subtract
                                         ).then_inc(S["diff"][u], 1)
                    for u in range(2):
                        ve.wait_ge(S["diff"][u], i * 2 + 2)
                        ve.tensor_scalar(dm[:, u, :], dm[:, u, :], 0.0, None, ALU.min).then_inc(S["diff"][u], 1)
                    for step in range(8):
                        for u in range(2):
                            d, at, t = tiles(dm[:, u, :]), tiles(aT_[:, u, :]), tiles(tT[:, u, :])
                            if step:
                                ve.wait_ge(S["dve"][u], i * 8 + step + 1)
                            if step == 0:
                                ve.wait_ge(S["expd"][u], i + 2)
                                ins = ve.tensor_tensor(d, d, every_tile(tab[:, TABLES["incl"]]), ALU.mult)
                            elif step == 1:
                                ve.wait_ge(S["paired"][u], i + 2)
                                ins = ve.tensor_tensor(flat(AT[:, heads[u], :]), ps[:, 4 * u + 3, :], dm[:, u, :], ALU.mult)
                            elif step == 2:
                                ins = ve.tensor_tensor(at, d, every_tile(tab[:, TABLES["strict"]]), ALU.mult)
                            elif step == 3:
                                ins = ve.tensor_tensor(aT_[:, u, :], ps[:, 4 * u + 1, :], aT_[:, u, :], ALU.mult)
                            elif step == 4:
                                ins = ve.tensor_tensor(aT_[:, u, :], ps[:, 4 * u + 2, :], aT_[:, u, :], ALU.mult)
                            elif step == 5:
                                m0 = TABLES.at["level"][0]
                                ins = ve.tensor_tensor(t, at, every_tile(tab[:, m0:m0 + P]), ALU.mult)
                            elif step == 6:
                                ins = ve.tensor_tensor(t, every_tile(ident), t, ALU.subtract)
                            else:
                                ve.wait_ge(S["exprow"][u], i + 2)
                                apart(ve)
                                ins = ve.tensor_copy(egl[:, heads[u], :].rearrange("p a n -> p n a"),
                                                     tiles(mm_[:, u, :])[:, :, P - 1:P])
                            ins.then_inc(S["dve"][u], 1)
                    for u in range(2):
                        ve.wait_ge(S["kv_tr"][u], i + 2)
                        ktok, vtok_ = tiles(ps[:, 4 * u, :]), tiles(ps[:, 4 * u + 1, :])
                        ve.tensor_tensor(flat(KD[:, heads[u], :]).rearrange("p (n i) -> p n i", n=TT), ktok,
                                         tiles(dm[:, u, :])[:, :, P - 1:P].to_broadcast([P, TT, P]), ALU.mult
                                         ).then_inc(S["kv_ready"][u], 1)
                        ve.tensor_tensor(tiles(ks[:, u, :]), ktok, bycol(2, u), ALU.mult).then_inc(S["kv_ready"][u], 1)
                        ve.tensor_tensor(tiles(vs[:, u, :]), vtok_, bycol(1, u), ALU.mult).then_inc(S["kv_ready"][u], 1)
                    for lv in range(1, LEVELS + 1):
                        for u in range(2):
                            ve.wait_ge(S["xy_done"][u], i * LEVELS + lv + 1)
                            ve.tensor_tensor(tT[:, u, :], tT[:, u, :], ps[:, 4 * u + 2, :], ALU.subtract
                                             ).then_inc(S["updated"][u], 1)
                            if lv < LEVELS:
                                ve.tensor_tensor(tn[:, u, :], tn[:, u, :], ps[:, 4 * u + 3, :], ALU.subtract
                                                 ).then_inc(S["updated"][u], 1)
                    for u in range(2):
                        ve.wait_ge(S["fin_done"][u], i + 2)
                        for n, keep in enumerate((V, K)):
                            ve.tensor_scalar(flat(keep[:, heads[u], :]), ps[:, 4 * u + n, :], 1.0, None, ALU.mult
                                             ).then_inc(S["fin_kept"][u], 1)

            @block.tensor
            def _(pe):
                def four(out, lhsT, rhs):
                    for n in range(TT):
                        c = slice(n * P, (n + 1) * P)
                        m = pe.matmul(out[:, c], lhsT[:, c], rhs[:, c], start=True, stop=True)
                    return m
                with pe.Fori(0, HEADS // 2) as i:
                    heads = [bass.ds(i * 2 + u, 1) for u in range(2)]
                    B = [[ps[:, 4 * u + n, :] for n in range(4)] for u in range(2)]
                    for u in range(2):
                        pe.wait_ge(S["rowed"][u], i * 2 + 2 + 1)
                        pe.wait_ge(S["fin_kept"][u], i * 2 + 1)
                        for a in range(2):
                            m = pe.matmul(B[u][a], tab[0:8, TABLES["ones"]], rowm[0:8, u, a, :], start=True, stop=True)
                        m.then_inc(S["spread"][u], 1)
                    for u in range(2):
                        pe.wait_ge(S["staged"][u], i * 2 + 2 + 1)
                        pe.wait_ge(S["updated"][u], i * (2 * LEVELS - 1) + 1)
                        four(B[u][2], ks[:, u, :], ks[:, u, :])
                        for n in range(TT):
                            q = Q[:, heads[u], n * P:(n + 1) * P]
                            m = pe.matmul(B[u][3][:, n * P:(n + 1) * P], ks[:, u, n * P:(n + 1) * P], flat(q),
                                          start=True, stop=True)
                        m.then_inc(S["paired"][u], 1)
                    for u in range(2):
                        pe.wait_ge(S["dve"][u], i * 8 + 7 + 1)
                        for n in range(TT):
                            c = slice(n * P, (n + 1) * P)
                            m = pe.transpose(B[u][2][:, c], tT[:, u, c], ident)
                        m.then_inc(S["t_tr"][u], 1)
                        pe.wait_ge(S["exprow"][u], i + 2)
                        for n in range(TT):
                            c = slice(n * P, (n + 1) * P)
                            pe.transpose(B[u][0][:, c], ks[:, u, c], ident)
                            m = pe.transpose(B[u][1][:, c], vs[:, u, c], ident)
                        m.then_inc(S["kv_tr"][u], 1)
                    for lv in range(1, LEVELS + 1):
                        for u in range(2):
                            pe.wait_ge(S["masked"][u], i * LEVELS + lv + 1)
                            pe.wait_ge(S["t_copy"][u], i + 2)
                            pe.wait_ge(S["updated"][u], i * (2 * LEVELS - 1) + 2 * (lv - 1) + 1)
                            four(B[u][2], bmT[:, u, :], tn[:, u, :]).then_inc(S["m_done"][u], 1)
                        for u in range(2):
                            pe.wait_ge(S["m_copy"][u], i * LEVELS + lv + 1)
                            if lv < LEVELS:
                                four(B[u][3], tT[:, u, :], mm_[:, u, :])
                            four(B[u][2], mm_[:, u, :], tT[:, u, :]).then_inc(S["xy_done"][u], 1)
                    for u in range(2):
                        pe.wait_ge(S["updated"][u], i * (2 * LEVELS - 1) + 2 * LEVELS - 1 + 1)
                        pe.wait_ge(S["kv_ready"][u], i * 3 + 3 + 1)
                        four(B[u][0], tT[:, u, :], vs[:, u, :])
                        four(B[u][1], ks[:, u, :], tT[:, u, :]).then_inc(S["fin_done"][u], 1)
        st.close()

        retire()
        st = gdn.enter_context(ExitStack())
        St = sb("St", [P, HEADS, P], on=st)
        vn = sb("vn", [P, HEADS, P], on=st)
        s_zero, ws_done, vn_done, so_done, sd_done, o_kept2 = (
            [sem(f"{n}{g}") for g in range(2)] for n in ("s_zero", "ws_done", "vn_done", "so_done", "sd_done", "o_kept2"))
        s_next = [sem(f"s_next{g}") for g in range(2)]
        with nc.Block() as block:
            @block.tensor
            def _(pe):
                for n in range(TT):
                    c = slice(n * P, (n + 1) * P)
                    for g in range(2):
                        pe.wait_ge(s_next[g], 2 * n + 1)
                        for h in range(4):
                            m = pe.matmul(ps[:, g, h * P:(h + 1) * P], K[:, 4 * g + h, c], St[:, 4 * g + h, :],
                                          start=True, stop=True)
                        m.then_inc(ws_done[g], 1)
                    for g in range(2):
                        pe.wait_ge(vn_done[g], n + 1)
                        if n:
                            pe.wait_ge(o_kept2[g], n)
                        for h in range(4):
                            out = ps[:, 2 + g, h * P:(h + 1) * P]
                            pe.matmul(out, St[:, 4 * g + h, :], Q[:, 4 * g + h, c], start=True, stop=False)
                            m = pe.matmul(out, vn[:, 4 * g + h, :], AT[:, 4 * g + h, c], start=False, stop=True)
                        m.then_inc(so_done[g], 1)
                        if n < TT - 1:
                            for h in range(4):
                                m = pe.matmul(ps[:, 4 + g, h * P:(h + 1) * P], KD[:, 4 * g + h, c],
                                              vn[:, 4 * g + h, :], start=True, stop=True)
                            m.then_inc(sd_done[g], 1)

            @block.vector
            def _(ve):
                for g in range(2):
                    ve.memset(St[:, 4 * g:4 * g + 4, :], 0.0).then_inc(s_next[g], 1)
                for n in range(TT):
                    for g in range(2):
                        hs = slice(4 * g, 4 * g + 4)
                        ve.wait_ge(ws_done[g], n + 1)
                        if n:
                            ve.wait_ge(sd_done[g], n)
                            ve.wait_ge(so_done[g], n)
                        ve.tensor_tensor(vn[:, hs, :], V[:, hs, n * P:(n + 1) * P],
                                         ps[:, g, :].rearrange("p (h e) -> p h e", h=4), ALU.subtract
                                         ).then_inc(vn_done[g], 1)
                    for g in range(2):
                        if n == TT - 1:
                            break
                        hs = slice(4 * g, 4 * g + 4)
                        ve.wait_ge(so_done[g], n + 1)
                        ve.tensor_tensor(St[:, hs, :], St[:, hs, :], egl[:, hs, n:n + 1].to_broadcast([P, 4, P]),
                                         ALU.mult).then_inc(s_next[g], 1)
                        ve.wait_ge(s_next[g], 2 * n + 2)
                        ve.wait_ge(sd_done[g], n + 1)
                        ve.tensor_tensor(St[:, hs, :], St[:, hs, :], ps[:, 4 + g, :].rearrange("p (h e) -> p h e", h=4),
                                         ALU.add).then_inc(s_next[g], 1)

            @block.scalar
            def _(act):
                for n in range(TT):
                    for g in range(2):
                        act.wait_ge(so_done[g], n + 1)
                        act.activation(Q[:, 4 * g:4 * g + 4, n * P:(n + 1) * P],
                                       ps[:, 2 + g, :].rearrange("p (h e) -> p h e", h=4), ACT.Copy
                                       ).then_inc(o_kept2[g], 1)
        st.close()

        on_sq, on_sum, on_ms, on_root, on_step, on_done = (
            sem(n) for n in ("on_sq", "on_sum", "on_ms", "on_root", "on_step", "on_done"))
        with nc.Block() as block:
            @block.scalar
            def _(act):
                for h in range(HEADS):
                    act.activation(hn[:, h, :], Q[:, h, :], ACT.Square).then_inc(on_sq, 1)
                for h in range(HEADS):
                    act.wait_ge(on_ms, h + 1)
                    act.activation(mix[:, h, :], mix[:, h, :], ACT.Sqrt).then_inc(on_root, 1)

            @block.tensor
            def _(pe):
                for h in range(HEADS):
                    pe.wait_ge(on_sq, h + 1)
                    pe.matmul(ps[:, h, :], ones, hn[:, h, :], start=True, stop=True).then_inc(on_sum, 1)

            @block.vector
            def _(ve):
                for h in range(HEADS):
                    ve.wait_ge(on_sum, h + 1)
                    ve.tensor_scalar(mix[:, h, :], ps[:, h, :], 1.0 / P, EPS, ALU.mult, ALU.add).then_inc(on_ms, 1)
                for h in range(HEADS):
                    ve.wait_ge(on_root, h + 1)
                    ve.reciprocal(mix[:, h, :], mix[:, h, :]).then_inc(on_step, 1)
                    ve.wait_ge(on_step, 2 * h + 1)
                    ve.scalar_tensor_tensor(mix[:, h, :], Q[:, h, :], col("ogain"), mix[:, h, :], ALU.mult, ALU.mult
                                            ).then_inc(on_step, 1)
                    ve.wait_ge(on_step, 2 * h + 2)
                    ve.tensor_tensor(Q[:, h, :], mix[:, h, :], Z[:, h, :], ALU.mult).then_inc(on_done, 1)
        project_out("gdnout", Q, STREAM["gdnout"].start, None, STREAM["gu0"].start + SLOTS)
        gdn.close()

        def feed_forward(layer):
            norm(f"fn{layer}", res, hn, lambda k: col("ffn", 8 * layer + k))
            with ExitStack() as st:
                act_ = sb(f"ff_act{layer}", [P, FT, T], on=st)
                sg = sb(f"ff_sg{layer}", [P, 4, T], on=st)
                B0 = STREAM[f"gu{layer}"].start
                B1 = STREAM[f"down{layer}"].start
                silu_done, act_ready, added = (sem(f"ff_{n}{layer}") for n in ("silu", "act", "added"))
                turns, rest = FT // 4, FT % 4
                with nc.Block() as block:
                    @block.sync
                    def _(sp):
                        load_blocks(sp, B1 + FT + SLOTS)

                    @block.tensor
                    def _(pe):
                        def up(i, pairs, extra):
                            for j in range(2 * pairs):
                                pe.wait_ge(act_ready, i * 4 + extra + j // 2 + 1)
                                if extra:
                                    w = block_here(pe, B0 + 2 * extra + j)
                                else:
                                    w = block_here(pe, B0 + j, i)
                                dense_tile(pe, w, hn, ps[:, j, :])
                        with pe.Fori(0, turns) as i:
                            up(i, 4, 0)
                        up(0, rest, 4 * turns)
                        pe.wait_ge(act_ready, 4 + FT)
                        for f in range(FT):
                            w = block_here(pe, B1 + f)
                            for n in range(KT):
                                m = pe.matmul(ps[:, n, :], w[:, n * P:(n + 1) * P], act_[:, f, :],
                                              start=f == 0, stop=f == FT - 1)
                            m.then_inc(blocks_done, 1)

                    @block.scalar
                    def _(act):
                        def gate(i, pairs, extra):
                            for p in range(pairs):
                                act.wait_ge(blocks_done, i * 8 + B0 + 2 * extra + 2 * p + 1)
                                act.wait_ge(act_ready, i * 4 + extra + p + 1)
                                act.activation(sg[:, p, :], ps[:, 2 * p, :], ACT.Silu).then_inc(silu_done, 1)
                        with act.Fori(0, turns) as i:
                            gate(i, 4, 0)
                        gate(0, rest, 4 * turns)

                    @block.vector
                    def _(ve):
                        ve.sem_inc(act_ready, 4)

                        def gated(i, pairs, extra):
                            for p in range(pairs):
                                ve.wait_ge(silu_done, i * 4 + extra + p + 1)
                                ve.wait_ge(blocks_done, i * 8 + B0 + 2 * extra + 2 * p + 2)
                                ve.tensor_tensor(flat(act_[:, bass.ds(i * 4 + extra + p, 1), :]), sg[:, p, :],
                                                 ps[:, 2 * p + 1, :], ALU.mult).then_inc(act_ready, 1)
                        with ve.Fori(0, turns) as i:
                            gated(i, 4, 0)
                        gated(0, rest, 4 * turns)
                        ve.wait_ge(blocks_done, B1 + FT)
                        for n in range(KT):
                            ve.tensor_tensor(res[:, n, :], ps[:, n, :], res[:, n, :], ALU.add).then_inc(added, 1)

        feed_forward(0)

        retire()
        sbt = ctx.enter_context(ExitStack())
        Q = sb("sbQ", [P, HEADS, T], on=sbt)
        K = sb("sbK", [P, HEADS, T], on=sbt)
        V = mix[:, :, :].rearrange("p (t a) (c d) -> p t (a c) d", a=2, d=P)
        st = sbt.enter_context(ExitStack())
        hk = sb("hk", [P, KT, T], on=st)
        norm("kv", res, hk, lambda k: col("kvn", k))
        norm("an", res, hn, lambda k: col("attn", 8 + k))
        sq = sb("sb_sq", [P, HEADS, T], on=st)
        rs = sb("sb_rs", [P, HEADS, T], on=st)

        def heads_normed(name, src, dst, gain, first_block):
            squared, summed, mean_read, rooted, step, done = (
                sem(f"{name}_{n}") for n in ("squared", "summed", "mean_read", "rooted", "step", "done"))
            with nc.Block() as block:
                @block.sync
                def _(sp):
                    load_blocks(sp, first_block + HEADS + SLOTS)

                @block.tensor
                def _(pe):
                    for q in (0, 4):
                        for h in range(q, q + 4):
                            if q:
                                pe.wait_ge(done, h - 3)
                            dense_tile(pe, block_here(pe, first_block + h), src, ps[:, h % 4, :])
                        for h in range(q, q + 4):
                            pe.wait_ge(squared, h + 1)
                            if q:
                                pe.wait_ge(mean_read, h - 3)
                            pe.matmul(ps[:, 4 + h % 4, :], ones, sq[:, h, :], start=True, stop=True).then_inc(summed, 1)

                @block.scalar
                def _(act):
                    for q in (0, 4):
                        for h in range(q, q + 4):
                            act.wait_ge(blocks_done, first_block + h + 1)
                            act.activation(sq[:, h, :], ps[:, h % 4, :], ACT.Square).then_inc(squared, 1)
                        for h in range(q, q + 4):
                            act.wait_ge(mean_read, h + 1)
                            act.activation(rs[:, h, :], rs[:, h, :], ACT.Sqrt).then_inc(rooted, 1)

                @block.vector
                def _(ve):
                    for q in (0, 4):
                        for h in range(q, q + 4):
                            ve.wait_ge(summed, h + 1)
                            ve.tensor_scalar(rs[:, h, :], ps[:, 4 + h % 4, :], 1.0 / P, EPS, ALU.mult, ALU.add
                                             ).then_inc(mean_read, 1)
                        for h in range(q, q + 4):
                            ve.wait_ge(rooted, h + 1)
                            ve.reciprocal(rs[:, h, :], rs[:, h, :]).then_inc(step, 1)
                            ve.wait_ge(step, h + 1)
                            ve.wait_ge(squared, h + 1)
                            ve.scalar_tensor_tensor(dst[:, h, :], ps[:, h % 4, :], gain, rs[:, h, :],
                                                    ALU.mult, ALU.mult).then_inc(done, 1)

        heads_normed("kh", hk, K, col("kgain"), STREAM["sbk"].start)
        v_kept = sem("v_kept")
        BV2 = STREAM["sbv"].start
        with nc.Block() as block:
            @block.sync
            def _(sp):
                load_blocks(sp, STREAM["sbq"].start + SLOTS)

            @block.tensor
            def _(pe):
                for k in range(KT):
                    w = block_here(pe, BV2 + k)
                    for n in range(8):
                        t, half = n // 2, n % 2
                        m = pe.matmul(ps[:, n, :], hk[:, k, t * P:(t + 1) * P], w[:, half * 512:(half + 1) * 512],
                                      start=k == 0, stop=k == KT - 1)
                    m.then_inc(blocks_done, 1)

            @block.scalar
            def _(act):
                act.wait_ge(blocks_done, BV2 + KT)
                for n in range(8):
                    act.activation(mix[:, n, :], ps[:, n, :], ACT.Copy).then_inc(v_kept, 1)
        heads_normed("qh", hn, Q, col("qgain"), STREAM["sbq"].start)
        st.close()

        WIDTH = [T - a * P for a in range(TT)]
        OFF = [sum(WIDTH[:a]) for a in range(TT)]
        PACKED = sum(WIDTH)
        scale = float(P) ** -0.5
        st = sbt.enter_context(ExitStack())
        ks = sb("a_ks", [P, 2, T], on=st)
        vs = sb("a_vs", [P, 2, TT, P], on=st)
        lo, sp_, ln = (sb(f"a_{n}", [P, 2, PACKED], on=st) for n in ("lo", "sp", "ln"))
        names = ("staged", "z_done", "abs_done", "ln_done", "z_read", "summed", "fail_ready", "rest_done", "log_a",
                 "exp_done", "att_ready", "o_done", "o_kept")
        A = {n: [sem(f"a_{n}{u}") for u in range(2)] for n in names}
        with nc.Block() as block:
            @block.scalar
            def _(act):
                with act.Fori(0, HEADS // 2) as i:
                    heads = [bass.ds(i * 2 + u, 1) for u in range(2)]
                    for u in range(2):
                        act.wait_ge(A["o_done"][u], i + 1)
                        apart(act)
                        act.activation(ks[:, u, :], flat(K[:, heads[u], :]), ACT.Copy).then_inc(A["staged"][u], 1)
                        act.activation(vs[:, u, :, :], V[:, :, heads[u], :].rearrange("p t a d -> p t (a d)"), ACT.Copy
                                       ).then_inc(A["staged"][u], 1)
                    for u in range(2):
                        act.wait_ge(A["z_done"][u], i + 2)
                        for a in range(TT):
                            act.activation(ln[:, u, OFF[a]:OFF[a] + WIDTH[a]], ps[:, 4 * u + a, 0:WIDTH[a]], ACT.Abs,
                                           scale=scale).then_inc(A["abs_done"][u], 1)
                    for u in range(2):
                        act.wait_ge(A["abs_done"][u], i * 4 + 4 + 1)
                        act.activation(ln[:, u, :], ln[:, u, :], ACT.Exp, scale=-1.0).then_inc(A["ln_done"][u], 1)
                        act.wait_ge(A["ln_done"][u], i * 2 + 2)
                        act.activation(ln[:, u, :], ln[:, u, :], ACT.Ln, bias=1.0).then_inc(A["ln_done"][u], 1)
                    for u in range(2):
                        act.wait_ge(A["log_a"][u], i * 4 + 4 + 1)
                        act.activation(lo[:, u, :], lo[:, u, :], ACT.Exp).then_inc(A["exp_done"][u], 1)
                    for u in range(2):
                        act.wait_ge(A["o_done"][u], i + 2)
                        apart(act)
                        act.activation(flat(Q[:, heads[u], :]), ps[:, 4 * u, :], ACT.Copy).then_inc(A["o_kept"][u], 1)

            @block.gpsimd
            def _(pool):
                credit(pool, A.values())
                with pool.Fori(0, HEADS // 2) as i:
                    for u in range(2):
                        pool.wait_ge(A["summed"][u], i * 2 + 2 + 1)
                        for a in range(TT):
                            d = sp_[:, u, OFF[a]:OFF[a] + P]
                            pool.tensor_tensor(d, d, tab[:, TABLES["strict"]], ALU.mult).then_inc(A["fail_ready"][u], 1)
                    for u in range(2):
                        pool.wait_ge(A["exp_done"][u], i + 2)
                        for a in range(TT):
                            d = lo[:, u, OFF[a]:OFF[a] + P]
                            pool.tensor_tensor(d, d, tab[:, TABLES["strict"]], ALU.mult).then_inc(A["att_ready"][u], 1)

            @block.vector
            def _(ve):
                with ve.Fori(0, HEADS // 2) as i:
                    for u in range(2):
                        ve.wait_ge(A["o_done"][u], i + 1)
                        for a in range(TT):
                            c = slice(OFF[a], OFF[a] + WIDTH[a])
                            z = ps[:, 4 * u + a, 0:WIDTH[a]]
                            ve.wait_ge(A["abs_done"][u], i * 4 + a + 2)
                            ve.tensor_scalar(lo[:, u, c], z, scale, 0.0, ALU.mult, ALU.min).then_inc(A["z_read"][u], 1)
                            ve.tensor_scalar(sp_[:, u, c], z, scale, 0.0, ALU.mult, ALU.max).then_inc(A["z_read"][u], 1)
                    for u in range(2):
                        ve.wait_ge(A["z_read"][u], i * 8 + 8 + 1)
                        ve.wait_ge(A["ln_done"][u], i * 2 + 2 + 1)
                        ve.tensor_tensor(sp_[:, u, :], sp_[:, u, :], ln[:, u, :], ALU.add).then_inc(A["summed"][u], 1)
                        ve.tensor_tensor(lo[:, u, :], lo[:, u, :], ln[:, u, :], ALU.subtract).then_inc(A["summed"][u], 1)
                    for u in range(2):
                        ve.wait_ge(A["summed"][u], i * 2 + 2 + 1)
                        ve.wait_ge(A["rest_done"][u], i + 2)
                        for a in range(TT):
                            c = slice(OFF[a], OFF[a] + WIDTH[a])
                            ve.tensor_tensor(lo[:, u, c], lo[:, u, c], ps[:, 4 * u + a, 0:WIDTH[a]], ALU.subtract
                                             ).then_inc(A["log_a"][u], 1)

            @block.tensor
            def _(pe):
                with pe.Fori(0, HEADS // 2) as i:
                    heads = [bass.ds(i * 2 + u, 1) for u in range(2)]
                    for u in range(2):
                        pe.wait_ge(A["staged"][u], i * 2 + 2 + 1)
                        pe.wait_ge(A["o_kept"][u], i + 1)
                        for a in range(TT):
                            m = pe.matmul(ps[:, 4 * u + a, 0:WIDTH[a]], ks[:, u, a * P:(a + 1) * P],
                                          flat(Q[:, heads[u], a * P:T]), start=True, stop=True)
                        m.then_inc(A["z_done"][u], 1)
                    for u in range(2):
                        pe.wait_ge(A["fail_ready"][u], i * 4 + 4 + 1)
                        for a in range(TT):
                            for b in range(a, TT):
                                m = pe.matmul(ps[:, 4 * u + a, (b - a) * P:WIDTH[a]],
                                              tab[:, TABLES["after"]] if a == b else ones,
                                              sp_[:, u, OFF[b]:OFF[b] + WIDTH[b]], start=a == b, stop=a == b,
                                              skip_group_check=a != b)
                        m.then_inc(A["rest_done"][u], 1)
                    for u in range(2):
                        pe.wait_ge(A["att_ready"][u], i * 4 + 4 + 1)
                        for a in range(TT):
                            m = pe.matmul(ps[:, 4 * u, a * P:T], vs[:, u, a, :], lo[:, u, OFF[a]:OFF[a] + WIDTH[a]],
                                          start=a == 0, stop=a == 0, skip_group_check=a != 0)
                        m.then_inc(A["o_done"][u], 1)
        st.close()
        project_out("sbout", Q, STREAM["sbout"].start, None, STREAM["gu1"].start + SLOTS)
        sbt.close()
        feed_forward(1)
        stored = sem("stored")
        with nc.Block() as block:
            @block.sync
            def _(sp):
                sp.dma_start(outT.rearrange("(k p) t -> p k t", p=P), res[:, :, :]).then_inc(stored, 16)
                sp.wait_ge(stored, 16)

def kernel(**inputs):
    import concourse.bacc as bacc
    from concourse.bass_utils import run_bass_kernel_spmd

    a = {k: np.asarray(v) for k, v in inputs.items()}

    def by_tile(w):
        return w.reshape(KT, P, -1, P).transpose(2, 1, 0, 3).reshape(-1, P, 1024)

    def by_row(w):
        return w.reshape(-1, P, 1024)

    def pairs(w):
        return w.reshape(4, 2, P, 512).transpose(0, 2, 1, 3).reshape(4, P, 1024)

    def column(v):
        return v.reshape(-1, P).T

    w_in, gdn = a["w_in"][0], a["gdn_w_in_2"][0]
    ei = by_tile(a["w_expert_in"][0].transpose(1, 0, 2).reshape(D, NEXP * 512)).reshape(NEXP, 4, P, 1024)
    ei = ei[:, [0, 2, 1, 3]]
    eo = by_row(a["w_expert_out"][0].reshape(-1, D)).reshape(NEXP, 2, P, 1024)
    gt = by_tile(gdn[:, :4096]).reshape(4, 8, P, 1024).transpose(1, 0, 2, 3)
    gu = [by_tile(w).reshape(2, FT, P, 1024).transpose(1, 0, 2, 3).reshape(-1, P, 1024) for w in a["ffn_w_gu_2"]]
    stream = np.concatenate([
        by_tile(a["w_ada"][0]), by_tile(w_in[:, 256:512]), pairs(w_in[:, 512:1024]), by_tile(w_in[:, 0:256]),
        by_tile(w_in[:, 1024:1536]), by_tile(w_in[:, 1568:2080]), by_tile(a["w_out"][0]),
        np.concatenate([ei, eo], axis=1).reshape(-1, P, 1024), gt.reshape(-1, P, 1024),
        by_tile(a["gdn_w_out_2"][0]), gu[0], by_row(a["ffn_w_down_2"][0]), by_tile(a["w_kv_2"][:, :D]),
        by_row(a["w_kv_2"][:, D:]), by_tile(a["sb_w_q_2"][0]), by_tile(a["sb_w_out_2"][0]), gu[1],
        by_row(a["ffn_w_down_2"][1])])
    small = np.concatenate([
        w_in[:, 1536:1568].reshape(KT, P, 32).transpose(1, 0, 2).reshape(P, -1),
        gdn[:, 4096:4112].reshape(KT, P, 16).transpose(1, 0, 2).reshape(P, -1),
        np.concatenate([a["w_router_group"][0], a["w_router_expert"][0]], axis=1).reshape(KT, P, 36)
        .transpose(1, 0, 2).reshape(P, -1),
        a["w_pool"][0].transpose(1, 0, 2).reshape(P, -1)], axis=1)
    params = np.concatenate([
        column(a["b_ada"][0]), column(a["norm1_g"][0]), column(a["norm2_g"][0]), column(a["final_norm_g"]),
        column(a["attn_norm_2"].reshape(-1)), column(a["ffn_norm_2"].reshape(-1)), column(a["kv_norm_2"]),
        column(a["gla_norm_g"][0]), column(a["pool_scale"][0]), column(a["b_decay"][0].reshape(-1)),
        a["gdn_conv_w_2"][0].reshape(4, 24, P).transpose(2, 1, 0).reshape(P, 96), column(a["gdn_o_gain_2"][0]),
        column(a["k_gain_2"]), column(a["sb_q_gain_2"][0]),
        np.stack([a["c"][0], a["c_ctx"]], axis=1).reshape(KT, P, 2).transpose(1, 0, 2).reshape(P, 16)], axis=1)
    arrays = {
        "xT": a["x"][0].T, "ctxT": a["ctx"][0].T, "stream": stream, "small": small, "params": params,
        "heads8": np.stack([a["gdn_a_log_2"][0], a["gdn_dt_bias_2"][0]], axis=1), "wdec": a["w_decay"][0],
        "table": tables()}
    arrays = {k: np.ascontiguousarray(v) for k, v in arrays.items()}
    nc = bacc.Bacc("TRN2", target_bir_lowering=False, num_devices=1)
    aps = [nc.dram_tensor(k, v.shape, F32, kind="ExternalInput").ap() for k, v in arrays.items()]
    out = nc.dram_tensor("outT", (D, T), F32, kind="ExternalOutput").ap()
    program(nc, *aps, out)
    r = run_bass_kernel_spmd(nc, [arrays], core_ids=[0])
    return np.ascontiguousarray(r.results[0]["outT"].T)[None]
```

```python
from contextlib import ExitStack

import numpy as np
import concourse.bass as bass
from concourse import mybir

F32 = mybir.dt.float32
U8 = mybir.dt.uint8
F32R = mybir.dt.float32r
ALU = mybir.AluOpType
ACT = mybir.ActivationFunctionType
AX = mybir.AxisListType
P = 128
D = 1024
KT = D // P
T = 512
TT = T // P
CTX = 256
TA = T + CTX
EPS = 1e-6
SLOTS = 8
NEXP = 32
FF = 2816
FT = FF // P
HEADS = 8
GRID_W = 64
ROWS = T // GRID_W
WINDOWS = (2, 4, 8, 16)
LEVELS = 6
MASKED_LOW = -3.0e38
MAXTILES = 40
MINTILES = 2 * T // P


class Cols:

    def __init__(self, parts):
        self.at, n = {}, 0
        for name, width in parts:
            self.at[name] = (n, n + width)
            n += width
        self.n = n

    def __getitem__(self, name):
        return slice(*self.at[name])


PARAMS = Cols([("b_ada", 48), ("norm1", 8), ("norm2", 8), ("final", 8), ("attn", 16), ("ffn", 16), ("kvn", 8),
               ("gla", 1), ("pscale", 4), ("bdec", 4), ("conv", 96), ("ogain", 1), ("kgain", 1), ("qgain", 1),
               ("cvec", 16)])
TABLES = Cols([("ident", P), ("ones", P), ("incl", P), ("strict", P), ("after", P),
               ("glaf", P), ("glab", P), ("level", P * (LEVELS + 1)), ("rank", 8), ("resetg", TA), ("resetd", T),
               ("rcount", 4 * T), ("tile", MAXTILES), ("token", TT)])
STREAM = Cols([("ada", 48), ("k", 2), ("v", 4), ("q", 2), ("g", 4), ("p", 4), ("out", 8),
               ("gdn", 32), ("gdnout", 8), ("gu0", 2 * FT), ("down0", FT), ("sbk", 8), ("sbv", 8), ("sbq", 8),
               ("sbout", 8), ("gu1", 2 * FT), ("down1", FT)])
SMALL = Cols([("wa", 8 * 32), ("wab", 8 * 16), ("router", 8 * 36), ("pool", 4 * P)])


def tables():
    t = np.zeros((P, TABLES.n), np.float32)
    j, i = np.arange(P)[:, None], np.arange(P)[None, :]
    t[:, TABLES["ident"]] = j == i
    t[:, TABLES["ones"]] = 1
    t[:, TABLES["incl"]] = j <= i
    t[:, TABLES["strict"]] = j < i
    t[:, TABLES["after"]] = j > i
    same = j // 64 == i // 64
    t[:, TABLES["glaf"]] = same & (j <= i)
    t[:, TABLES["glab"]] = same & (j >= i)
    lv = t[:, TABLES["level"]].reshape(P, LEVELS + 1, P)
    for n in range(LEVELS + 1):
        s = 1 << n
        lv[:, n] = (j // (2 * s) == i // (2 * s)) & (j % (2 * s) < s) & (i % (2 * s) >= s)
    t[:, TABLES["level"]] = lv.reshape(P, -1)
    t[:, TABLES["rank"]] = 8 - np.arange(8)
    t[:, TABLES["resetg"]] = np.arange(TA) % 64 != 0
    t[:, TABLES["resetd"]] = np.arange(T) % P != 0
    rc = np.zeros((4, ROWS, GRID_W), np.float32)
    for g, w in enumerate(WINDOWS):
        lo, hi = w // 2, w - 1 - w // 2
        count = [np.clip(np.arange(n) + hi + 1, 0, n) - np.clip(np.arange(n) - lo, 0, n) for n in (ROWS, GRID_W)]
        rc[g] = 1.0 / (count[0][:, None] * count[1][None, :])
    t[:, TABLES["rcount"]] = rc.reshape(1, -1)
    t[:, TABLES["tile"]] = np.arange(MAXTILES)
    t[:, TABLES["token"]] = np.arange(P)[:, None] + P * np.arange(TT)
    return t


def flat(ap):
    return ap.rearrange("p a n -> p (a n)")


def program(nc, xT, ctxT, stream, experts, small, params, heads8, wdec, table, outT):
    with ExitStack() as ctx:
        def sb(name, shape, dt=F32, on=None):
            return (on or ctx).enter_context(nc.sbuf_tensor(name, shape, dt))

        live = []

        def sem(name):
            live.append(nc.alloc_semaphore(name))
            return live[-1]

        def kept_sem(name):
            return ctx.enter_context(nc.semaphore(name))

        def retire():
            nc.clear_and_free_semaphores(list(live))
            live.clear()
            nc.all_engine_barrier()

        ring = sb("ring", [P, SLOTS, 1024])
        res = sb("res", [P, KT, T])
        hn = sb("hn", [P, KT, T])
        par = sb("par", [P, PARAMS.n])
        tab = sb("tab", [P, TABLES.n])
        sml = sb("sml", [P, SMALL.n])
        mod = sb("mod", [P, 48, 2])
        ab8 = sb("ab8", [8, 2])
        ps = ctx.enter_context(nc.psum_tensor("ps", [P, 8, 512], F32))

        h2_dram = nc.dram_tensor("h2_dram", (T, D), F32).ap()
        y_dram = nc.dram_tensor("y_dram", (MAXTILES * P, D), F32).ap()
        tok_dram = nc.dram_tensor("tok_dram", (MAXTILES * P, 1), F32).ap()
        h_stored = kept_sem("h_stored")

        ident = tab[:, TABLES["ident"]]
        ones = tab[:, TABLES["ones"]]

        def col(name, i=0):
            a = PARAMS.at[name][0] + i
            return par[:, a:a + 1]

        block_in = [kept_sem(f"block_in{s}") for s in range(SLOTS)]
        blocks_done = kept_sem("blocks_done")
        issued = [0]

        def load_blocks(sp, upto_block):
            upto_block = min(upto_block, STREAM.n)

            def one(b, i=None):
                s = b % SLOTS
                back = b - SLOTS + 1
                if i is None:
                    if back > 0:
                        sp.wait_ge(blocks_done, back)
                    src = stream[b]
                else:
                    sp.wait_ge(blocks_done, i * SLOTS + back)
                    src = flat(stream[bass.ds(i * SLOTS + b, 1)].rearrange("a p n -> p a n"))
                sp.dma_start(ring[:, s, :], src).then_inc(block_in[s], 16)

            while issued[0] < SLOTS and issued[0] < upto_block:
                one(issued[0])
                issued[0] += 1
            turns = (upto_block - issued[0]) // SLOTS
            if turns > 1:
                with sp.Fori(0, turns) as i:
                    for j in range(SLOTS):
                        one(issued[0] + j, i)
                issued[0] += turns * SLOTS
            while issued[0] < upto_block:
                one(issued[0])
                issued[0] += 1

        def block_here(pe, b, later=None):
            v = 16 * (b // SLOTS + 1)
            pe.wait_ge(block_in[b % SLOTS], v if later is None else later * 16 + v)
            return ring[:, b % SLOTS, :]

        def dense_tile(pe, w, act, out):
            for k in range(KT):
                m = pe.matmul(out, w[:, k * P:(k + 1) * P], act[:, k, :], start=k == 0, stop=k == KT - 1)
            m.then_inc(blocks_done, 1)

        def credit(pool, sems):
            for pair in sems:
                for s in pair:
                    pool.sem_inc(s, 1)

        def apart(eng):
            eng.wait_ge(small_in, 48)

        small_in = kept_sem("small_in")
        x_in = sem("x_in")
        hctx = sb("hctx", [P, KT, CTX])
        hand = ExitStack()
        cs = sb("cs", [P, 8, 2], on=hand)
        mrow = sb("mrow", [2, D], on=hand)
        cs_ready, par_in = sem("cs_ready"), sem("par_in")
        row_kept, mod_turned, turning = sem("row_kept"), sem("mod_turned"), sem("turning")
        mod_ready = sem("mod_ready")
        with nc.Block() as block:
            @block.scalar
            def _(act):
                act.dma_start(par[:, :], params).then_inc(par_in, 16)
                act.dma_start(sml[:, :], small).then_inc(small_in, 16)
                act.dma_start(tab[:, :], table).then_inc(small_in, 16)
                act.dma_start(ab8[:, :], heads8).then_inc(small_in, 16)
                act.dma_start(res[:, :, :], xT.rearrange("(k p) t -> p k t", p=P)).then_inc(x_in, 16)
                act.dma_start(hctx[:, :, :], ctxT.rearrange("(k p) t -> p k t", p=P)).then_inc(x_in, 16)
                act.wait_ge(par_in, 16)
                act.activation(cs[:, :, :], par[:, PARAMS["cvec"]].rearrange("p (k c) -> p k c", c=2),
                               ACT.Silu).then_inc(cs_ready, 1)

            @block.sync
            def _(sp):
                load_blocks(sp, STREAM["k"].start + SLOTS)

            @block.tensor
            def _(pe):
                pe.wait_ge(cs_ready, 1)
                pe.wait_ge(small_in, 48)
                with pe.Fori(0, 6) as i:
                    for k in range(KT):
                        w = block_here(pe, k, i)
                        for half in range(2):
                            m = pe.matmul(ps[0:2, half, :], cs[:, k, :], w[:, half * 512:(half + 1) * 512],
                                          start=k == 0, stop=k == KT - 1)
                        m.then_inc(blocks_done, 1)
                    pe.wait_ge(row_kept, i + 1)
                    pe.wait_ge(mod_ready, i + 1)
                    pe.sem_inc(turning, 1)
                    for n in range(KT):
                        m = pe.transpose(ps[:, 2, 2 * n:2 * n + 2], mrow[:, n * P:(n + 1) * P], tab[0:2, 0:2])
                    m.then_inc(mod_turned, 1)

            @block.vector
            def _(ve):
                ve.wait_ge(par_in, 16)
                ve.sem_inc(mod_ready, 1)
                with ve.Fori(0, 6) as i:
                    ve.wait_ge(blocks_done, i * SLOTS + SLOTS)
                    ve.tensor_copy(mrow[:, :].rearrange("p (a n) -> p a n", a=2), ps[0:2, 0:2, :]).then_inc(row_kept, 1)
                    ve.wait_ge(mod_turned, i + 1)
                    ve.tensor_tensor(mod[:, bass.ds(i * 8, 8), :],
                                     ps[:, 2, 0:16].rearrange("p (n c) -> p n c", c=2),
                                     par[:, bass.ds(i * 8, 8)].unsqueeze(2).to_broadcast([P, 8, 2]),
                                     ALU.add).then_inc(mod_ready, 1)
        hand.close()

        def norm(name, src, dst, gain, shift=None, n=T, first_wait=None):
            with ExitStack() as st:
                sq = sb(name + "_sq", [P, KT, n], on=st)
                rs = sb(name + "_rs", [P, n], on=st)
                squared, summed, root, scaled = (sem(name + s) for s in ("_squared", "_summed", "_root", "_scaled"))
                with nc.Block() as block:
                    @block.scalar
                    def _(act):
                        if first_wait:
                            act.wait_ge(*first_wait)
                        for k in range(KT):
                            act.activation(sq[:, k, :], src[:, k, :], ACT.Square).then_inc(squared, 1)
                        act.wait_ge(root, 1)
                        act.activation(rs[:, :], rs[:, :], ACT.Sqrt).then_inc(root, 1)
                        if shift is not None:
                            for k in range(KT):
                                act.wait_ge(scaled, k + 1)
                                act.activation(dst[:, k, :], dst[:, k, :], ACT.Identity, bias=shift(k))

                    @block.tensor
                    def _(pe):
                        for k in range(KT):
                            pe.wait_ge(squared, k + 1)
                            m = pe.matmul(ps[:, 0, 0:n], ones, sq[:, k, :], start=k == 0, stop=k == KT - 1)
                        m.then_inc(summed, 1)

                    @block.vector
                    def _(ve):
                        ve.wait_ge(summed, 1)
                        ve.tensor_scalar(rs[:, :], ps[:, 0, 0:n], 1.0 / D, EPS, ALU.mult, ALU.add).then_inc(root, 1)
                        ve.wait_ge(root, 2)
                        ve.reciprocal(rs[:, :], rs[:, :]).then_inc(root, 1)
                        ve.wait_ge(root, 3)
                        ve.wait_ge(squared, KT)
                        for k in range(KT):
                            ve.scalar_tensor_tensor(dst[:, k, :], src[:, k, :], gain(k), rs[:, :],
                                                    ALU.mult, ALU.mult).then_inc(scaled, 1)

        gscale = sb("gscale", [P, 3, KT])
        gready = sem("gready")
        with nc.Block() as block:
            @block.vector
            def _(ve):
                for n, (part, c, g) in enumerate(((8, 0, "norm1"), (8, 1, "norm1"), (32, 0, "norm2"))):
                    ve.scalar_tensor_tensor(gscale[:, n, :], mod[:, part:part + 8, c], 1.0, par[:, PARAMS[g]],
                                            ALU.add, ALU.mult).then_inc(gready, 1)
                ve.wait_ge(x_in, 32)
        norm("n1", res, hn, lambda k: gscale[:, 0, k:k + 1], lambda k: mod[:, k, 0:1])
        norm("n1c", hctx, hctx, lambda k: gscale[:, 1, k:k + 1], lambda k: mod[:, k, 1:2], n=CTX)

        mixed = ctx.enter_context(ExitStack())
        mix = sb("mix", [P, KT, T], on=mixed)
        gla = ctx.enter_context(ExitStack())
        gs = mix[:, 4:8, :]
        kT = sb("kT", [P, 2, TA], on=gla)
        qT = sb("qT", [P, 2, T], on=gla)
        vtok = sb("vtok", [P, 6, 512], on=gla)
        pT = sb("pT", [P, 4, T], on=gla)
        aT = sb("aT", [32, TA], on=gla)
        wd = sb("wd", [32, 512], on=gla)
        wd_zero, wd_in = sem("wd_zero"), sem("wd_in")
        evac_k, evac_v, evac_n, a_sum = sem("evac_k"), sem("evac_v"), sem("evac_n"), sem("a_sum")
        BK, BV, BQ = STREAM["k"].start, STREAM["v"].start, STREAM["q"].start
        with nc.Block() as block:
            @block.sync
            def _(sp):
                load_blocks(sp, STREAM["out"].start + SLOTS)

            @block.gpsimd
            def _(pool):
                pool.memset(wd[:, :], 0.0).then_inc(wd_zero, 1)
                pool.wait_ge(wd_zero, 1)
                pool.dma_start(wd[0:16, 0:256], wdec[0]).then_inc(wd_in, 16)
                pool.dma_start(wd[16:32, 256:512], wdec[1]).then_inc(wd_in, 16)

            @block.tensor
            def _(pe):
                for n in range(2):
                    w = block_here(pe, BK + n)
                    for k in range(KT):
                        pe.matmul(ps[:, 2 * n, :], w[:, k * P:(k + 1) * P], hn[:, k, :], start=k == 0, stop=k == KT - 1)
                    for k in range(KT):
                        m = pe.matmul(ps[:, 2 * n + 1, 0:CTX], w[:, k * P:(k + 1) * P], hctx[:, k, :],
                                      start=k == 0, stop=k == KT - 1)
                    m.then_inc(blocks_done, 1)
                wa = sml[:, SMALL["wa"]].rearrange("p (k n) -> p k n", k=KT)
                for k in range(KT):
                    pe.matmul(ps[0:32, 6, :], wa[:, k, :], hn[:, k, :], start=k == 0, stop=k == KT - 1)
                for k in range(KT):
                    m = pe.matmul(ps[0:32, 7, 0:CTX], wa[:, k, :], hctx[:, k, :], start=k == 0, stop=k == KT - 1)
                m.then_inc(a_sum, 1)
                pe.wait_ge(evac_k, 4)
                for b in range(4):
                    w = block_here(pe, BV + b)
                    for kk in range(2):
                        k = 2 * b + kk
                        for t in range(6):
                            h = hn[:, k, t * P:(t + 1) * P] if t < 4 else hctx[:, k, (t - 4) * P:(t - 3) * P]
                            m = pe.matmul(ps[:, t, :], h, w[:, kk * 512:(kk + 1) * 512], start=k == 0, stop=k == KT - 1)
                    m.then_inc(blocks_done, 1)
                for n in range(10):
                    w = block_here(pe, BQ + n)
                    bank = (6 + n) % 8
                    if n < 2:
                        pe.wait_ge(evac_k, 5 + n)
                    elif n < 8:
                        pe.wait_ge(evac_v, n - 1)
                    else:
                        pe.wait_ge(evac_n, n - 7)
                    dense_tile(pe, w, hn, ps[:, bank, :])

            @block.scalar
            def _(act):
                for n in range(2):
                    act.wait_ge(blocks_done, BK + n + 1)
                    act.activation(kT[:, n, 0:T], ps[:, 2 * n, :], ACT.Copy).then_inc(evac_k, 1)
                    act.activation(kT[:, n, T:TA], ps[:, 2 * n + 1, 0:CTX], ACT.Copy).then_inc(evac_k, 1)
                act.wait_ge(a_sum, 1)
                act.activation(aT[:, 0:T], ps[0:32, 6, :], ACT.Copy).then_inc(evac_k, 1)
                act.activation(aT[:, T:TA], ps[0:32, 7, 0:CTX], ACT.Copy).then_inc(evac_k, 1)
                act.wait_ge(blocks_done, BV + 4)
                for t in range(6):
                    act.activation(vtok[:, t, :], ps[:, t, :], ACT.Copy).then_inc(evac_v, 1)
                for n in range(10):
                    act.wait_ge(blocks_done, BQ + n + 1)
                    out = qT[:, n, :] if n < 2 else gs[:, n - 2, :] if n < 6 else pT[:, n - 6, :]
                    act.activation(out, ps[:, (6 + n) % 8, :], ACT.Silu if 2 <= n < 6 else ACT.Copy,
                                   scale=0.125 if n < 2 else 1.0).then_inc(evac_n, 1)

        st = gla.enter_context(ExitStack())
        qbm = hn[:, :, :].rearrange("p (a b) t -> p a b t", b=2)
        kb = hctx[:, :, :].rearrange("p (a b) t -> p a (b t)", b=2)
        tot = sb("tot", [P, 4, 12], on=gla)
        SS = sb("SS", [P, 4, 12, P], on=gla)
        kstT = sb("kstT", [P, 2, 4, 2, P], on=gla)
        kst = sb("kst", [P, 4, TA], on=st)
        cum = sb("cum", [P, TA], on=st)
        la = sb("la", [P, TA], on=st)
        lg = sb("lg", [P, TA], on=st)
        bb = sb("bb", [P, TA], on=st)
        dl = mix[:, 2:4, :].rearrange("p a t -> p (a t)")[:, 0:TA]
        e1, e2 = mix[:, 0, :], mix[:, 1, :]
        y_cleared = sem("y_cleared")
        z_sum, z_log, z_dve, z_exp, z_zero = sem("z_sum"), sem("z_log"), sem("z_dve"), sem("z_exp"), sem("z_zero")
        with nc.Block() as block:
            @block.gpsimd
            def _(pool):
                pool.memset(qbm[:, :, :, :], 0.0).then_inc(z_zero, 1)
                pool.memset(kstT[:, :, :, :, :], 0.0).then_inc(z_zero, 1)
                pool.wait_ge(z_zero, 2)
                zeros = kstT[:, 0, :, :, :].rearrange("p a b c -> p (a b c)")
                pool.dma_start(y_dram[MINTILES * P:, :].rearrange("(n p) d -> p n d", p=P),
                               zeros.unsqueeze(1).to_broadcast([P, MAXTILES - MINTILES, D])).then_inc(y_cleared, 16)
                pool.memset(SS[:, :, 0, :], 0.0).then_inc(z_zero, 1)
                pool.wait_ge(y_cleared, 16)

            @block.tensor
            def _(pe):
                pe.wait_ge(wd_in, 32)
                for dp in range(4):
                    pe.matmul(ps[:, 2 * dp, :], wd[:, dp * P:(dp + 1) * P], aT[:, 0:T], start=True, stop=True)
                    pe.matmul(ps[:, 2 * dp + 1, 0:CTX], wd[:, dp * P:(dp + 1) * P], aT[:, T:TA],
                              start=True, stop=True).then_inc(z_sum, 1)

            @block.scalar
            def _(act):
                n = [0]

                def step(ins):
                    n[0] += 1
                    ins.then_inc(z_log, 1)
                    act.wait_ge(z_log, n[0])
                for dp in range(4):
                    bias = col("bdec", dp)
                    act.wait_ge(z_dve, 11 * dp + 2)
                    act.activation(lg[:, 0:T], ps[:, 2 * dp, :], ACT.Abs, bias=bias).then_inc(z_log, 1)
                    n[0] += 1
                    step(act.activation(lg[:, T:TA], ps[:, 2 * dp + 1, 0:CTX], ACT.Abs, bias=bias))
                    step(act.activation(lg[:, :], lg[:, :], ACT.Exp, scale=-1.0))
                    step(act.activation(lg[:, :], lg[:, :], ACT.Ln, bias=1.0))
                    act.wait_ge(z_dve, 11 * dp + 7)
                    act.activation(e1, bb[:, 0:T], ACT.Exp, scale=1.0 / 16).then_inc(z_exp, 1)
                    act.activation(e2, bb[:, 0:T], ACT.Exp, scale=-1.0 / 16).then_inc(z_exp, 1)
                    act.activation(lg[:, :], dl, ACT.Exp, scale=1.0 / 16).then_inc(z_exp, 1)
                    act.activation(tot[:, dp, :], tot[:, dp, :], ACT.Exp, scale=1.0 / 16).then_inc(z_exp, 1)

            @block.vector
            def _(ve):
                n = [0]

                def step(ins):
                    n[0] += 1
                    ins.then_inc(z_dve, 1)
                    ve.wait_ge(z_dve, n[0])
                ve.wait_ge(z_zero, 3)
                for dp in range(4):
                    pair, back = dp % 2, dp // 2
                    bias = col("bdec", dp)
                    ve.wait_ge(z_sum, dp + 1)
                    step(ve.tensor_scalar(la[:, 0:T], ps[:, 2 * dp, :], bias, 0.0, ALU.add, ALU.min))
                    step(ve.tensor_scalar(la[:, T:TA], ps[:, 2 * dp + 1, 0:CTX], bias, 0.0, ALU.add, ALU.min))
                    ve.wait_ge(z_log, 4 * dp + 4)
                    step(ve.tensor_tensor(la[:, :], la[:, :], lg[:, :], ALU.subtract))
                    step(ve.tensor_tensor_scan(cum[:, :], tab[:, TABLES["resetg"]], la[:, :], 0.0, ALU.mult, ALU.add))
                    chunks = [x.rearrange("p (c j) -> p c j", j=64) for x in (cum[:, :], bb[:, :], dl)]
                    t3 = tot[:, dp, :].unsqueeze(2).to_broadcast([P, 12, 64])
                    step(ve.tensor_copy(tot[:, dp, :].unsqueeze(2), chunks[0][:, :, 63:64]))
                    if back:
                        step(ve.tensor_tensor(dl, cum[:, :], la[:, :], ALU.subtract))
                        step(ve.tensor_tensor(chunks[1], t3, chunks[2], ALU.subtract))
                    else:
                        step(ve.tensor_copy(bb[:, :], cum[:, :]))
                        step(ve.tensor_tensor(chunks[2], t3, chunks[1], ALU.subtract))
                    ve.wait_ge(z_exp, 4 * dp + 4)
                    for h in range(2):
                        r = slice(64 * h, 64 * h + 64)
                        step(ve.tensor_tensor(qbm[r, dp, h, :], qT[r, pair, :], e1[r, :], ALU.mult))
                    step(ve.tensor_tensor(kb[:, dp, :], kT[:, pair, 0:T], e2, ALU.mult))
                    step(ve.tensor_tensor(kst[:, dp, :], kT[:, pair, :], lg[:, :], ALU.mult))

        def chunk_of(d, s):
            return (8 + s if s < 4 else s - 4) if d == 0 else (11 - s if s < 4 else 11 - s)
        tr_done, tr_copied, ds_done, ds_used = sem("tr_done"), sem("tr_copied"), sem("ds_done"), sem("ds_used")
        STEPS = 11
        with nc.Block() as block:
            @block.tensor
            def _(pe):
                for s in range(STEPS):
                    u = s % 2
                    if s >= 2:
                        pe.wait_ge(tr_copied, 2 * (s - 1))
                    for dp in range(4):
                        c = chunk_of(dp // 2, s)
                        tile = c // 2
                        m = pe.transpose(ps[:, u, dp * P:(dp + 1) * P], kst[:, dp, tile * P:(tile + 1) * P], ident)
                    m.then_inc(tr_done, 1)
                    pe.wait_ge(tr_copied, 2 * (s + 1))
                    for pair in range(2):
                        if s >= 2:
                            pe.wait_ge(ds_used, 8 * (s - 2) + 4 * pair + 4)
                        for d in range(2):
                            c = chunk_of(d, s)
                            m = pe.matmul(ps[:, 2 + u + 2 * pair, d * 256:d * 256 + 256],
                                          kstT[:, u, 2 * d + pair, c % 2, :],
                                          vtok[:, c // 2, pair * 256:pair * 256 + 256], start=True, stop=True)
                        m.then_inc(ds_done, 1)

            @block.scalar
            def _(act):
                for s in range(STEPS):
                    act.wait_ge(tr_done, s + 1)
                    if s >= 2:
                        act.wait_ge(ds_done, 2 * (s - 1))
                    for d in range(2):
                        half = chunk_of(d, s) % 2
                        r = slice(64 * half, 64 * half + 64)
                        act.activation(kstT[r, s % 2, 2 * d:2 * d + 2, half, :],
                                       ps[r, s % 2, 256 * d:256 * d + 256].rearrange("p (a n) -> p a n", a=2),
                                       ACT.Copy).then_inc(tr_copied, 1)

            @block.vector
            def _(ve):
                for s in range(STEPS):
                    for pair in range(2):
                        ve.wait_ge(ds_done, 2 * s + pair + 1)
                        if s:
                            ve.wait_ge(ds_used, 8 * (s - 1) + 4 * pair + 4)
                        for d in range(2):
                            dp = 2 * d + pair
                            c = chunk_of(d, s)
                            for h in range(2):
                                r = slice(64 * h, 64 * h + 64)
                                o = d * 256 + h * P
                                ve.scalar_tensor_tensor(SS[r, dp, s + 1, :], SS[r, dp, s, :], tot[r, dp, c:c + 1],
                                                        ps[r, 2 + s % 2 + 2 * pair, o:o + P],
                                                        ALU.mult, ALU.add).then_inc(ds_used, 1)
        st.close()

        sc = sb("sc", [P, 2, 2, 512], on=gla)
        masks = sb("masks", [P, 2, P], U8, on=gla)
        oT = sb("oT", [P, 4, T], on=gla)
        sc_zero, sc_done, sc_kept, o_done, o_kept = (sem(n) for n in ("sc_zero", "sc_done", "sc_kept", "o_done", "o_kept"))
        with nc.Block() as block:
            @block.gpsimd
            def _(pool):
                pool.memset(sc[:, :, :, :], 0.0).then_inc(sc_zero, 1)

            @block.tensor
            def _(pe):
                for t in range(TT):
                    cols = slice(t * P, (t + 1) * P)
                    for d in range(2):
                        if t >= 2:
                            pe.wait_ge(sc_kept, 2 * (t - 2) + d + 1)
                        for h in range(4):
                            dp = 2 * d + h // 2
                            m = pe.matmul(ps[:, 2 * (t % 2) + d, h * P:(h + 1) * P], kb[:, dp, cols],
                                          qbm[:, dp, h % 2, cols], start=True, stop=True)
                        m.then_inc(sc_done, 1)
                    pe.wait_ge(sc_kept, 2 * t + 2)
                    if t >= 2:
                        pe.wait_ge(o_kept, t - 1)
                    for h in range(4):
                        out = ps[:, 4 + t % 2, h * P:(h + 1) * P]
                        pe.matmul(out, vtok[:, t, h * P:(h + 1) * P], sc[:, t % 2, 0, h * P:(h + 1) * P],
                                  start=True, stop=False)
                        for d in range(2):
                            dp = 2 * d + h // 2
                            for cc in range(2):
                                c = 2 * t + cc
                                s = 4 + c if d == 0 else 11 - c
                                pe.matmul(out[:, 64 * cc:64 * cc + 64], SS[:, dp, s, :],
                                          qbm[:, dp, h % 2, c * 64:(c + 1) * 64], start=False, stop=False,
                                          skip_group_check=True)
                        m = pe.matmul(out, vtok[:, t, h * P:(h + 1) * P], sc[:, t % 2, 1, h * P:(h + 1) * P],
                                      start=False, stop=True)
                    m.then_inc(o_done, 1)

            @block.vector
            def _(ve):
                ve.tensor_copy(masks[:, 0, :], tab[:, TABLES["glaf"]]).then_inc(sc_zero, 1)
                ve.tensor_copy(masks[:, 1, :], tab[:, TABLES["glab"]]).then_inc(sc_zero, 1)
                ve.wait_ge(sc_zero, 3)
                for t in range(TT):
                    if t >= 2:
                        ve.wait_ge(o_done, t - 1)
                    for d in range(2):
                        ve.wait_ge(sc_done, 2 * t + d + 1)
                        ve.copy_predicated(sc[:, t % 2, d, :].rearrange("p (h i) -> p h i", h=4),
                                           masks[:, d, :].unsqueeze(1).to_broadcast([P, 4, P]),
                                           ps[:, 2 * (t % 2) + d, :].rearrange("p (h i) -> p h i", h=4)
                                           ).then_inc(sc_kept, 1)

            @block.scalar
            def _(act):
                for t in range(TT):
                    act.wait_ge(o_done, t + 1)
                    act.activation(oT[:, :, t * P:(t + 1) * P],
                                   ps[:, 4 + t % 2, :].rearrange("p (h i) -> p h i", h=4), ACT.Copy).then_inc(o_kept, 1)

        sq, rs = hn[:, 0:4, :], hn[:, 4:8, :]
        grid = (ROWS + 16) * (GRID_W + 16)
        spare = SS[:, :, :, :].rearrange("p a b c -> p (a b c)")
        bufs = [spare[:, n * grid:(n + 1) * grid].rearrange("p (r c) -> p r c", c=GRID_W + 16) for n in range(3)]
        o_ms, o_pow = sem("o_ms"), sem("o_pow")
        o_sq, o_sum, o_root, o_mix = sem("o_sq"), sem("o_sum"), sem("o_root"), sem("o_mix")
        pool_step, pooled, pool_mm, pool_out = sem("pool_step"), sem("pooled"), sem("pool_mm"), sem("pool_out")
        with nc.Block() as block:
            @block.scalar
            def _(act):
                for h in range(4):
                    act.activation(sq[:, h, :], oT[:, h, :], ACT.Square).then_inc(o_sq, 1)
                for h in range(4):
                    act.wait_ge(o_ms, h + 1)
                    act.activation(rs[:, h, :], rs[:, h, :], ACT.Sqrt).then_inc(o_pow, 1)

            @block.tensor
            def _(pe):
                for h in range(4):
                    pe.wait_ge(o_sq, h + 1)
                    pe.matmul(ps[:, h, :], ones, sq[:, h, :], start=True, stop=True).then_inc(o_sum, 1)
                wp = sml[:, SMALL["pool"]].rearrange("p (g n) -> p g n", g=4)
                for g in range(4):
                    pe.wait_ge(pooled, g + 1)
                    pe.matmul(ps[:, 4 + g, :], wp[:, g, :], pT[:, g, :], start=True, stop=True).then_inc(pool_mm, 1)

            @block.gpsimd
            def _(pool):
                n = [0]

                def step(ins):
                    n[0] += 1
                    ins.then_inc(pool_step, 1)
                    pool.wait_ge(pool_step, n[0])
                for g, w in enumerate(WINDOWS):
                    lo = w // 2
                    a, b, c = bufs
                    if g:
                        pool.wait_ge(pooled, g)
                    pool.memset(a[:, :, :], 0.0).then_inc(pool_step, 1)
                    pool.memset(b[:, :, :], 0.0).then_inc(pool_step, 1)
                    n[0] += 2
                    pool.wait_ge(pool_step, n[0])
                    step(pool.tensor_copy(a[:, lo:lo + ROWS, lo:lo + GRID_W],
                                          pT[:, g, :].rearrange("p (r c) -> p r c", c=GRID_W)))
                    s = 1
                    width = GRID_W + 16
                    while s < w:
                        step(pool.tensor_tensor(b[:, 0:ROWS + 16, 0:width - s], a[:, 0:ROWS + 16, 0:width - s],
                                                a[:, 0:ROWS + 16, s:width], ALU.add))
                        a, b = b, a
                        s *= 2
                    s = 1
                    rows = ROWS + 16
                    while s < w:
                        step(pool.tensor_tensor(b[:, 0:rows - s, 0:GRID_W], a[:, 0:rows - s, 0:GRID_W],
                                                a[:, s:rows, 0:GRID_W], ALU.add))
                        a, b = b, a
                        s *= 2
                    rc = tab[:, TABLES["rcount"]].rearrange("p (g r c) -> p g r c", g=4, c=GRID_W)[:, g]
                    step(pool.tensor_tensor(c[:, 0:ROWS, 0:GRID_W], a[:, 0:ROWS, 0:GRID_W], rc, ALU.mult))
                    p3 = pT[:, g, :].rearrange("p (r c) -> p r c", c=GRID_W)
                    pool.tensor_tensor(p3, c[:, 0:ROWS, 0:GRID_W], p3, ALU.subtract).then_inc(pooled, 1)
                pool.wait_ge(pooled, 4)

            @block.vector
            def _(ve):
                n = [0]

                def step(ins):
                    n[0] += 1
                    ins.then_inc(o_root, 1)
                    ve.wait_ge(o_root, n[0])
                for h in range(4):
                    ve.wait_ge(o_sum, h + 1)
                    ve.tensor_scalar(rs[:, h, :], ps[:, h, :], 1.0 / P, EPS, ALU.mult, ALU.add).then_inc(o_ms, 1)
                for h in range(4):
                    ve.wait_ge(o_pow, h + 1)
                    step(ve.reciprocal(rs[:, h, :], rs[:, h, :]))
                    step(ve.scalar_tensor_tensor(rs[:, h, :], oT[:, h, :], col("gla"), rs[:, h, :], ALU.mult, ALU.mult))
                    ve.tensor_tensor(mix[:, h, :], rs[:, h, :], gs[:, h, :], ALU.mult).then_inc(o_mix, 1)
                ve.wait_ge(o_mix, 4)
                for g in range(4):
                    ve.wait_ge(pool_mm, g + 1)
                    ve.tensor_scalar(mix[:, 4 + g, :], ps[:, 4 + g, :], col("pscale", g), None, ALU.mult).then_inc(pool_out, 1)
        gla.close()

        def project_out(name, act_in, first_block, gate, next_block):
            added = sem(name + "_added")
            with nc.Block() as block:
                @block.sync
                def _(sp):
                    load_blocks(sp, next_block)

                @block.tensor
                def _(pe):
                    for n in range(KT):
                        dense_tile(pe, block_here(pe, first_block + n), act_in, ps[:, n, :])

                @block.vector
                def _(ve):
                    for n in range(KT):
                        ve.wait_ge(blocks_done, first_block + n + 1)
                        if gate is None:
                            ve.tensor_tensor(res[:, n, :], ps[:, n, :], res[:, n, :], ALU.add).then_inc(added, 1)
                        else:
                            ve.scalar_tensor_tensor(res[:, n, :], ps[:, n, :], gate(n), res[:, n, :],
                                                    ALU.mult, ALU.add).then_inc(added, 1)

        project_out("mixout", mix, STREAM["out"].start, lambda n: mod[:, 16 + n, 0:1], STREAM["gdn"].start + SLOTS)
        norm("n2", res, hn, lambda k: gscale[:, 2, k:k + 1], lambda k: mod[:, 24 + k, 0:1])

        retire()
        moe = ctx.enter_context(ExitStack())
        htok = mix[:, :, :].rearrange("p (t h) n -> p t (h n)", h=2)
        h_tr, h_kept = sem("h_tr"), [sem("h_kept_act"), sem("h_kept_dve")]
        with nc.Block() as block:
            @block.tensor
            def _(pe):
                for n in range(8):
                    t, half = n // 2, n % 2
                    for k in range(4):
                        m = pe.transpose(ps[:, n, k * P:(k + 1) * P], hn[:, 4 * half + k, t * P:(t + 1) * P], ident)
                    m.then_inc(h_tr, 1)

            @block.scalar
            def _(act):
                for n in range(0, 8, 2):
                    act.wait_ge(h_tr, n + 1)
                    act.activation(mix[:, n, :], ps[:, n, :], ACT.Copy).then_inc(h_kept[0], 1)

            @block.vector
            def _(ve):
                for n in range(1, 8, 2):
                    ve.wait_ge(h_tr, n + 1)
                    ve.tensor_copy(mix[:, n, :], ps[:, n, :]).then_inc(h_kept[1], 1)

            @block.sync
            def _(sp):
                for t in range(TT):
                    sp.wait_ge(h_kept[0], t + 1)
                    sp.wait_ge(h_kept[1], t + 1)
                    sp.dma_start(h2_dram[t * P:(t + 1) * P, :], htok[:, t, :]).then_inc(h_stored, 16)

        I32 = mybir.dt.int32
        w_up, w_down = sb("w_up", [P, 2, KT * 512], on=moe), sb("w_down", [P, 2, 2 * D], on=moe)
        lgt = sb("lgt", [P, TT, 36], on=moe)
        gt_ = sb("gt_", [P, 8, TT, 8], on=moe)
        prod = sb("prod", [P, 3, TT, 4, 8], on=moe)
        one = sb("one", [P, 8, TT, 1], on=moe)
        ex_ = sb("ex_", [P, 4, NEXP], on=moe)
        cmp_ = sb("cmp_", [1, MAXTILES, NEXP], on=moe)
        meta_f = sb("meta_f", [1, MAXTILES + 1], on=moe)
        meta = sb("meta", [1, MAXTILES + 1], I32, on=moe)
        slot_f = sb("slot_f", [P, 2, TT, 1], on=moe)
        slot_i = sb("slot_i", [P, 2, TT], I32, on=moe)
        tok_f = sb("tok_f", [MAXTILES, P], on=moe)
        tok_i = sb("tok_i", [P, MAXTILES], I32, on=moe)
        logits_done, r_step, r_exp, ranked = sem("logits_done"), sem("r_step"), sem("r_exp"), sem("ranked")
        slots_ready, tok_zero, tok_filled, tok_sent, tok_back, tok_tr, tok_ready = (
            sem(n) for n in ("slots_ready", "tok_zero", "tok_filled", "tok_sent", "tok_back", "tok_tr", "tok_ready"))
        onehot_ready = sem("onehot_ready")
        with nc.Block() as block:
            @block.tensor
            def _(pe):
                wr = sml[:, SMALL["router"]].rearrange("p (k n) -> p k n", k=KT)
                for t in range(TT):
                    for k in range(KT):
                        m = pe.matmul(ps[:, 0, t * 36:(t + 1) * 36], hn[:, k, t * P:(t + 1) * P], wr[:, k, :],
                                      start=k == 0, stop=k == KT - 1)
                m.then_inc(logits_done, 1)
                pe.wait_ge(onehot_ready, 1)
                chosen = prod[:, 2].rearrange("p t g e -> p t (g e)")
                for t in range(TT):
                    for b in range(t + 1):
                        pe.matmul(ps[:, 1, t * NEXP:(t + 1) * NEXP], tab[:, TABLES["strict"]] if b == t else ones,
                                  chosen[:, b, :], start=b == 0, stop=b == t)
                for t in range(TT):
                    m = pe.matmul(ps[:, 2, 0:NEXP], ones, chosen[:, t, :], start=t == 0, stop=t == TT - 1)
                m.then_inc(ranked, 1)
                pe.wait_ge(tok_back, 16)
                pe.transpose(ps[:, 3, 0:MAXTILES], tok_f[:, :], tab[0:MAXTILES, 0:MAXTILES]).then_inc(tok_tr, 1)

            @block.scalar
            def _(act):
                act.wait_ge(r_step, 3)
                act.activation(gt_[:, 1, :, 0:4], gt_[:, 0, :, 0:4], ACT.Exp).then_inc(r_exp, 1)
                act.wait_ge(r_step, 20)
                act.activation(one[:, 5], one[:, 4], ACT.Exp).then_inc(r_exp, 1)

            @block.gpsimd
            def _(pool):
                pool.memset(tok_f[:, :], 0.0).then_inc(tok_zero, 1)
                pool.wait_ge(tok_zero, 1)
                pool.dma_start(tok_dram.rearrange("(n p) a -> n (p a)", p=P), tok_f[:, :]).then_inc(tok_filled, 16)
                pool.wait_ge(tok_filled, 16)
                pool.wait_ge(slots_ready, 1)
                for n in range(2):
                    for t in range(TT):
                        pool.indirect_dma_start(
                            out=tok_dram, out_offset=bass.IndirectOffsetOnAxis(ap=slot_i[:, n, t:t + 1], axis=0),
                            in_=tab[:, TABLES.at["token"][0] + t:TABLES.at["token"][0] + t + 1], in_offset=None
                        ).then_inc(tok_sent, 16)
                pool.wait_ge(tok_sent, 2 * TT * 16)
                pool.dma_start(tok_f[:, :], tok_dram.rearrange("(n p) a -> n (p a)", p=P)).then_inc(tok_back, 16)

            @block.vector
            def _(ve):
                n = [0]

                def step(ins):
                    n[0] += 1
                    ins.then_inc(r_step, 1)
                    ve.wait_ge(r_step, n[0])

                def wide(x, width):
                    return x.to_broadcast([P, TT, width])
                rank = tab[:, TABLES["rank"]].unsqueeze(1)

                def first_of(eq, width, top, hot):
                    step(ve.tensor_tensor(hot, eq, rank[:, :, 0:width].to_broadcast([P, TT, width]), ALU.mult))
                    step(ve.tensor_reduce(top, hot, AX.X, ALU.max))
                    step(ve.tensor_tensor(hot, hot, wide(top, width), ALU.is_equal))
                ve.wait_ge(logits_done, 1)
                step(ve.tensor_copy(lgt[:, :, :], ps[:, 0, 0:144].rearrange("p (t n) -> p t n", t=TT)))
                group = lgt[:, :, 0:4]
                step(ve.tensor_reduce(one[:, 0], group, AX.X, ALU.max))
                step(ve.tensor_tensor(gt_[:, 0, :, 0:4], group, wide(one[:, 0], 4), ALU.subtract))
                ve.wait_ge(r_exp, 1)
                step(ve.tensor_reduce(one[:, 1], gt_[:, 1, :, 0:4], AX.X, ALU.add))
                step(ve.reciprocal(one[:, 1], one[:, 1]))
                step(ve.tensor_tensor(gt_[:, 2, :, 0:4], group, wide(one[:, 0], 4), ALU.is_equal))
                first_of(gt_[:, 2, :, 0:4], 4, one[:, 2], gt_[:, 3, :, 0:4])
                hot_g = gt_[:, 3, :, 0:4].unsqueeze(3).to_broadcast([P, TT, 4, 8])
                step(ve.tensor_tensor(prod[:, 0], lgt[:, :, 4:36].rearrange("p t (g e) -> p t g e", g=4),
                                      hot_g, ALU.mult))
                le, eq, h1, h2, rest = (gt_[:, n, :, :] for n in (4, 5, 6, 7, 0))
                step(ve.tensor_reduce(le.unsqueeze(3), prod[:, 0].rearrange("p t g e -> p t e g"), AX.X, ALU.add))
                step(ve.tensor_reduce(one[:, 2], le, AX.X, ALU.max))
                step(ve.tensor_tensor(eq, le, wide(one[:, 2], 8), ALU.is_equal))
                first_of(eq, 8, one[:, 3], h1)
                step(ve.scalar_tensor_tensor(rest, h1, MASKED_LOW, le, ALU.mult, ALU.add))
                step(ve.tensor_reduce(one[:, 3], rest, AX.X, ALU.max))
                step(ve.tensor_tensor(eq, rest, wide(one[:, 3], 8), ALU.is_equal))
                step(ve.tensor_tensor(one[:, 4], one[:, 3], one[:, 2], ALU.subtract))
                first_of(eq, 8, one[:, 7], h2)
                step(ve.tensor_tensor(prod[:, 0], hot_g, h1.unsqueeze(2).to_broadcast([P, TT, 4, 8]), ALU.mult))
                step(ve.tensor_tensor(prod[:, 1], hot_g, h2.unsqueeze(2).to_broadcast([P, TT, 4, 8]), ALU.mult))
                ve.tensor_tensor(prod[:, 2], prod[:, 0], prod[:, 1], ALU.add).then_inc(onehot_ready, 1)
                step(ve.memset(one[:, 6], 1.0))
                ve.wait_ge(r_exp, 2)
                step(ve.tensor_tensor(one[:, 6], one[:, 5], one[:, 6], ALU.add))
                step(ve.reciprocal(one[:, 6], one[:, 6]))
                step(ve.tensor_tensor(one[:, 6], one[:, 6], one[:, 1], ALU.mult))
                step(ve.tensor_tensor(one[:, 5], one[:, 5], one[:, 6], ALU.mult))
                ve.wait_ge(ranked, 1)
                count, ntile, upto_, first = (ex_[:, n, :] for n in range(4))
                step(ve.tensor_copy(count, ps[:, 2, 0:NEXP]))
                step(ve.tensor_scalar(ntile, count, 0.5, None, ALU.is_gt))
                for m in range(1, TT):
                    step(ve.scalar_tensor_tensor(ntile, count, m * P + 0.5, ntile, ALU.is_gt, ALU.add))
                step(ve.tensor_tensor_scan(upto_, ones[:, 0:NEXP], ntile, 0.0, ALU.mult, ALU.add))
                step(ve.tensor_tensor(first, upto_, ntile, ALU.subtract))
                step(ve.tensor_scalar(first, first, float(P), None, ALU.mult))
                slot = gt_[:, 0:4].rearrange("p a t e -> p (a t e)").rearrange("p (t e) -> p t e", t=TT)
                step(ve.tensor_tensor(slot, ps[:, 1, 0:TT * NEXP].rearrange("p (t e) -> p t e", t=TT),
                                      first.unsqueeze(1).to_broadcast([P, TT, NEXP]), ALU.add))
                for a in range(2):
                    picked = prod[:, a].rearrange("p t g e -> p t (g e)")
                    step(ve.tensor_tensor(picked, picked, slot, ALU.mult))
                    step(ve.tensor_reduce(slot_f[:, a], picked, AX.X, ALU.add))
                ve.tensor_copy(slot_i[:, :, :], slot_f[:, :, :, :].rearrange("p a t o -> p a (t o)")).then_inc(slots_ready, 1)
                number = tab[0:1, TABLES["tile"]]
                step(ve.tensor_tensor(cmp_[:, :, :], number.unsqueeze(2).to_broadcast([1, MAXTILES, NEXP]),
                                      ex_[0:1, 2, :].unsqueeze(1).to_broadcast([1, MAXTILES, NEXP]), ALU.is_ge))
                step(ve.tensor_reduce(meta_f[:, 0:MAXTILES].unsqueeze(2), cmp_[:, :, :], AX.X, ALU.add))
                step(ve.tensor_scalar(meta_f[:, 0:MAXTILES], meta_f[:, 0:MAXTILES], NEXP - 1.0, None, ALU.min))
                even = number.rearrange("p (a b) -> p a b", b=2)[:, :, 0]
                step(ve.tensor_scalar(cmp_[:, 0, 0:MAXTILES // 2], even, ex_[0:1, 2, NEXP - 1:NEXP], None, ALU.is_lt))
                step(ve.tensor_reduce(meta_f[:, MAXTILES:], cmp_[:, 0, 0:MAXTILES // 2], AX.X, ALU.add))
                step(ve.tensor_copy(meta[:, :], meta_f[:, :]))
                ve.wait_ge(tok_tr, 1)
                ve.tensor_copy(tok_i[:, :], ps[:, 3, 0:MAXTILES]).then_inc(tok_ready, 1)
                ve.wait_ge(tok_ready, 1)

        hg = sb("hg", [P, 2, D], on=moe)
        hgT = sb("hgT", [P, 2, KT, P], on=moe)
        sg = sb("sg", [P, 2, 256], on=moe)
        hid = sb("hid", [P, 2, 256], on=moe)
        hidT = sb("hidT", [P, 2, 2, P], on=moe)
        ytile = sb("ytile", [P, 2, D], on=moe)
        idx = sb("idx", [P, 2, 1], I32, on=moe)
        names = ("up_in", "down_in", "idx_set", "gathered", "turned", "copied_a", "copied_b", "up_done", "gate", "hid_done", "hid_tr",
                 "hid_copied", "down_done", "y_a", "y_b", "y_stored")
        M = {n: [sem(f"m_{n}{u}") for u in range(2)] for n in names}
        gathering = sem("gathering")
        dma_names = ("up_in", "down_in", "gathered", "y_stored")
        with nc.Block() as block:
            def pairs(eng):
                return eng.value_load(meta[0:1, MAXTILES:MAXTILES + 1], min_val=1, max_val=MAXTILES // 2)

            @block.sync
            def _(sp):
                with sp.Fori(0, pairs(sp)) as i:
                    tile = [flat(experts[bass.ds(sp.value_load(meta[0:1, bass.ds(i * 2 + u, 1)], min_val=0,
                                                               max_val=NEXP - 1), 1)].rearrange("a p n -> p a n"))
                            for u in range(2)]
                    for u in range(2):
                        sp.wait_ge(M["up_done"][u], i + 1)
                        sp.dma_start(w_up[:, u, :], tile[u][:, 0:KT * 512]).then_inc(M["up_in"][u], 16)
                    for u in range(2):
                        sp.wait_ge(M["down_done"][u], i + 1)
                        sp.dma_start(w_down[:, u, :], tile[u][:, KT * 512:]).then_inc(M["down_in"][u], 16)

            @block.gpsimd
            def _(pool):
                credit(pool, [v for n, v in M.items() if n not in dma_names])
                pool.wait_ge(h_stored, TT * 16)
                turns = pairs(pool)
                with pool.Fori(0, turns) as i:
                    for u in range(2):
                        pool.wait_ge(M["turned"][u], i + 1)
                        apart(pool)
                        pool.tensor_copy(idx[:, u, :], tok_i[:, bass.ds(i * 2 + u, 1)]).then_inc(M["idx_set"][u], 1)
                        pool.wait_ge(M["idx_set"][u], i + 2)
                        pool.sem_inc(gathering, 1)
                        pool.indirect_dma_start(
                            out=hg[:, u, :], out_offset=None, in_=h2_dram,
                            in_offset=bass.IndirectOffsetOnAxis(ap=idx[:, u, :], axis=0)).then_inc(M["gathered"][u], 16)
                for u in range(2):
                    pool.wait_ge(M["y_stored"][u], turns * 16 + 1)

            @block.tensor
            def _(pe):
                with pe.Fori(0, pairs(pe)) as i:
                    for u in range(2):
                        pe.wait_ge(M["gathered"][u], i * 16 + 16)
                        pe.wait_ge(M["y_a"][u], i + 1)
                        pe.wait_ge(M["y_b"][u], i + 1)
                        for k in range(KT):
                            m = pe.transpose(ps[:, 2 * u + k // 4, (k % 4) * P:(k % 4 + 1) * P],
                                             hg[:, u, k * P:(k + 1) * P], ident)
                        m.then_inc(M["turned"][u], 1)
                    for u in range(2):
                        pe.wait_ge(M["up_in"][u], i * 16 + 16)
                        pe.wait_ge(M["copied_a"][u], i + 2)
                        pe.wait_ge(M["copied_b"][u], i + 2)
                        pe.wait_ge(M["hid_done"][u], i + 1)
                        for k in range(KT):
                            m = pe.matmul(ps[:, 4 + u, :], hgT[:, u, k, :], w_up[:, u, k * 512:(k + 1) * 512],
                                          start=k == 0, stop=k == KT - 1)
                        m.then_inc(M["up_done"][u], 1)

                    def turn_hidden(u):
                        pe.wait_ge(M["hid_done"][u], i + 2)
                        pe.wait_ge(M["hid_copied"][u], i + 1)
                        for f in range(2):
                            m = pe.transpose(ps[:, 6 + u, f * P:(f + 1) * P], hid[:, u, f * P:(f + 1) * P], ident)
                        m.then_inc(M["hid_tr"][u], 1)

                    def down(u, half):
                        for f in range(2):
                            o = f * D + half * 512
                            m = pe.matmul(ps[:, 2 * u + half, :], hidT[:, u, f, :], w_down[:, u, o:o + 512],
                                          start=f == 0, stop=f == 1)
                        return m
                    turn_hidden(0)
                    pe.wait_ge(M["down_in"][0], i * 16 + 16)
                    pe.wait_ge(M["hid_copied"][0], i + 2)
                    down(0, 0)
                    turn_hidden(1)
                    down(0, 1).then_inc(M["down_done"][0], 1)
                    pe.wait_ge(M["down_in"][1], i * 16 + 16)
                    pe.wait_ge(M["hid_copied"][1], i + 2)
                    down(1, 0)
                    down(1, 1).then_inc(M["down_done"][1], 1)

            @block.scalar
            def _(act):
                with act.Fori(0, pairs(act)) as i:
                    for u in range(2):
                        act.wait_ge(M["turned"][u], i + 2)
                        act.activation(hgT[:, u, 0:4, :].rearrange("p k n -> p (k n)"), ps[:, 2 * u, :], ACT.Copy
                                       ).then_inc(M["copied_a"][u], 1)
                    for u in range(2):
                        act.wait_ge(M["up_done"][u], i + 2)
                        act.activation(sg[:, u, :], ps[:, 4 + u, 0:256], ACT.Silu).then_inc(M["gate"][u], 1)
                    for u in range(2):
                        act.wait_ge(M["down_done"][u], i + 2)
                        act.wait_ge(M["y_stored"][u], i * 16 + 1)
                        act.activation(ytile[:, u, 0:512], ps[:, 2 * u, :], ACT.Copy).then_inc(M["y_a"][u], 1)
                        act.wait_ge(M["y_a"][u], i + 2)
                        act.wait_ge(M["y_b"][u], i + 2)
                        act.dma_start(y_dram[bass.ds((i * 2 + u) * P, P), :], ytile[:, u, :]
                                      ).then_inc(M["y_stored"][u], 16)

            @block.vector
            def _(ve):
                for u in range(2):
                    ve.sem_inc(M["y_stored"][u], 1)
                with ve.Fori(0, pairs(ve)) as i:
                    for u in range(2):
                        ve.wait_ge(M["turned"][u], i + 2)
                        ve.tensor_copy(hgT[:, u, 4:8, :].rearrange("p k n -> p (k n)"), ps[:, 2 * u + 1, :]
                                       ).then_inc(M["copied_b"][u], 1)
                    for u in range(2):
                        ve.wait_ge(M["gate"][u], i + 2)
                        ve.tensor_tensor(hid[:, u, :], sg[:, u, :], ps[:, 4 + u, 256:512], ALU.mult
                                         ).then_inc(M["hid_done"][u], 1)
                    for u in range(2):
                        ve.wait_ge(M["hid_tr"][u], i + 2)
                        ve.tensor_copy(hidT[:, u, :, :].rearrange("p f n -> p (f n)"), ps[:, 6 + u, 0:256]
                                       ).then_inc(M["hid_copied"][u], 1)
                    for u in range(2):
                        ve.wait_ge(M["down_done"][u], i + 2)
                        ve.wait_ge(M["y_stored"][u], i * 16 + 1)
                        ve.tensor_copy(ytile[:, u, 512:1024], ps[:, 2 * u + 1, :]).then_inc(M["y_b"][u], 1)

        acc = mix[:, :, :].rearrange("p (t h) n -> p t h n", h=2)
        rows_back, weighed = [sem(f"rows_back{t}") for t in range(TT)], sem("weighed")
        yrow = w_up[:, :, :].rearrange("p a (t n) -> p a t n", t=TT)
        with nc.Block() as block:
            @block.gpsimd
            def _(pool):
                for t in range(TT):
                    for a in range(2):
                        pool.indirect_dma_start(
                            out=yrow[:, a, t, :], out_offset=None, in_=y_dram,
                            in_offset=bass.IndirectOffsetOnAxis(ap=slot_i[:, a, t:t + 1], axis=0)
                        ).then_inc(rows_back[t], 16)

            @block.vector
            def _(ve):
                for t in range(TT):
                    ve.wait_ge(rows_back[t], 32)
                    y1, y2 = yrow[:, 0, t, :], yrow[:, 1, t, :]
                    ve.tensor_scalar(y1, y1, one[:, 6, t, :], None, ALU.mult).then_inc(weighed, 1)
                    ve.wait_ge(weighed, 2 * t + 1)
                    ve.scalar_tensor_tensor(htok[:, t, :], y2, one[:, 5, t, :], y1, ALU.mult, ALU.add).then_inc(weighed, 1)
        y_done, y_added = sem("y_done"), sem("y_added")
        with nc.Block() as block:
            @block.tensor
            def _(pe):
                for k in range(KT):
                    for t in range(TT):
                        m = pe.transpose(ps[:, k, t * P:(t + 1) * P],
                                         acc[:, t, k // 4, (k % 4) * P:(k % 4 + 1) * P], ident)
                    m.then_inc(y_done, 1)

            @block.vector
            def _(ve):
                for k in range(KT):
                    ve.wait_ge(y_done, k + 1)
                    ve.scalar_tensor_tensor(res[:, k, :], ps[:, k, :], mod[:, 40 + k, 0:1], res[:, k, :],
                                            ALU.mult, ALU.add).then_inc(y_added, 1)
        moe.close()
        norm("fin", res, res, lambda k: col("final", k))

        retire()
        norm("gn", res, hn, lambda k: col("attn", k))
        V = mix
        gdn = ctx.enter_context(ExitStack())
        Q = sb("Q", [P, HEADS, T], on=gdn)
        K = sb("K", [P, HEADS, T], on=gdn)
        Z = sb("Z", [P, HEADS, T], on=gdn)
        gcols = sb("gcols", [P, 3, TT, HEADS], on=gdn)
        egl = sb("egl", [P, HEADS, TT], on=gdn)
        rows = tab[0:8, TABLES["rcount"]].rearrange("p (a t) -> p a t", a=4)
        ea = sb("ea", [8, 1], on=gdn)
        ab_done, ab_act, ab_dve, ab_tr, ab_cols = (sem(n) for n in ("ab_done", "ab_act", "ab_dve", "ab_tr", "ab_cols"))
        with nc.Block() as block:
            @block.tensor
            def _(pe):
                wab = sml[:, SMALL["wab"]].rearrange("p (k n) -> p k n", k=KT)
                for part in range(2):
                    for k in range(KT):
                        m = pe.matmul(ps[0:8, part, :], wab[:, k, 8 * part:8 * part + 8], hn[:, k, :],
                                      start=k == 0, stop=k == KT - 1)
                m.then_inc(ab_done, 1)
                pe.wait_ge(ab_dve, 6)
                for a in range(3):
                    for t in range(TT):
                        o = (a * TT + t) * 8
                        m = pe.transpose(ps[:, 2, o:o + 8], rows[:, a, t * P:(t + 1) * P], tab[0:8, 0:8])
                m.then_inc(ab_tr, 1)

            @block.scalar
            def _(act):
                n = [0]

                def step(ins):
                    n[0] += 1
                    ins.then_inc(ab_act, 1)
                    act.wait_ge(ab_act, n[0])
                act.wait_ge(ab_done, 1)
                step(act.activation(rows[:, 1, :], ps[0:8, 0, :], ACT.Sigmoid))
                step(act.activation(ea[:, :], ab8[:, 0:1], ACT.Exp))
                step(act.activation(rows[:, 3, :], ps[0:8, 1, :], ACT.Abs, bias=ab8[:, 1:2]))
                step(act.activation(rows[:, 3, :], rows[:, 3, :], ACT.Exp, scale=-1.0))
                step(act.activation(rows[:, 3, :], rows[:, 3, :], ACT.Ln, bias=1.0))
                act.wait_ge(ab_dve, 5)
                step(act.activation(rows[:, 3, :], rows[:, 0, :], ACT.Exp))

            @block.vector
            def _(ve):
                n = [0]

                def step(ins):
                    n[0] += 1
                    ins.then_inc(ab_dve, 1)
                    ve.wait_ge(ab_dve, n[0])
                ve.wait_ge(ab_act, 5)
                step(ve.tensor_scalar(rows[:, 0, :], ps[0:8, 1, :], ab8[:, 1:2], 0.0, ALU.add, ALU.max))
                step(ve.tensor_tensor(rows[:, 0, :], rows[:, 0, :], rows[:, 3, :], ALU.add))
                step(ve.tensor_scalar(rows[:, 3, :], rows[:, 0, :], ea[:, :], -1.0, ALU.mult, ALU.mult))
                step(ve.tensor_tensor_scan(rows[:, 0, :], tab[0:8, TABLES["resetd"]], rows[:, 3, :], 0.0,
                                           ALU.mult, ALU.add))
                step(ve.nop())
                ve.wait_ge(ab_act, 6)
                step(ve.tensor_tensor(rows[:, 2, :], rows[:, 1, :], rows[:, 3, :], ALU.mult))
                ve.wait_ge(ab_tr, 1)
                ve.tensor_copy(gcols[:, :, :, :].rearrange("p a t h -> p (a t h)"), ps[:, 2, 0:96]).then_inc(ab_cols, 1)

        st = gdn.enter_context(ExitStack())
        cin = sb("cin", [P, 2, 3, T + 3], on=st)
        cv = sb("cv", [P, 2, 3, T], on=st)
        sq = hctx[:, :, :].rearrange("p (u j b) t -> p u j (b t)", u=2, j=2)
        rs = sb("g_rs", [P, 2, 2, T], on=st)
        BG = STREAM["gdn"].start
        cin_zero = sem("cin_zero")
        (copied, gated_z, conv_step, conved, silued, squared, summed, mean_read, rooted, qk_step, qk_done) = (
            [sem(f"g_{n}{u}") for u in range(2)] for n in
            ("copied", "gated_z", "conv_step", "conved", "silued", "squared", "summed", "mean_read", "rooted",
             "qk_step", "qk_done"))
        with nc.Block() as block:
            @block.sync
            def _(sp):
                load_blocks(sp, STREAM["gdnout"].start + SLOTS)

            @block.gpsimd
            def _(pool):
                credit(pool, (copied, gated_z, conv_step, conved, silued, squared, summed, mean_read, rooted, qk_step,
                              qk_done))
                pool.memset(cin[:, :, :, 0:3], 0.0).then_inc(cin_zero, 1)

            @block.tensor
            def _(pe):
                with pe.Fori(0, HEADS // 2) as i:
                    for u in range(2):
                        for j in range(4):
                            if j < 2:
                                pe.wait_ge(mean_read[u], i * 2 + 1)
                            elif j == 2:
                                pe.wait_ge(copied[u], i * 3 + 1)
                            else:
                                pe.wait_ge(gated_z[u], i + 1)
                            dense_tile(pe, block_here(pe, BG + 4 * u + j, i), hn, ps[:, 4 * u + j, :])
                    for u in range(2):
                        for j in range(2):
                            pe.wait_ge(squared[u], i * 2 + j + 2)
                            pe.matmul(ps[:, 4 * u + j, :], ones, sq[:, u, j, :], start=True, stop=True).then_inc(summed[u], 1)

            @block.scalar
            def _(act):
                with act.Fori(0, HEADS // 2) as i:
                    for u in range(2):
                        for j in range(3):
                            act.wait_ge(blocks_done, i * 8 + BG + 4 * u + j + 1)
                            act.wait_ge(conved[u], i * 3 + 1)
                            act.activation(cin[:, u, j, 3:], ps[:, 4 * u + j, :], ACT.Copy).then_inc(copied[u], 1)
                        act.wait_ge(blocks_done, i * 8 + BG + 4 * u + 4)
                        apart(act)
                        act.activation(flat(Z[:, bass.ds(i * 2 + u, 1), :]), ps[:, 4 * u + 3, :], ACT.Silu).then_inc(gated_z[u], 1)
                    for u in range(2):
                        for j in range(3):
                            act.wait_ge(conved[u], i * 3 + j + 2)
                            apart(act)
                            out = cv[:, u, j, :] if j < 2 else flat(V[:, bass.ds(i * 2 + u, 1), :])
                            act.activation(out, cv[:, u, j, :], ACT.Silu).then_inc(silued[u], 1)
                        for j in range(2):
                            act.wait_ge(silued[u], i * 3 + j + 2)
                            act.wait_ge(summed[u], i * 2 + 1)
                            act.activation(sq[:, u, j, :], cv[:, u, j, :], ACT.Square).then_inc(squared[u], 1)
                    for u in range(2):
                        for j in range(2):
                            act.wait_ge(mean_read[u], i * 2 + j + 2)
                            act.activation(rs[:, u, j, :], rs[:, u, j, :], ACT.Sqrt).then_inc(rooted[u], 1)

            @block.vector
            def _(ve):
                ve.wait_ge(cin_zero, 1)
                with ve.Fori(0, HEADS // 2) as i:
                    for u in range(2):
                        for j in range(3):
                            ve.wait_ge(copied[u], i * 3 + j + 2)
                            if j == 2:
                                ve.wait_ge(silued[u], i * 3 + 1)
                            else:
                                ve.wait_ge(squared[u], i * 2 + 1)
                            for w in range(4):
                                tap = par[:, bass.ds((i * 2 + u) * 4 + PARAMS.at["conv"][0] + 32 * j + w, 1)]
                                if w == 0:
                                    ins = ve.tensor_scalar(cv[:, u, j, :], cin[:, u, j, 0:T], tap, None, ALU.mult)
                                else:
                                    ve.wait_ge(conv_step[u], i * 9 + 3 * j + w + 1)
                                    ins = ve.scalar_tensor_tensor(cv[:, u, j, :], cin[:, u, j, w:w + T], tap,
                                                                  cv[:, u, j, :], ALU.mult, ALU.add)
                                ins.then_inc(conv_step[u] if w < 3 else conved[u], 1)
                    for u in range(2):
                        for j in range(2):
                            ve.wait_ge(summed[u], i * 2 + j + 2)
                            ve.wait_ge(qk_done[u], i * 2 + 1)
                            ve.tensor_scalar(rs[:, u, j, :], ps[:, 4 * u + j, :], EPS, None, ALU.add).then_inc(mean_read[u], 1)
                    for u in range(2):
                        for j in range(2):
                            ve.wait_ge(rooted[u], i * 2 + j + 2)
                            ve.reciprocal(rs[:, u, j, :], rs[:, u, j, :]).then_inc(qk_step[u], 1)
                            ve.wait_ge(qk_step[u], i * 2 + j + 2)
                            ve.scalar_tensor_tensor(flat((Q, K)[j][:, bass.ds(i * 2 + u, 1), :]), cv[:, u, j, :],
                                                    (P ** -0.5, 1.0)[j], rs[:, u, j, :], ALU.mult, ALU.mult
                                                    ).then_inc(qk_done[u], 1)
        st.close()

        def tiles(x):
            return x.rearrange("p (n i) -> p n i", n=TT)

        def every_tile(mask):
            return mask.unsqueeze(1).to_broadcast([P, TT, P])
        KD = sb("KD", [P, HEADS, T], on=gdn)
        AT = hn
        st = gdn.enter_context(ExitStack())
        rowm = hctx[:, :, :].rearrange("p (u a b) t -> p u a (b t)", u=2, a=2)
        dm, aT_, bmT, mm_, tn, tT = (sb(f"inv_{n}", [P, 2, T], on=st) for n in ("dm", "aT", "bmT", "m", "t", "tT"))
        ks = sb("ks", [P, 2, T], on=st)
        vs = sml[:, 0:2 * T].rearrange("p (u t) -> p u t", u=2)
        names = ("staged", "rowed", "spread", "diff", "expd", "exprow", "paired", "dve", "qdec", "t_tr", "kv_tr",
                 "t_copy", "kv_ready", "masked", "m_done", "m_copy", "xy_done", "updated", "fin_done", "fin_kept")
        S = {n: [sem(f"i_{n}{u}") for u in range(2)] for n in names}
        with nc.Block() as block:
            @block.scalar
            def _(act):
                with act.Fori(0, HEADS // 2) as i:
                    heads = [bass.ds(i * 2 + u, 1) for u in range(2)]
                    for u in range(2):
                        act.wait_ge(S["fin_done"][u], i + 1)
                        apart(act)
                        act.activation(ks[:, u, :], flat(K[:, heads[u], :]), ACT.Copy).then_inc(S["staged"][u], 1)
                        act.activation(vs[:, u, :], flat(V[:, heads[u], :]), ACT.Copy).then_inc(S["staged"][u], 1)
                    for u in range(2):
                        act.wait_ge(S["diff"][u], i * 2 + 3)
                        act.activation(mm_[:, u, :], ps[:, 4 * u, :], ACT.Exp).then_inc(S["exprow"][u], 1)
                        act.activation(dm[:, u, :], dm[:, u, :], ACT.Exp).then_inc(S["expd"][u], 1)
                    for u in range(2):
                        act.wait_ge(S["t_tr"][u], i + 2)
                        act.activation(tn[:, u, :], ps[:, 4 * u + 2, :], ACT.Copy).then_inc(S["t_copy"][u], 1)
                    for lv in range(1, LEVELS + 1):
                        for u in range(2):
                            act.wait_ge(S["m_done"][u], i * LEVELS + lv + 1)
                            if lv == 1:
                                act.wait_ge(S["qdec"][u], i + 2)
                            act.activation(mm_[:, u, :], ps[:, 4 * u + 2, :], ACT.Copy).then_inc(S["m_copy"][u], 1)

            @block.gpsimd
            def _(pool):
                credit(pool, S.values())
                with pool.Fori(0, HEADS // 2) as i:
                    heads = [bass.ds(i * 2 + u, 1) for u in range(2)]
                    for u in range(2):
                        pool.wait_ge(S["exprow"][u], i + 2)
                        pool.wait_ge(S["paired"][u], i + 2)
                        apart(pool)
                        q = flat(Q[:, heads[u], :])
                        pool.tensor_tensor(q, q, mm_[:, u, :], ALU.mult).then_inc(S["qdec"][u], 1)
                    for lv in range(1, LEVELS + 1):
                        for u in range(2):
                            if lv == 1:
                                pool.wait_ge(S["dve"][u], i * 8 + 8 + 1)
                            pool.wait_ge(S["m_done"][u], i * LEVELS + lv - 1 + 1)
                            m0 = TABLES.at["level"][0] + lv * P
                            pool.tensor_tensor(tiles(bmT[:, u, :]), tiles(aT_[:, u, :]),
                                               every_tile(tab[:, m0:m0 + P]), ALU.mult).then_inc(S["masked"][u], 1)

            @block.vector
            def _(ve):
                with ve.Fori(0, HEADS // 2) as i:
                    heads = [bass.ds(i * 2 + u, 1) for u in range(2)]

                    def bycol(a, u):
                        return gcols[:, a, :, heads[u]].to_broadcast([P, TT, P])
                    for u in range(2):
                        for a in range(2):
                            ve.tensor_scalar(rowm[0:8, u, a, :], rows[:, a, :], tab[0:8, heads[u]], None,
                                             ALU.mult).then_inc(S["rowed"][u], 1)
                    for u in range(2):
                        ve.wait_ge(S["spread"][u], i + 2)
                        ve.tensor_tensor(tiles(dm[:, u, :]), tiles(ps[:, 4 * u, :]), bycol(0, u), ALU.subtract
                                         ).then_inc(S["diff"][u], 1)
                    for u in range(2):
                        ve.wait_ge(S["diff"][u], i * 2 + 2)
                        ve.tensor_scalar(dm[:, u, :], dm[:, u, :], 0.0, None, ALU.min).then_inc(S["diff"][u], 1)
                    for step in range(8):
                        for u in range(2):
                            d, at, t = tiles(dm[:, u, :]), tiles(aT_[:, u, :]), tiles(tT[:, u, :])
                            if step:
                                ve.wait_ge(S["dve"][u], i * 8 + step + 1)
                            if step == 0:
                                ve.wait_ge(S["expd"][u], i + 2)
                                ins = ve.tensor_tensor(d, d, every_tile(tab[:, TABLES["incl"]]), ALU.mult)
                            elif step == 1:
                                ve.wait_ge(S["paired"][u], i + 2)
                                ins = ve.tensor_tensor(flat(AT[:, heads[u], :]), ps[:, 4 * u + 3, :], dm[:, u, :], ALU.mult)
                            elif step == 2:
                                ins = ve.tensor_tensor(at, d, every_tile(tab[:, TABLES["strict"]]), ALU.mult)
                            elif step == 3:
                                ins = ve.tensor_tensor(aT_[:, u, :], ps[:, 4 * u + 1, :], aT_[:, u, :], ALU.mult)
                            elif step == 4:
                                ins = ve.tensor_tensor(aT_[:, u, :], ps[:, 4 * u + 2, :], aT_[:, u, :], ALU.mult)
                            elif step == 5:
                                m0 = TABLES.at["level"][0]
                                ins = ve.tensor_tensor(t, at, every_tile(tab[:, m0:m0 + P]), ALU.mult)
                            elif step == 6:
                                ins = ve.tensor_tensor(t, every_tile(ident), t, ALU.subtract)
                            else:
                                ve.wait_ge(S["exprow"][u], i + 2)
                                apart(ve)
                                ins = ve.tensor_copy(egl[:, heads[u], :].rearrange("p a n -> p n a"),
                                                     tiles(mm_[:, u, :])[:, :, P - 1:P])
                            ins.then_inc(S["dve"][u], 1)
                    for u in range(2):
                        ve.wait_ge(S["kv_tr"][u], i + 2)
                        ktok, vtok_ = tiles(ps[:, 4 * u, :]), tiles(ps[:, 4 * u + 1, :])
                        ve.tensor_tensor(flat(KD[:, heads[u], :]).rearrange("p (n i) -> p n i", n=TT), ktok,
                                         tiles(dm[:, u, :])[:, :, P - 1:P].to_broadcast([P, TT, P]), ALU.mult
                                         ).then_inc(S["kv_ready"][u], 1)
                        ve.tensor_tensor(tiles(ks[:, u, :]), ktok, bycol(2, u), ALU.mult).then_inc(S["kv_ready"][u], 1)
                        ve.tensor_tensor(tiles(vs[:, u, :]), vtok_, bycol(1, u), ALU.mult).then_inc(S["kv_ready"][u], 1)
                    for lv in range(1, LEVELS + 1):
                        for u in range(2):
                            ve.wait_ge(S["xy_done"][u], i * LEVELS + lv + 1)
                            ve.tensor_tensor(tT[:, u, :], tT[:, u, :], ps[:, 4 * u + 2, :], ALU.subtract
                                             ).then_inc(S["updated"][u], 1)
                            if lv < LEVELS:
                                ve.tensor_tensor(tn[:, u, :], tn[:, u, :], ps[:, 4 * u + 3, :], ALU.subtract
                                                 ).then_inc(S["updated"][u], 1)
                    for u in range(2):
                        ve.wait_ge(S["fin_done"][u], i + 2)
                        for n, keep in enumerate((V, K)):
                            ve.tensor_scalar(flat(keep[:, heads[u], :]), ps[:, 4 * u + n, :], 1.0, None, ALU.mult
                                             ).then_inc(S["fin_kept"][u], 1)

            @block.tensor
            def _(pe):
                def four(out, lhsT, rhs):
                    for n in range(TT):
                        c = slice(n * P, (n + 1) * P)
                        m = pe.matmul(out[:, c], lhsT[:, c], rhs[:, c], start=True, stop=True)
                    return m
                with pe.Fori(0, HEADS // 2) as i:
                    heads = [bass.ds(i * 2 + u, 1) for u in range(2)]
                    B = [[ps[:, 4 * u + n, :] for n in range(4)] for u in range(2)]
                    for u in range(2):
                        pe.wait_ge(S["rowed"][u], i * 2 + 2 + 1)
                        pe.wait_ge(S["fin_kept"][u], i * 2 + 1)
                        for a in range(2):
                            m = pe.matmul(B[u][a], tab[0:8, TABLES["ones"]], rowm[0:8, u, a, :], start=True, stop=True)
                        m.then_inc(S["spread"][u], 1)
                    for u in range(2):
                        pe.wait_ge(S["staged"][u], i * 2 + 2 + 1)
                        pe.wait_ge(S["updated"][u], i * (2 * LEVELS - 1) + 1)
                        four(B[u][2], ks[:, u, :], ks[:, u, :])
                        for n in range(TT):
                            q = Q[:, heads[u], n * P:(n + 1) * P]
                            m = pe.matmul(B[u][3][:, n * P:(n + 1) * P], ks[:, u, n * P:(n + 1) * P], flat(q),
                                          start=True, stop=True)
                        m.then_inc(S["paired"][u], 1)
                    for u in range(2):
                        pe.wait_ge(S["dve"][u], i * 8 + 7 + 1)
                        for n in range(TT):
                            c = slice(n * P, (n + 1) * P)
                            m = pe.transpose(B[u][2][:, c], tT[:, u, c], ident)
                        m.then_inc(S["t_tr"][u], 1)
                        pe.wait_ge(S["exprow"][u], i + 2)
                        for n in range(TT):
                            c = slice(n * P, (n + 1) * P)
                            pe.transpose(B[u][0][:, c], ks[:, u, c], ident)
                            m = pe.transpose(B[u][1][:, c], vs[:, u, c], ident)
                        m.then_inc(S["kv_tr"][u], 1)
                    for lv in range(1, LEVELS + 1):
                        for u in range(2):
                            pe.wait_ge(S["masked"][u], i * LEVELS + lv + 1)
                            pe.wait_ge(S["t_copy"][u], i + 2)
                            pe.wait_ge(S["updated"][u], i * (2 * LEVELS - 1) + 2 * (lv - 1) + 1)
                            four(B[u][2], bmT[:, u, :], tn[:, u, :]).then_inc(S["m_done"][u], 1)
                        for u in range(2):
                            pe.wait_ge(S["m_copy"][u], i * LEVELS + lv + 1)
                            if lv < LEVELS:
                                four(B[u][3], tT[:, u, :], mm_[:, u, :])
                            four(B[u][2], mm_[:, u, :], tT[:, u, :]).then_inc(S["xy_done"][u], 1)
                    for u in range(2):
                        pe.wait_ge(S["updated"][u], i * (2 * LEVELS - 1) + 2 * LEVELS - 1 + 1)
                        pe.wait_ge(S["kv_ready"][u], i * 3 + 3 + 1)
                        four(B[u][0], tT[:, u, :], vs[:, u, :])
                        four(B[u][1], ks[:, u, :], tT[:, u, :]).then_inc(S["fin_done"][u], 1)
        st.close()

        retire()
        st = gdn.enter_context(ExitStack())
        St = sb("St", [P, HEADS, P], on=st)
        vn = sb("vn", [P, HEADS, P], on=st)
        s_zero, ws_done, vn_done, so_done, sd_done, o_kept2 = (
            [sem(f"{n}{g}") for g in range(2)] for n in ("s_zero", "ws_done", "vn_done", "so_done", "sd_done", "o_kept2"))
        s_next = [sem(f"s_next{g}") for g in range(2)]
        with nc.Block() as block:
            @block.tensor
            def _(pe):
                for n in range(TT):
                    c = slice(n * P, (n + 1) * P)
                    for g in range(2):
                        pe.wait_ge(s_next[g], 2 * n + 1)
                        for h in range(4):
                            m = pe.matmul(ps[:, g, h * P:(h + 1) * P], K[:, 4 * g + h, c], St[:, 4 * g + h, :],
                                          start=True, stop=True)
                        m.then_inc(ws_done[g], 1)
                    for g in range(2):
                        pe.wait_ge(vn_done[g], n + 1)
                        if n:
                            pe.wait_ge(o_kept2[g], n)
                        for h in range(4):
                            out = ps[:, 2 + g, h * P:(h + 1) * P]
                            pe.matmul(out, St[:, 4 * g + h, :], Q[:, 4 * g + h, c], start=True, stop=False)
                            m = pe.matmul(out, vn[:, 4 * g + h, :], AT[:, 4 * g + h, c], start=False, stop=True)
                        m.then_inc(so_done[g], 1)
                        if n < TT - 1:
                            for h in range(4):
                                m = pe.matmul(ps[:, 4 + g, h * P:(h + 1) * P], KD[:, 4 * g + h, c],
                                              vn[:, 4 * g + h, :], start=True, stop=True)
                            m.then_inc(sd_done[g], 1)

            @block.vector
            def _(ve):
                for g in range(2):
                    ve.memset(St[:, 4 * g:4 * g + 4, :], 0.0).then_inc(s_next[g], 1)
                for n in range(TT):
                    for g in range(2):
                        hs = slice(4 * g, 4 * g + 4)
                        ve.wait_ge(ws_done[g], n + 1)
                        if n:
                            ve.wait_ge(sd_done[g], n)
                            ve.wait_ge(so_done[g], n)
                        ve.tensor_tensor(vn[:, hs, :], V[:, hs, n * P:(n + 1) * P],
                                         ps[:, g, :].rearrange("p (h e) -> p h e", h=4), ALU.subtract
                                         ).then_inc(vn_done[g], 1)
                    for g in range(2):
                        if n == TT - 1:
                            break
                        hs = slice(4 * g, 4 * g + 4)
                        ve.wait_ge(so_done[g], n + 1)
                        ve.tensor_tensor(St[:, hs, :], St[:, hs, :], egl[:, hs, n:n + 1].to_broadcast([P, 4, P]),
                                         ALU.mult).then_inc(s_next[g], 1)
                        ve.wait_ge(s_next[g], 2 * n + 2)
                        ve.wait_ge(sd_done[g], n + 1)
                        ve.tensor_tensor(St[:, hs, :], St[:, hs, :], ps[:, 4 + g, :].rearrange("p (h e) -> p h e", h=4),
                                         ALU.add).then_inc(s_next[g], 1)

            @block.scalar
            def _(act):
                for n in range(TT):
                    for g in range(2):
                        act.wait_ge(so_done[g], n + 1)
                        act.activation(Q[:, 4 * g:4 * g + 4, n * P:(n + 1) * P],
                                       ps[:, 2 + g, :].rearrange("p (h e) -> p h e", h=4), ACT.Copy
                                       ).then_inc(o_kept2[g], 1)
        st.close()

        on_sq, on_sum, on_ms, on_root, on_step, on_done = (
            sem(n) for n in ("on_sq", "on_sum", "on_ms", "on_root", "on_step", "on_done"))
        with nc.Block() as block:
            @block.scalar
            def _(act):
                for h in range(HEADS):
                    act.activation(hn[:, h, :], Q[:, h, :], ACT.Square).then_inc(on_sq, 1)
                for h in range(HEADS):
                    act.wait_ge(on_ms, h + 1)
                    act.activation(mix[:, h, :], mix[:, h, :], ACT.Sqrt).then_inc(on_root, 1)

            @block.tensor
            def _(pe):
                for h in range(HEADS):
                    pe.wait_ge(on_sq, h + 1)
                    pe.matmul(ps[:, h, :], ones, hn[:, h, :], start=True, stop=True).then_inc(on_sum, 1)

            @block.vector
            def _(ve):
                for h in range(HEADS):
                    ve.wait_ge(on_sum, h + 1)
                    ve.tensor_scalar(mix[:, h, :], ps[:, h, :], 1.0 / P, EPS, ALU.mult, ALU.add).then_inc(on_ms, 1)
                for h in range(HEADS):
                    ve.wait_ge(on_root, h + 1)
                    ve.reciprocal(mix[:, h, :], mix[:, h, :]).then_inc(on_step, 1)
                    ve.wait_ge(on_step, 2 * h + 1)
                    ve.scalar_tensor_tensor(mix[:, h, :], Q[:, h, :], col("ogain"), mix[:, h, :], ALU.mult, ALU.mult
                                            ).then_inc(on_step, 1)
                    ve.wait_ge(on_step, 2 * h + 2)
                    ve.tensor_tensor(Q[:, h, :], mix[:, h, :], Z[:, h, :], ALU.mult).then_inc(on_done, 1)
        project_out("gdnout", Q, STREAM["gdnout"].start, None, STREAM["gu0"].start + SLOTS)
        gdn.close()

        def three(pe, out, w_hi, w_lo, a_hi, a_lo, start, stop):
            pe.matmul(out, w_hi, a_hi, start=start, stop=False)
            pe.matmul(out, w_lo, a_hi, start=False, stop=False)
            return pe.matmul(out, w_hi, a_lo, start=False, stop=stop)

        def feed_forward(layer):
            norm(f"fn{layer}", res, hn, lambda k: col("ffn", 8 * layer + k))
            with ExitStack() as st:
                act_ = sb(f"ff_act{layer}", [P, FT, T], on=st)
                sg = hctx[:, :, :].rearrange("p (a b) t -> p a (b t)", b=2)
                w_hi, w_lo = (sb(f"ff_w{n}{layer}", [P, 2, 1024], F32R, on=st) for n in ("hi", "lo"))
                a_hi, a_lo = (sb(f"ff_a{n}{layer}", [P, 2, T], F32R, on=st) for n in ("hi", "lo"))
                h_hi, h_lo = (sb(f"ff_h{n}{layer}", [P, KT, T], F32R, on=st) for n in ("hi", "lo"))
                B0 = STREAM[f"gu{layer}"].start
                B1 = STREAM[f"down{layer}"].start
                silu_done, act_ready, added, h_split, w_rounded, tile_done, a_rounded, a_split, row_done, h_rest = (
                    sem(f"ff_{n}{layer}") for n in ("silu", "act", "added", "h_split", "w_rounded", "tile_done",
                                                    "a_rounded", "a_split", "row_done", "h_rest"))
                turns, rest = FT // 4, FT % 4
                with nc.Block() as block:
                    @block.sync
                    def _(sp):
                        load_blocks(sp, B1 + FT + SLOTS)

                    @block.tensor
                    def _(pe):
                        def up(i, pairs, extra):
                            for j in range(2 * pairs):
                                pe.wait_ge(act_ready, i * 4 + extra + j // 2 + 1)
                                b = B0 + 2 * extra + j
                                pe.wait_ge(blocks_done, i * SLOTS + b + 1)
                                for k in range(KT):
                                    c = slice(k * P, (k + 1) * P)
                                    m = three(pe, ps[:, j, :], w_hi[:, j % 2, c], w_lo[:, j % 2, c],
                                              h_hi[:, k, :], h_lo[:, k, :], k == 0, k == KT - 1)
                                m.then_inc(tile_done, 1)
                        pe.wait_ge(h_rest, KT)
                        with pe.Fori(0, turns) as i:
                            up(i, 4, 0)
                        up(0, rest, 4 * turns)
                        pe.wait_ge(act_ready, 4 + FT)
                        for f in range(FT):
                            pe.wait_ge(blocks_done, B1 + f + 1)
                            pe.wait_ge(a_split, f + 1)
                            for n in range(KT):
                                c = slice(n * P, (n + 1) * P)
                                m = three(pe, ps[:, n, :], w_hi[:, f % 2, c], w_lo[:, f % 2, c],
                                          a_hi[:, f % 2, :], a_lo[:, f % 2, :], f == 0, f == FT - 1)
                            m.then_inc(row_done, 1)

                    def round_block(act, j, i=None):
                        b = B0 + j
                        s, v = b % SLOTS, 16 * (b // SLOTS + 1)
                        act.wait_ge(block_in[s], v if i is None else i * 16 + v)
                        if j >= 2 * FT + 2:
                            act.wait_ge(row_done, j - 2 * FT - 1)
                        elif i is not None or j >= 2:
                            act.wait_ge(tile_done, (0 if i is None else i * SLOTS) + j + 1)
                        act.activation(w_hi[:, j % 2, :], ring[:, s, :], ACT.Copy).then_inc(w_rounded, 1)

                    def rest_of_block(ve, j, i=None):
                        ve.wait_ge(w_rounded, (0 if i is None else i * SLOTS) + j + 1)
                        ve.tensor_tensor(w_lo[:, j % 2, :], ring[:, (B0 + j) % SLOTS, :], w_hi[:, j % 2, :].bitcast(F32),
                                         ALU.subtract).then_inc(blocks_done, 1)

                    def round_row(act, f):
                        if f >= 2:
                            act.wait_ge(row_done, f - 1)
                        act.wait_ge(act_ready, 4 + f + 1)
                        act.activation(a_hi[:, f % 2, :], act_[:, f, :], ACT.Copy).then_inc(a_rounded, 1)

                    def rest_of_row(ve, f):
                        ve.wait_ge(a_rounded, f + 1)
                        ve.tensor_tensor(a_lo[:, f % 2, :], act_[:, f, :], a_hi[:, f % 2, :].bitcast(F32),
                                         ALU.subtract).then_inc(a_split, 1)

                    @block.scalar
                    def _(act):
                        act.sem_inc(tile_done, 2)
                        for k in range(KT):
                            act.activation(h_hi[:, k, :], hn[:, k, :], ACT.Copy).then_inc(h_split, 1)
                        round_block(act, 0)
                        round_block(act, 1)

                        def gate(i, pairs, extra):
                            t = 0 if i is None else i
                            for p in range(pairs):
                                act.wait_ge(tile_done, t * 8 + 2 * extra + 2 * p + 1 + 2)
                                act.wait_ge(act_ready, t * 4 + extra + p + 1)
                                act.activation(sg[:, p, :], ps[:, 2 * p, :], ACT.Silu).then_inc(silu_done, 1)
                                for j in range(2):
                                    round_block(act, 2 * (extra + p) + 2 + j, i)
                        with act.Fori(0, turns) as i:
                            gate(i, 4, 0)
                        gate(None, rest, 4 * turns)
                        round_row(act, 0)
                        for f in range(FT):
                            if f + 1 < FT:
                                round_row(act, f + 1)
                            if f + 2 < FT:
                                round_block(act, 2 * FT + f + 2)

                    @block.vector
                    def _(ve):
                        ve.sem_inc(act_ready, 4)
                        for k in range(KT):
                            ve.wait_ge(h_split, k + 1)
                            ve.tensor_tensor(h_lo[:, k, :], hn[:, k, :], h_hi[:, k, :].bitcast(F32),
                                             ALU.subtract).then_inc(h_rest, 1)
                        rest_of_block(ve, 0)
                        rest_of_block(ve, 1)

                        def gated(i, pairs, extra):
                            t = 0 if i is None else i
                            for p in range(pairs):
                                rest_of_block(ve, 2 * (extra + p) + 2, i)
                                ve.wait_ge(silu_done, t * 4 + extra + p + 1)
                                ve.wait_ge(tile_done, t * 8 + 2 * extra + 2 * p + 2 + 2)
                                at = act_[:, extra + p, :] if i is None else flat(act_[:, bass.ds(i * 4 + p, 1), :])
                                ve.tensor_tensor(at, sg[:, p, :], ps[:, 2 * p + 1, :], ALU.mult).then_inc(act_ready, 1)
                                rest_of_block(ve, 2 * (extra + p) + 3, i)
                        with ve.Fori(0, turns) as i:
                            gated(i, 4, 0)
                        gated(None, rest, 4 * turns)
                        rest_of_row(ve, 0)
                        for f in range(FT):
                            if f + 1 < FT:
                                rest_of_row(ve, f + 1)
                            if f + 2 < FT:
                                rest_of_block(ve, 2 * FT + f + 2)
                        for n in range(KT):
                            ve.wait_ge(row_done, FT)
                            ve.tensor_tensor(res[:, n, :], ps[:, n, :], res[:, n, :], ALU.add).then_inc(added, 1)

        mixed.close()
        feed_forward(0)

        retire()
        sbt = ctx.enter_context(ExitStack())
        mix = sb("sbV", [P, KT, T], on=sbt)
        Q = sb("sbQ", [P, HEADS, T], on=sbt)
        K = sb("sbK", [P, HEADS, T], on=sbt)
        V = mix[:, :, :].rearrange("p (t a) (c d) -> p t (a c) d", a=2, d=P)
        st = sbt.enter_context(ExitStack())
        hk = sb("hk", [P, KT, T], on=st)
        norm("kv", res, hk, lambda k: col("kvn", k))
        norm("an", res, hn, lambda k: col("attn", 8 + k))
        sq = sb("sb_sq", [P, HEADS, T], on=st)
        rs = sb("sb_rs", [P, HEADS, T], on=st)

        def heads_normed(name, src, dst, gain, first_block):
            squared, summed, mean_read, rooted, step, done = (
                sem(f"{name}_{n}") for n in ("squared", "summed", "mean_read", "rooted", "step", "done"))
            with nc.Block() as block:
                @block.sync
                def _(sp):
                    load_blocks(sp, first_block + HEADS + SLOTS)

                @block.tensor
                def _(pe):
                    for q in (0, 4):
                        for h in range(q, q + 4):
                            if q:
                                pe.wait_ge(done, h - 3)
                            dense_tile(pe, block_here(pe, first_block + h), src, ps[:, h % 4, :])
                        for h in range(q, q + 4):
                            pe.wait_ge(squared, h + 1)
                            if q:
                                pe.wait_ge(mean_read, h - 3)
                            pe.matmul(ps[:, 4 + h % 4, :], ones, sq[:, h, :], start=True, stop=True).then_inc(summed, 1)

                @block.scalar
                def _(act):
                    for q in (0, 4):
                        for h in range(q, q + 4):
                            act.wait_ge(blocks_done, first_block + h + 1)
                            act.activation(sq[:, h, :], ps[:, h % 4, :], ACT.Square).then_inc(squared, 1)
                        for h in range(q, q + 4):
                            act.wait_ge(mean_read, h + 1)
                            act.activation(rs[:, h, :], rs[:, h, :], ACT.Sqrt).then_inc(rooted, 1)

                @block.vector
                def _(ve):
                    for q in (0, 4):
                        for h in range(q, q + 4):
                            ve.wait_ge(summed, h + 1)
                            ve.tensor_scalar(rs[:, h, :], ps[:, 4 + h % 4, :], 1.0 / P, EPS, ALU.mult, ALU.add
                                             ).then_inc(mean_read, 1)
                        for h in range(q, q + 4):
                            ve.wait_ge(rooted, h + 1)
                            ve.reciprocal(rs[:, h, :], rs[:, h, :]).then_inc(step, 1)
                            ve.wait_ge(step, h + 1)
                            ve.wait_ge(squared, h + 1)
                            ve.scalar_tensor_tensor(dst[:, h, :], ps[:, h % 4, :], gain, rs[:, h, :],
                                                    ALU.mult, ALU.mult).then_inc(done, 1)

        heads_normed("kh", hk, K, col("kgain"), STREAM["sbk"].start)
        v_kept = sem("v_kept")
        BV2 = STREAM["sbv"].start
        with nc.Block() as block:
            @block.sync
            def _(sp):
                load_blocks(sp, STREAM["sbq"].start + SLOTS)

            @block.tensor
            def _(pe):
                for k in range(KT):
                    w = block_here(pe, BV2 + k)
                    for n in range(8):
                        t, half = n // 2, n % 2
                        m = pe.matmul(ps[:, n, :], hk[:, k, t * P:(t + 1) * P], w[:, half * 512:(half + 1) * 512],
                                      start=k == 0, stop=k == KT - 1)
                    m.then_inc(blocks_done, 1)

            @block.scalar
            def _(act):
                act.wait_ge(blocks_done, BV2 + KT)
                for n in range(8):
                    act.activation(mix[:, n, :], ps[:, n, :], ACT.Copy).then_inc(v_kept, 1)
        heads_normed("qh", hn, Q, col("qgain"), STREAM["sbq"].start)
        st.close()

        WIDTH = [T - a * P for a in range(TT)]
        OFF = [sum(WIDTH[:a]) for a in range(TT)]
        PACKED = sum(WIDTH)
        scale = float(P) ** -0.5
        st = sbt.enter_context(ExitStack())
        ks = sb("a_ks", [P, 2, T], on=st)
        vs = sb("a_vs", [P, 2, TT, P], on=st)
        lo, sp_, ln = (sb(f"a_{n}", [P, 2, PACKED], on=st) for n in ("lo", "sp", "ln"))
        names = ("staged", "z_done", "abs_done", "ln_done", "z_read", "summed", "fail_ready", "rest_done", "log_a",
                 "exp_done", "att_ready", "o_done", "o_kept")
        A = {n: [sem(f"a_{n}{u}") for u in range(2)] for n in names}
        with nc.Block() as block:
            @block.scalar
            def _(act):
                with act.Fori(0, HEADS // 2) as i:
                    heads = [bass.ds(i * 2 + u, 1) for u in range(2)]
                    for u in range(2):
                        act.wait_ge(A["o_done"][u], i + 1)
                        apart(act)
                        act.activation(ks[:, u, :], flat(K[:, heads[u], :]), ACT.Copy).then_inc(A["staged"][u], 1)
                        act.activation(vs[:, u, :, :], V[:, :, heads[u], :].rearrange("p t a d -> p t (a d)"), ACT.Copy
                                       ).then_inc(A["staged"][u], 1)
                    for u in range(2):
                        act.wait_ge(A["z_done"][u], i + 2)
                        for a in range(TT):
                            act.activation(ln[:, u, OFF[a]:OFF[a] + WIDTH[a]], ps[:, 4 * u + a, 0:WIDTH[a]], ACT.Abs,
                                           scale=scale).then_inc(A["abs_done"][u], 1)
                    for u in range(2):
                        act.wait_ge(A["abs_done"][u], i * 4 + 4 + 1)
                        act.activation(ln[:, u, :], ln[:, u, :], ACT.Exp, scale=-1.0).then_inc(A["ln_done"][u], 1)
                        act.wait_ge(A["ln_done"][u], i * 2 + 2)
                        act.activation(ln[:, u, :], ln[:, u, :], ACT.Ln, bias=1.0).then_inc(A["ln_done"][u], 1)
                    for u in range(2):
                        act.wait_ge(A["log_a"][u], i * 4 + 4 + 1)
                        act.activation(lo[:, u, :], lo[:, u, :], ACT.Exp).then_inc(A["exp_done"][u], 1)
                    for u in range(2):
                        act.wait_ge(A["o_done"][u], i + 2)
                        apart(act)
                        act.activation(flat(Q[:, heads[u], :]), ps[:, 4 * u, :], ACT.Copy).then_inc(A["o_kept"][u], 1)

            @block.gpsimd
            def _(pool):
                credit(pool, A.values())
                with pool.Fori(0, HEADS // 2) as i:
                    for u in range(2):
                        pool.wait_ge(A["summed"][u], i * 2 + 2 + 1)
                        for a in range(TT):
                            d = sp_[:, u, OFF[a]:OFF[a] + P]
                            pool.tensor_tensor(d, d, tab[:, TABLES["strict"]], ALU.mult).then_inc(A["fail_ready"][u], 1)
                    for u in range(2):
                        pool.wait_ge(A["exp_done"][u], i + 2)
                        for a in range(TT):
                            d = lo[:, u, OFF[a]:OFF[a] + P]
                            pool.tensor_tensor(d, d, tab[:, TABLES["strict"]], ALU.mult).then_inc(A["att_ready"][u], 1)

            @block.vector
            def _(ve):
                with ve.Fori(0, HEADS // 2) as i:
                    for u in range(2):
                        ve.wait_ge(A["o_done"][u], i + 1)
                        for a in range(TT):
                            c = slice(OFF[a], OFF[a] + WIDTH[a])
                            z = ps[:, 4 * u + a, 0:WIDTH[a]]
                            ve.wait_ge(A["abs_done"][u], i * 4 + a + 2)
                            ve.tensor_scalar(lo[:, u, c], z, scale, 0.0, ALU.mult, ALU.min).then_inc(A["z_read"][u], 1)
                            ve.tensor_scalar(sp_[:, u, c], z, scale, 0.0, ALU.mult, ALU.max).then_inc(A["z_read"][u], 1)
                    for u in range(2):
                        ve.wait_ge(A["z_read"][u], i * 8 + 8 + 1)
                        ve.wait_ge(A["ln_done"][u], i * 2 + 2 + 1)
                        ve.tensor_tensor(sp_[:, u, :], sp_[:, u, :], ln[:, u, :], ALU.add).then_inc(A["summed"][u], 1)
                        ve.tensor_tensor(lo[:, u, :], lo[:, u, :], ln[:, u, :], ALU.subtract).then_inc(A["summed"][u], 1)
                    for u in range(2):
                        ve.wait_ge(A["summed"][u], i * 2 + 2 + 1)
                        ve.wait_ge(A["rest_done"][u], i + 2)
                        for a in range(TT):
                            c = slice(OFF[a], OFF[a] + WIDTH[a])
                            ve.tensor_tensor(lo[:, u, c], lo[:, u, c], ps[:, 4 * u + a, 0:WIDTH[a]], ALU.subtract
                                             ).then_inc(A["log_a"][u], 1)

            @block.tensor
            def _(pe):
                with pe.Fori(0, HEADS // 2) as i:
                    heads = [bass.ds(i * 2 + u, 1) for u in range(2)]
                    for u in range(2):
                        pe.wait_ge(A["staged"][u], i * 2 + 2 + 1)
                        pe.wait_ge(A["o_kept"][u], i + 1)
                        for a in range(TT):
                            m = pe.matmul(ps[:, 4 * u + a, 0:WIDTH[a]], ks[:, u, a * P:(a + 1) * P],
                                          flat(Q[:, heads[u], a * P:T]), start=True, stop=True)
                        m.then_inc(A["z_done"][u], 1)
                    for u in range(2):
                        pe.wait_ge(A["fail_ready"][u], i * 4 + 4 + 1)
                        for a in range(TT):
                            for b in range(a, TT):
                                m = pe.matmul(ps[:, 4 * u + a, (b - a) * P:WIDTH[a]],
                                              tab[:, TABLES["after"]] if a == b else ones,
                                              sp_[:, u, OFF[b]:OFF[b] + WIDTH[b]], start=a == b, stop=a == b,
                                              skip_group_check=a != b)
                        m.then_inc(A["rest_done"][u], 1)
                    for u in range(2):
                        pe.wait_ge(A["att_ready"][u], i * 4 + 4 + 1)
                        for a in range(TT):
                            m = pe.matmul(ps[:, 4 * u, a * P:T], vs[:, u, a, :], lo[:, u, OFF[a]:OFF[a] + WIDTH[a]],
                                          start=a == 0, stop=a == 0, skip_group_check=a != 0)
                        m.then_inc(A["o_done"][u], 1)
        st.close()
        project_out("sbout", Q, STREAM["sbout"].start, None, STREAM["gu1"].start + SLOTS)
        sbt.close()
        feed_forward(1)
        stored = sem("stored")
        with nc.Block() as block:
            @block.sync
            def _(sp):
                sp.dma_start(outT.rearrange("(k p) t -> p k t", p=P), res[:, :, :]).then_inc(stored, 16)
                sp.wait_ge(stored, 16)

def kernel(**inputs):
    import concourse.bacc as bacc
    from concourse.bass_utils import run_bass_kernel_spmd

    a = {k: np.asarray(v) for k, v in inputs.items()}

    def by_tile(w):
        return w.reshape(KT, P, -1, P).transpose(2, 1, 0, 3).reshape(-1, P, 1024)

    def by_row(w):
        return w.reshape(-1, P, 1024)

    def pairs(w):
        return w.reshape(4, 2, P, 512).transpose(0, 2, 1, 3).reshape(4, P, 1024)

    def column(v):
        return v.reshape(-1, P).T

    w_in, gdn = a["w_in"][0], a["gdn_w_in_2"][0]
    ei = a["w_expert_in"][0].reshape(NEXP, KT, P, 512).transpose(0, 2, 1, 3).reshape(NEXP, P, -1)
    eo = a["w_expert_out"][0].reshape(NEXP, 2, P, D).transpose(0, 2, 1, 3).reshape(NEXP, P, -1)
    gt = by_tile(gdn[:, :4096]).reshape(4, 8, P, 1024).transpose(1, 0, 2, 3)
    gu = [by_tile(w).reshape(2, FT, P, 1024).transpose(1, 0, 2, 3).reshape(-1, P, 1024) for w in a["ffn_w_gu_2"]]
    stream = np.concatenate([
        a["w_ada"][0].reshape(KT, P, 6, D).transpose(2, 0, 1, 3).reshape(-1, P, D), by_tile(w_in[:, 256:512]), pairs(w_in[:, 512:1024]), by_tile(w_in[:, 0:256]),
        by_tile(w_in[:, 1024:1536]), by_tile(w_in[:, 1568:2080]), by_tile(a["w_out"][0]),
        gt.reshape(-1, P, 1024),
        by_tile(a["gdn_w_out_2"][0]), gu[0], by_row(a["ffn_w_down_2"][0]), by_tile(a["w_kv_2"][:, :D]),
        by_row(a["w_kv_2"][:, D:]), by_tile(a["sb_w_q_2"][0]), by_tile(a["sb_w_out_2"][0]), gu[1],
        by_row(a["ffn_w_down_2"][1])])
    small = np.concatenate([
        w_in[:, 1536:1568].reshape(KT, P, 32).transpose(1, 0, 2).reshape(P, -1),
        gdn[:, 4096:4112].reshape(KT, P, 16).transpose(1, 0, 2).reshape(P, -1),
        np.concatenate([a["w_router_group"][0], a["w_router_expert"][0]], axis=1).reshape(KT, P, 36)
        .transpose(1, 0, 2).reshape(P, -1),
        a["w_pool"][0].transpose(1, 0, 2).reshape(P, -1)], axis=1)
    params = np.concatenate([
        column(a["b_ada"][0]), column(a["norm1_g"][0]), column(a["norm2_g"][0]), column(a["final_norm_g"]),
        column(a["attn_norm_2"].reshape(-1)), column(a["ffn_norm_2"].reshape(-1)), column(a["kv_norm_2"]),
        column(a["gla_norm_g"][0]), column(a["pool_scale"][0]), column(a["b_decay"][0].reshape(-1)),
        a["gdn_conv_w_2"][0].reshape(4, 24, P).transpose(2, 1, 0).reshape(P, 96), column(a["gdn_o_gain_2"][0]),
        column(a["k_gain_2"]), column(a["sb_q_gain_2"][0]),
        np.stack([a["c"][0], a["c_ctx"]], axis=1).reshape(KT, P, 2).transpose(1, 0, 2).reshape(P, 16)], axis=1)
    arrays = {
        "xT": a["x"][0].T, "ctxT": a["ctx"][0].T, "stream": stream,
        "experts": np.concatenate([ei, eo], axis=2), "small": small, "params": params,
        "heads8": np.stack([a["gdn_a_log_2"][0], a["gdn_dt_bias_2"][0]], axis=1), "wdec": a["w_decay"][0],
        "table": tables()}
    arrays = {k: np.ascontiguousarray(v) for k, v in arrays.items()}
    nc = bacc.Bacc("TRN2", target_bir_lowering=False, num_devices=1)
    aps = [nc.dram_tensor(k, v.shape, F32, kind="ExternalInput").ap() for k, v in arrays.items()]
    out = nc.dram_tensor("outT", (D, T), F32, kind="ExternalOutput").ap()
    program(nc, *aps, out)
    r = run_bass_kernel_spmd(nc, [arrays], core_ids=[0])
    return np.ascontiguousarray(r.results[0]["outT"].T)[None]
```

```python
from contextlib import ExitStack

import numpy as np
import concourse.bass as bass
from concourse import mybir

F32 = mybir.dt.float32
U8 = mybir.dt.uint8
F32R = mybir.dt.float32r
ALU = mybir.AluOpType
ACT = mybir.ActivationFunctionType
AX = mybir.AxisListType
P = 128
D = 1024
KT = D // P
T = 512
TT = T // P
CTX = 256
TA = T + CTX
EPS = 1e-6
SLOTS = 8
NEXP = 32
FF = 2816
FT = FF // P
HEADS = 8
GRID_W = 64
ROWS = T // GRID_W
WINDOWS = (2, 4, 8, 16)
LEVELS = 6
MASKED_LOW = -3.0e38
MAXTILES = 40
MINTILES = 2 * T // P


class Cols:

    def __init__(self, parts):
        self.at, n = {}, 0
        for name, width in parts:
            self.at[name] = (n, n + width)
            n += width
        self.n = n

    def __getitem__(self, name):
        return slice(*self.at[name])


PARAMS = Cols([("b_ada", 48), ("norm1", 8), ("norm2", 8), ("final", 8), ("attn", 16), ("ffn", 16), ("kvn", 8),
               ("gla", 1), ("pscale", 4), ("bdec", 4), ("conv", 96), ("ogain", 1), ("kgain", 1), ("qgain", 1),
               ("cvec", 16)])
TABLES = Cols([("ident", P), ("ones", P), ("incl", P), ("strict", P), ("after", P),
               ("glaf", P), ("glab", P), ("level", P * (LEVELS + 1)), ("rank", 8), ("resetg", TA), ("resetd", T),
               ("rcount", 4 * T), ("tile", MAXTILES), ("token", TT)])
STREAM = Cols([("ada", 16), ("k", 2), ("v", 4), ("q", 2), ("g", 4), ("p", 4), ("ada2", 32), ("out", 8),
               ("gdn", 32), ("gdnout", 8), ("gu0", 2 * FT), ("down0", FT), ("sbq", 8), ("sbk", 8), ("sbv", 8),
               ("sbout", 8), ("gu1", 2 * FT), ("down1", FT)])
SMALL = Cols([("wa", 8 * 32), ("wab", 8 * 16), ("router", 8 * 36), ("pool", 4 * P)])


def tables():
    t = np.zeros((P, TABLES.n), np.float32)
    j, i = np.arange(P)[:, None], np.arange(P)[None, :]
    t[:, TABLES["ident"]] = j == i
    t[:, TABLES["ones"]] = 1
    t[:, TABLES["incl"]] = j <= i
    t[:, TABLES["strict"]] = j < i
    t[:, TABLES["after"]] = j > i
    same = j // 64 == i // 64
    t[:, TABLES["glaf"]] = same & (j <= i)
    t[:, TABLES["glab"]] = same & (j >= i)
    lv = t[:, TABLES["level"]].reshape(P, LEVELS + 1, P)
    for n in range(LEVELS + 1):
        s = 1 << n
        lv[:, n] = (j // (2 * s) == i // (2 * s)) & (j % (2 * s) < s) & (i % (2 * s) >= s)
    t[:, TABLES["level"]] = lv.reshape(P, -1)
    t[:, TABLES["rank"]] = 8 - np.arange(8)
    t[:, TABLES["resetg"]] = np.arange(TA) % 64 != 0
    t[:, TABLES["resetd"]] = np.arange(T) % P != 0
    rc = np.zeros((4, ROWS, GRID_W), np.float32)
    for g, w in enumerate(WINDOWS):
        lo, hi = w // 2, w - 1 - w // 2
        count = [np.clip(np.arange(n) + hi + 1, 0, n) - np.clip(np.arange(n) - lo, 0, n) for n in (ROWS, GRID_W)]
        rc[g] = 1.0 / (count[0][:, None] * count[1][None, :])
    t[:, TABLES["rcount"]] = rc.reshape(1, -1)
    t[:, TABLES["tile"]] = np.arange(MAXTILES)
    t[:, TABLES["token"]] = np.arange(P)[:, None] + P * np.arange(TT)
    return t


def window_blocks():
    token = np.arange(P)
    blocks, at = [], {}
    for g, w in enumerate(WINDOWS):
        lo, hi = w // 2, w - 1 - w // 2
        across = (token % GRID_W)[:, None] - (token % GRID_W)[None, :]
        for dt in range(-TT + 1, TT):
            down = (token // GRID_W)[:, None] - (token // GRID_W)[None, :] + dt * (P // GRID_W)
            b = ((-lo <= across) & (across <= hi) & (-lo <= down) & (down <= hi)).astype(np.float32)
            if b.any():
                same = [n for n, other in enumerate(blocks) if (other == b).all()]
                at[g, dt] = same[0] if same else len(blocks)
                if not same:
                    blocks.append(b)
    return np.concatenate(blocks, axis=1), at


def flat(ap):
    return ap.rearrange("p a n -> p (a n)")


def program(nc, xT, ctxT, stream, experts, small, params, heads8, wdec, table, windows, outT):
    with ExitStack() as ctx:
        def sb(name, shape, dt=F32, on=None):
            return (on or ctx).enter_context(nc.sbuf_tensor(name, shape, dt))

        live = []

        def sem(name):
            live.append(nc.alloc_semaphore(name))
            return live[-1]

        def kept_sem(name):
            return ctx.enter_context(nc.semaphore(name))

        def retire():
            nc.clear_and_free_semaphores(list(live))
            live.clear()
            nc.all_engine_barrier()

        ring = sb("ring", [P, SLOTS, 1024])
        res = sb("res", [P, KT, T])
        hn = sb("hn", [P, KT, T])
        par = sb("par", [P, PARAMS.n])
        tab = sb("tab", [P, TABLES.n])
        sml = sb("sml", [P, SMALL.n])
        mod = sb("mod", [P, 48, 2])
        ab8 = sb("ab8", [8, 2])
        ps = ctx.enter_context(nc.psum_tensor("ps", [P, 8, 512], F32))

        h2_dram = nc.dram_tensor("h2_dram", (T, D), F32).ap()
        y_dram = nc.dram_tensor("y_dram", (MAXTILES * P, D), F32).ap()
        tok_dram = nc.dram_tensor("tok_dram", (MAXTILES * P, 1), F32).ap()
        h_stored = kept_sem("h_stored")

        ident = tab[:, TABLES["ident"]]
        ones = tab[:, TABLES["ones"]]

        def col(name, i=0):
            a = PARAMS.at[name][0] + i
            return par[:, a:a + 1]

        block_in = [kept_sem(f"block_in{s}") for s in range(SLOTS)]
        blocks_done = kept_sem("blocks_done")
        issued = [0]

        def load_blocks(sp, upto_block):
            upto_block = min(upto_block, STREAM.n)

            def one(b, i=None):
                s = b % SLOTS
                back = b - SLOTS + 1
                if i is None:
                    if back > 0:
                        sp.wait_ge(blocks_done, back)
                    src = stream[b]
                else:
                    sp.wait_ge(blocks_done, i * SLOTS + back)
                    src = flat(stream[bass.ds(i * SLOTS + b, 1)].rearrange("a p n -> p a n"))
                sp.dma_start(ring[:, s, :], src).then_inc(block_in[s], 16)

            while issued[0] < SLOTS and issued[0] < upto_block:
                one(issued[0])
                issued[0] += 1
            turns = (upto_block - issued[0]) // SLOTS
            if turns > 1:
                with sp.Fori(0, turns) as i:
                    for j in range(SLOTS):
                        one(issued[0] + j, i)
                issued[0] += turns * SLOTS
            while issued[0] < upto_block:
                one(issued[0])
                issued[0] += 1

        def block_here(pe, b, later=None):
            v = 16 * (b // SLOTS + 1)
            pe.wait_ge(block_in[b % SLOTS], v if later is None else later * 16 + v)
            return ring[:, b % SLOTS, :]

        def dense_tile(pe, w, act, out):
            for k in range(KT):
                m = pe.matmul(out, w[:, k * P:(k + 1) * P], act[:, k, :], start=k == 0, stop=k == KT - 1)
            m.then_inc(blocks_done, 1)

        def credit(pool, sems):
            for pair in sems:
                for s in pair:
                    pool.sem_inc(s, 1)

        def apart(eng):
            eng.wait_ge(small_in, 48)

        def mod_rows(pe, first, i, bank):
            for k in range(KT):
                w = block_here(pe, first + k, i)
                for half in range(2):
                    m = pe.matmul(ps[0:2, bank + half, :], cs[:, k, :], w[:, half * 512:(half + 1) * 512],
                                  start=k == 0, stop=k == KT - 1)
                m.then_inc(blocks_done, 1)

        def mod_columns(pe, mrow, bank):
            for n in range(KT):
                m = pe.transpose(ps[:, bank, 2 * n:2 * n + 2], mrow[:, n * P:(n + 1) * P], tab[0:2, 0:2])
            return m

        small_in = kept_sem("small_in")
        x_in = sem("x_in")
        hctx = sb("hctx", [P, KT, CTX])
        cs = sb("cs", [P, 8, 2])
        gscale = sb("gscale", [P, 3, KT])
        hand = ExitStack()
        mrow = sb("mrow", [2, D], on=hand)
        cs_ready, par_in = sem("cs_ready"), sem("par_in")
        row_kept, mod_turned, turning = sem("row_kept"), sem("mod_turned"), sem("turning")
        mod_ready = sem("mod_ready")
        with nc.Block() as block:
            @block.scalar
            def _(act):
                act.dma_start(par[:, :], params).then_inc(par_in, 16)
                act.dma_start(sml[:, :], small).then_inc(small_in, 16)
                act.dma_start(tab[:, :], table).then_inc(small_in, 16)
                act.dma_start(ab8[:, :], heads8).then_inc(small_in, 16)
                act.dma_start(res[:, :, :], xT.rearrange("(k p) t -> p k t", p=P)).then_inc(x_in, 16)
                act.dma_start(hctx[:, :, :], ctxT.rearrange("(k p) t -> p k t", p=P)).then_inc(x_in, 16)
                act.wait_ge(par_in, 16)
                act.activation(cs[:, :, :], par[:, PARAMS["cvec"]].rearrange("p (k c) -> p k c", c=2),
                               ACT.Silu).then_inc(cs_ready, 1)

            @block.sync
            def _(sp):
                load_blocks(sp, STREAM["k"].start + SLOTS)

            @block.tensor
            def _(pe):
                pe.wait_ge(cs_ready, 1)
                pe.wait_ge(small_in, 48)
                with pe.Fori(0, 2) as i:
                    pe.wait_ge(mod_ready, i + 1)
                    mod_rows(pe, 0, i, 0)
                    pe.wait_ge(row_kept, i + 1)
                    pe.sem_inc(turning, 1)
                    mod_columns(pe, mrow, 0).then_inc(mod_turned, 1)

            @block.vector
            def _(ve):
                ve.wait_ge(par_in, 16)
                ve.sem_inc(mod_ready, 1)
                with ve.Fori(0, 2) as i:
                    ve.wait_ge(blocks_done, i * SLOTS + SLOTS)
                    ve.tensor_copy(mrow[:, :].rearrange("p (a n) -> p a n", a=2), ps[0:2, 0:2, :]).then_inc(row_kept, 1)
                    ve.wait_ge(mod_turned, i + 1)
                    ve.tensor_tensor(mod[:, bass.ds(i * 8, 8), :],
                                     ps[:, 0, 0:16].rearrange("p (n c) -> p n c", c=2),
                                     par[:, bass.ds(i * 8, 8)].unsqueeze(2).to_broadcast([P, 8, 2]),
                                     ALU.add).then_inc(mod_ready, 1)
        hand.close()

        def norm(name, src, dst, gain, shift=None, n=T, also=None):
            with ExitStack() as st:
                sq = sb(name + "_sq", [P, KT, n], on=st)
                rs = sb(name + "_rs", [P, n], on=st)
                squared, summed, root, scaled = (sem(name + s) for s in ("_squared", "_summed", "_root", "_scaled"))
                with nc.Block() as block:
                    @block.scalar
                    def _(act):
                        for k in range(KT):
                            act.activation(sq[:, k, :], src[:, k, :], ACT.Square).then_inc(squared, 1)
                        act.wait_ge(root, 1)
                        act.activation(rs[:, :], rs[:, :], ACT.Sqrt).then_inc(root, 1)
                        if shift is not None:
                            for k in range(KT):
                                act.wait_ge(scaled, k + 1)
                                act.activation(dst[:, k, :], dst[:, k, :], ACT.Identity, bias=shift(k))

                    @block.tensor
                    def _(pe):
                        for k in range(KT):
                            pe.wait_ge(squared, k + 1)
                            m = pe.matmul(ps[:, 0, 0:n], ones, sq[:, k, :], start=k == 0, stop=k == KT - 1)
                        m.then_inc(summed, 1)

                    @block.vector
                    def _(ve):
                        ve.wait_ge(summed, 1)
                        ve.tensor_scalar(rs[:, :], ps[:, 0, 0:n], 1.0 / D, EPS, ALU.mult, ALU.add).then_inc(root, 1)
                        ve.wait_ge(root, 2)
                        ve.reciprocal(rs[:, :], rs[:, :]).then_inc(root, 1)
                        ve.wait_ge(root, 3)
                        ve.wait_ge(squared, KT)
                        for k in range(KT):
                            ve.scalar_tensor_tensor(dst[:, k, :], src[:, k, :], gain(k), rs[:, :],
                                                    ALU.mult, ALU.mult).then_inc(scaled, 1)
                            if also:
                                ve.scalar_tensor_tensor(also[0][:, k, :], src[:, k, :], also[1](k), rs[:, :],
                                                        ALU.mult, ALU.mult)

        gready = sem("gready")
        with nc.Block() as block:
            @block.vector
            def _(ve):
                for n, (part, c, g) in enumerate(((8, 0, "norm1"), (8, 1, "norm1"))):
                    ve.scalar_tensor_tensor(gscale[:, n, :], mod[:, part:part + 8, c], 1.0, par[:, PARAMS[g]],
                                            ALU.add, ALU.mult).then_inc(gready, 1)
                ve.wait_ge(x_in, 32)
        norm("n1", res, hn, lambda k: gscale[:, 0, k:k + 1], lambda k: mod[:, k, 0:1])
        norm("n1c", hctx, hctx, lambda k: gscale[:, 1, k:k + 1], lambda k: mod[:, k, 1:2], n=CTX)

        mixed = ctx.enter_context(ExitStack())
        mix = sb("mix", [P, KT, T], on=mixed)
        gla = ctx.enter_context(ExitStack())
        gs = mix[:, 4:8, :]
        kT = sb("kT", [P, 2, TA], on=gla)
        qT = sb("qT", [P, 2, T], on=gla)
        vtok = sb("vtok", [P, 6, 512], on=gla)
        ptok = sb("ptok", [P, TT, 4 * P], on=gla)
        aT = sb("aT", [32, TA], on=gla)
        wd = sb("wd", [32, 512], on=gla)
        wd_zero, wd_in = sem("wd_zero"), sem("wd_in")
        evac_k, evac_v, evac_n, a_sum = sem("evac_k"), sem("evac_v"), sem("evac_n"), sem("a_sum")
        BK, BV, BQ = STREAM["k"].start, STREAM["v"].start, STREAM["q"].start
        with nc.Block() as block:
            @block.sync
            def _(sp):
                load_blocks(sp, STREAM["ada2"].start + SLOTS)

            @block.gpsimd
            def _(pool):
                pool.memset(wd[:, :], 0.0).then_inc(wd_zero, 1)
                pool.wait_ge(wd_zero, 1)
                pool.dma_start(wd[0:16, 0:256], wdec[0]).then_inc(wd_in, 16)
                pool.dma_start(wd[16:32, 256:512], wdec[1]).then_inc(wd_in, 16)

            @block.tensor
            def _(pe):
                for n in range(2):
                    w = block_here(pe, BK + n)
                    for k in range(KT):
                        pe.matmul(ps[:, 2 * n, :], w[:, k * P:(k + 1) * P], hn[:, k, :], start=k == 0, stop=k == KT - 1)
                    for k in range(KT):
                        m = pe.matmul(ps[:, 2 * n + 1, 0:CTX], w[:, k * P:(k + 1) * P], hctx[:, k, :],
                                      start=k == 0, stop=k == KT - 1)
                    m.then_inc(blocks_done, 1)
                wa = sml[:, SMALL["wa"]].rearrange("p (k n) -> p k n", k=KT)
                for k in range(KT):
                    pe.matmul(ps[0:32, 6, :], wa[:, k, :], hn[:, k, :], start=k == 0, stop=k == KT - 1)
                for k in range(KT):
                    m = pe.matmul(ps[0:32, 7, 0:CTX], wa[:, k, :], hctx[:, k, :], start=k == 0, stop=k == KT - 1)
                m.then_inc(a_sum, 1)
                pe.wait_ge(evac_k, 4)
                for b in range(4):
                    w = block_here(pe, BV + b)
                    for kk in range(2):
                        k = 2 * b + kk
                        for t in range(6):
                            h = hn[:, k, t * P:(t + 1) * P] if t < 4 else hctx[:, k, (t - 4) * P:(t - 3) * P]
                            m = pe.matmul(ps[:, t, :], h, w[:, kk * 512:(kk + 1) * 512], start=k == 0, stop=k == KT - 1)
                    m.then_inc(blocks_done, 1)
                for n in range(6):
                    w = block_here(pe, BQ + n)
                    bank = (6 + n) % 8
                    if n < 2:
                        pe.wait_ge(evac_k, 5 + n)
                    else:
                        pe.wait_ge(evac_v, n - 1)
                    dense_tile(pe, w, hn, ps[:, bank, :])
                pe.wait_ge(evac_v, 6)
                pe.wait_ge(evac_n, 2)
                for b in range(4):
                    w = block_here(pe, BQ + 6 + b)
                    for kk in range(2):
                        k = 2 * b + kk
                        for t in range(TT):
                            m = pe.matmul(ps[:, 4 + t, :], hn[:, k, t * P:(t + 1) * P], w[:, kk * 512:(kk + 1) * 512],
                                          start=k == 0, stop=k == KT - 1)
                    m.then_inc(blocks_done, 1)

            @block.scalar
            def _(act):
                for n in range(2):
                    act.wait_ge(blocks_done, BK + n + 1)
                    act.activation(kT[:, n, 0:T], ps[:, 2 * n, :], ACT.Copy).then_inc(evac_k, 1)
                    act.activation(kT[:, n, T:TA], ps[:, 2 * n + 1, 0:CTX], ACT.Copy).then_inc(evac_k, 1)
                act.wait_ge(a_sum, 1)
                act.activation(aT[:, 0:T], ps[0:32, 6, :], ACT.Copy).then_inc(evac_k, 1)
                act.activation(aT[:, T:TA], ps[0:32, 7, 0:CTX], ACT.Copy).then_inc(evac_k, 1)
                act.wait_ge(blocks_done, BV + 4)
                for t in range(6):
                    act.activation(vtok[:, t, :], ps[:, t, :], ACT.Copy).then_inc(evac_v, 1)
                for n in range(6):
                    act.wait_ge(blocks_done, BQ + n + 1)
                    out = qT[:, n, :] if n < 2 else gs[:, n - 2, :]
                    act.activation(out, ps[:, (6 + n) % 8, :], ACT.Silu if 2 <= n < 6 else ACT.Copy,
                                   scale=0.125 if n < 2 else 1.0).then_inc(evac_n, 1)
                act.wait_ge(blocks_done, BQ + 10)
                for t in range(TT):
                    act.activation(ptok[:, t, :], ps[:, 4 + t, :], ACT.Copy).then_inc(evac_n, 1)

        st = gla.enter_context(ExitStack())
        qbm = hn[:, :, :].rearrange("p (a b) t -> p a b t", b=2)
        kb = hctx[:, :, :].rearrange("p (a b) t -> p a (b t)", b=2)
        tot = sb("tot", [P, 4, 12], on=gla)
        SS = sb("SS", [P, 4, 12, P], on=gla)
        kstT = sb("kstT", [P, 2, 4, 2, P], on=gla)
        kst = sb("kst", [P, 4, TA], on=st)
        cum = sb("cum", [P, TA], on=st)
        la = sb("la", [P, TA], on=st)
        lg = sb("lg", [P, TA], on=st)
        bb = sb("bb", [P, TA], on=st)
        dl = mix[:, 2:4, :].rearrange("p a t -> p (a t)")[:, 0:TA]
        e1, e2 = mix[:, 0, :], mix[:, 1, :]
        mrow = [kstT[0:2, u, :, :, :].rearrange("p a b c -> p (a b c)") for u in range(2)]
        row_kept, mod_turned, mod_ready = (sem(n + "2") for n in ("row_kept", "mod_turned", "mod_ready"))
        A2 = STREAM["ada2"].start
        z_sum, z_log, z_dve, z_exp, z_zero = sem("z_sum"), sem("z_log"), sem("z_dve"), sem("z_exp"), sem("z_zero")
        with nc.Block() as block:
            @block.gpsimd
            def _(pool):
                pool.memset(qbm[:, :, :, :], 0.0).then_inc(z_zero, 1)
                pool.memset(SS[:, :, 0, :], 0.0).then_inc(z_zero, 1)
                pool.wait_ge(mod_turned, 4)
                pool.memset(kstT[:, :, :, :, :], 0.0)

            @block.sync
            def _(sp):
                load_blocks(sp, STREAM["out"].start + SLOTS)

            @block.tensor
            def _(pe):
                pe.wait_ge(wd_in, 32)
                def decays(dp):
                    bank = 2 * (dp % 2)
                    if dp >= 2:
                        pe.wait_ge(z_dve, 11 * (dp - 2) + 2)
                        pe.wait_ge(z_log, 4 * (dp - 2) + 2)
                    pe.matmul(ps[:, bank, :], wd[:, dp * P:(dp + 1) * P], aT[:, 0:T], start=True, stop=True)
                    pe.matmul(ps[:, bank + 1, 0:CTX], wd[:, dp * P:(dp + 1) * P], aT[:, T:TA],
                              start=True, stop=True).then_inc(z_sum, 1)
                decays(0)
                decays(1)
                for t in range(4):
                    if t:
                        pe.wait_ge(row_kept, t)
                    mod_rows(pe, A2 + t * SLOTS, 0, 6)
                    pe.wait_ge(row_kept, t + 1)
                    if t >= 2:
                        pe.wait_ge(mod_ready, t - 1)
                    mod_columns(pe, mrow[t % 2], 4 + t % 2).then_inc(mod_turned, 1)
                    if t < 2:
                        decays(2 + t)

            @block.scalar
            def _(act):
                n = [0]

                def step(ins):
                    n[0] += 1
                    ins.then_inc(z_log, 1)
                    act.wait_ge(z_log, n[0])
                for dp in range(4):
                    bias = col("bdec", dp)
                    act.wait_ge(z_dve, 11 * dp + 2)
                    act.activation(lg[:, 0:T], ps[:, 2 * (dp % 2), :], ACT.Abs, bias=bias).then_inc(z_log, 1)
                    n[0] += 1
                    step(act.activation(lg[:, T:TA], ps[:, 2 * (dp % 2) + 1, 0:CTX], ACT.Abs, bias=bias))
                    step(act.activation(lg[:, :], lg[:, :], ACT.Exp, scale=-1.0))
                    step(act.activation(lg[:, :], lg[:, :], ACT.Ln, bias=1.0))
                    act.wait_ge(z_dve, 11 * dp + 7)
                    act.activation(e1, bb[:, 0:T], ACT.Exp, scale=1.0 / 16).then_inc(z_exp, 1)
                    act.activation(e2, bb[:, 0:T], ACT.Exp, scale=-1.0 / 16).then_inc(z_exp, 1)
                    act.activation(lg[:, :], dl, ACT.Exp, scale=1.0 / 16).then_inc(z_exp, 1)
                    act.activation(tot[:, dp, :], tot[:, dp, :], ACT.Exp, scale=1.0 / 16).then_inc(z_exp, 1)
                    act.wait_ge(blocks_done, A2 + (dp + 1) * SLOTS)
                    if dp >= 2:
                        act.wait_ge(mod_turned, dp - 1)
                    act.activation(mrow[dp % 2].rearrange("p (a n) -> p a n", a=2), ps[0:2, 6:8, :], ACT.Copy
                                   ).then_inc(row_kept, 1)

            @block.vector
            def _(ve):
                n = [0]

                def step(ins):
                    n[0] += 1
                    ins.then_inc(z_dve, 1)
                    ve.wait_ge(z_dve, n[0])
                ve.wait_ge(z_zero, 2)
                for dp in range(4):
                    pair, back = dp % 2, dp // 2
                    bias = col("bdec", dp)
                    ve.wait_ge(z_sum, dp + 1)
                    step(ve.tensor_scalar(la[:, 0:T], ps[:, 2 * (dp % 2), :], bias, 0.0, ALU.add, ALU.min))
                    step(ve.tensor_scalar(la[:, T:TA], ps[:, 2 * (dp % 2) + 1, 0:CTX], bias, 0.0, ALU.add, ALU.min))
                    ve.wait_ge(z_log, 4 * dp + 4)
                    step(ve.tensor_tensor(la[:, :], la[:, :], lg[:, :], ALU.subtract))
                    step(ve.tensor_tensor_scan(cum[:, :], tab[:, TABLES["resetg"]], la[:, :], 0.0, ALU.mult, ALU.add))
                    chunks = [x.rearrange("p (c j) -> p c j", j=64) for x in (cum[:, :], bb[:, :], dl)]
                    t3 = tot[:, dp, :].unsqueeze(2).to_broadcast([P, 12, 64])
                    step(ve.tensor_copy(tot[:, dp, :].unsqueeze(2), chunks[0][:, :, 63:64]))
                    if back:
                        step(ve.tensor_tensor(dl, cum[:, :], la[:, :], ALU.subtract))
                        step(ve.tensor_tensor(chunks[1], t3, chunks[2], ALU.subtract))
                    else:
                        step(ve.tensor_copy(bb[:, :], cum[:, :]))
                        step(ve.tensor_tensor(chunks[2], t3, chunks[1], ALU.subtract))
                    ve.wait_ge(z_exp, 4 * dp + 4)
                    for h in range(2):
                        r = slice(64 * h, 64 * h + 64)
                        step(ve.tensor_tensor(qbm[r, dp, h, :], qT[r, pair, :], e1[r, :], ALU.mult))
                    step(ve.tensor_tensor(kb[:, dp, :], kT[:, pair, 0:T], e2, ALU.mult))
                    step(ve.tensor_tensor(kst[:, dp, :], kT[:, pair, :], lg[:, :], ALU.mult))
                    for t in ([], [0], [1], [2, 3])[dp]:
                        ve.wait_ge(mod_turned, t + 1)
                        ve.tensor_tensor(mod[:, 16 + 8 * t:24 + 8 * t, :],
                                         ps[:, 4 + t % 2, 0:16].rearrange("p (n c) -> p n c", c=2),
                                         par[:, 16 + 8 * t:24 + 8 * t].unsqueeze(2).to_broadcast([P, 8, 2]),
                                         ALU.add).then_inc(mod_ready, 1)

        def chunk_of(d, s):
            return (8 + s if s < 4 else s - 4) if d == 0 else (11 - s if s < 4 else 11 - s)
        tr_done, tr_copied, ds_done, ds_used = sem("tr_done"), sem("tr_copied"), sem("ds_done"), sem("ds_used")
        STEPS = 11
        with nc.Block() as block:
            @block.tensor
            def _(pe):
                for s in range(STEPS):
                    u = s % 2
                    if s >= 2:
                        pe.wait_ge(tr_copied, 2 * (s - 1))
                    for dp in range(4):
                        c = chunk_of(dp // 2, s)
                        tile = c // 2
                        m = pe.transpose(ps[:, u, dp * P:(dp + 1) * P], kst[:, dp, tile * P:(tile + 1) * P], ident)
                    m.then_inc(tr_done, 1)
                    pe.wait_ge(tr_copied, 2 * (s + 1))
                    for pair in range(2):
                        if s >= 2:
                            pe.wait_ge(ds_used, 8 * (s - 2) + 4 * pair + 4)
                        for d in range(2):
                            c = chunk_of(d, s)
                            m = pe.matmul(ps[:, 2 + u + 2 * pair, d * 256:d * 256 + 256],
                                          kstT[:, u, 2 * d + pair, c % 2, :],
                                          vtok[:, c // 2, pair * 256:pair * 256 + 256], start=True, stop=True)
                        m.then_inc(ds_done, 1)

            @block.scalar
            def _(act):
                for s in range(STEPS):
                    act.wait_ge(tr_done, s + 1)
                    if s >= 2:
                        act.wait_ge(ds_done, 2 * (s - 1))
                    for d in range(2):
                        half = chunk_of(d, s) % 2
                        r = slice(64 * half, 64 * half + 64)
                        act.activation(kstT[r, s % 2, 2 * d:2 * d + 2, half, :],
                                       ps[r, s % 2, 256 * d:256 * d + 256].rearrange("p (a n) -> p a n", a=2),
                                       ACT.Copy).then_inc(tr_copied, 1)

            @block.vector
            def _(ve):
                for s in range(STEPS):
                    for pair in range(2):
                        ve.wait_ge(ds_done, 2 * s + pair + 1)
                        if s:
                            ve.wait_ge(ds_used, 8 * (s - 1) + 4 * pair + 4)
                        for d in range(2):
                            dp = 2 * d + pair
                            c = chunk_of(d, s)
                            for h in range(2):
                                r = slice(64 * h, 64 * h + 64)
                                o = d * 256 + h * P
                                ve.scalar_tensor_tensor(SS[r, dp, s + 1, :], SS[r, dp, s, :], tot[r, dp, c:c + 1],
                                                        ps[r, 2 + s % 2 + 2 * pair, o:o + P],
                                                        ALU.mult, ALU.add).then_inc(ds_used, 1)
        st.close()

        sc = sb("sc", [P, 2, 2, 512], on=gla)
        masks = sb("masks", [P, 2, P], U8, on=gla)
        oT = sb("oT", [P, 4, T], on=gla)
        win = sb("win", list(windows.shape), on=gla)
        win_in = sem("win_in")
        sc_zero, sc_done, sc_kept, o_done, o_kept = (sem(n) for n in ("sc_zero", "sc_done", "sc_kept", "o_done", "o_kept"))
        with nc.Block() as block:
            @block.sync
            def _(sp):
                sp.dma_start(win[:, :], windows).then_inc(win_in, 16)
                sp.wait_ge(win_in, 16)

            @block.gpsimd
            def _(pool):
                pool.memset(sc[:, :, :, :], 0.0).then_inc(sc_zero, 1)

            @block.tensor
            def _(pe):
                for t in range(TT):
                    cols = slice(t * P, (t + 1) * P)
                    for d in range(2):
                        if t >= 2:
                            pe.wait_ge(sc_kept, 2 * (t - 2) + d + 1)
                        for h in range(4):
                            dp = 2 * d + h // 2
                            m = pe.matmul(ps[:, 2 * (t % 2) + d, h * P:(h + 1) * P], kb[:, dp, cols],
                                          qbm[:, dp, h % 2, cols], start=True, stop=True)
                        m.then_inc(sc_done, 1)
                    pe.wait_ge(sc_kept, 2 * t + 2)
                    if t >= 2:
                        pe.wait_ge(o_kept, t - 1)
                    for h in range(4):
                        out = ps[:, 4 + t % 2, h * P:(h + 1) * P]
                        pe.matmul(out, vtok[:, t, h * P:(h + 1) * P], sc[:, t % 2, 0, h * P:(h + 1) * P],
                                  start=True, stop=False)
                        for d in range(2):
                            dp = 2 * d + h // 2
                            for cc in range(2):
                                c = 2 * t + cc
                                s = 4 + c if d == 0 else 11 - c
                                pe.matmul(out[:, 64 * cc:64 * cc + 64], SS[:, dp, s, :],
                                          qbm[:, dp, h % 2, c * 64:(c + 1) * 64], start=False, stop=False,
                                          skip_group_check=True)
                        m = pe.matmul(out, vtok[:, t, h * P:(h + 1) * P], sc[:, t % 2, 1, h * P:(h + 1) * P],
                                      start=False, stop=True)
                    m.then_inc(o_done, 1)

            @block.vector
            def _(ve):
                ve.tensor_copy(masks[:, 0, :], tab[:, TABLES["glaf"]]).then_inc(sc_zero, 1)
                ve.tensor_copy(masks[:, 1, :], tab[:, TABLES["glab"]]).then_inc(sc_zero, 1)
                ve.wait_ge(sc_zero, 3)
                for t in range(TT):
                    if t >= 2:
                        ve.wait_ge(o_done, t - 1)
                    for d in range(2):
                        ve.wait_ge(sc_done, 2 * t + d + 1)
                        ve.copy_predicated(sc[:, t % 2, d, :].rearrange("p (h i) -> p h i", h=4),
                                           masks[:, d, :].unsqueeze(1).to_broadcast([P, 4, P]),
                                           ps[:, 2 * (t % 2) + d, :].rearrange("p (h i) -> p h i", h=4)
                                           ).then_inc(sc_kept, 1)

            @block.scalar
            def _(act):
                for t in range(TT):
                    act.wait_ge(o_done, t + 1)
                    act.activation(oT[:, :, t * P:(t + 1) * P],
                                   ps[:, 4 + t % 2, :].rearrange("p (h i) -> p h i", h=4), ACT.Copy).then_inc(o_kept, 1)

        sq, rs = hn[:, 0:4, :], hn[:, 4:8, :]
        pT = SS[:, :, :, :].rearrange("p a b c -> p (a b c)")[:, 0:4 * T].rearrange("p (g t) -> p g t", g=4)
        block_at = window_blocks()[1]
        o_ms, o_pow = sem("o_ms"), sem("o_pow")
        o_sq, o_sum, o_root, o_mix = sem("o_sq"), sem("o_sum"), sem("o_root"), sem("o_mix")
        win_sum, scaled, pooled, pool_mm, pool_out = (
            sem(n) for n in ("win_sum", "win_scaled", "pooled", "pool_mm", "pool_out"))
        with nc.Block() as block:
            @block.scalar
            def _(act):
                for h in range(4):
                    act.activation(sq[:, h, :], oT[:, h, :], ACT.Square).then_inc(o_sq, 1)
                for h in range(4):
                    act.wait_ge(o_ms, h + 1)
                    act.activation(rs[:, h, :], rs[:, h, :], ACT.Sqrt).then_inc(o_pow, 1)

            @block.tensor
            def _(pe):
                for h in range(4):
                    pe.wait_ge(o_sq, h + 1)
                    pe.matmul(ps[:, h, :], ones, sq[:, h, :], start=True, stop=True).then_inc(o_sum, 1)
                wp = sml[:, SMALL["pool"]].rearrange("p (g n) -> p g n", g=4)

                def mixed_channels(g):
                    pe.wait_ge(pooled, g + 1)
                    pe.wait_ge(o_ms, g + 1)
                    pe.matmul(ps[:, g, :], wp[:, g, :], pT[:, g, :], start=True, stop=True).then_inc(pool_mm, 1)
                for g in range(4):
                    sums, own = ps[:, 4 + 2 * (g % 2), :], ps[:, 5 + 2 * (g % 2), :]
                    if g >= 2:
                        pe.wait_ge(pooled, g - 1)
                    for t in range(TT):
                        out = slice(t * P, (t + 1) * P)
                        near = [b for b in range(TT) if (g, b - t) in block_at]
                        for b in near:
                            n = block_at[g, b - t]
                            pe.matmul(sums[:, out], ptok[:, b, g * P:(g + 1) * P], win[:, n * P:(n + 1) * P],
                                      start=b == near[0], stop=b == near[-1])
                        m = pe.transpose(own[:, out], ptok[:, t, g * P:(g + 1) * P], ident)
                    m.then_inc(win_sum, 1)
                    if g:
                        mixed_channels(g - 1)
                mixed_channels(3)

            @block.vector
            def _(ve):
                ve.scalar_tensor_tensor(gscale[:, 2, :], mod[:, 32:40, 0], 1.0, par[:, PARAMS["norm2"]],
                                        ALU.add, ALU.mult)
                n = [0]

                def step(ins):
                    n[0] += 1
                    ins.then_inc(o_root, 1)
                    ve.wait_ge(o_root, n[0])
                for h in range(4):
                    ve.wait_ge(o_sum, h + 1)
                    ve.tensor_scalar(rs[:, h, :], ps[:, h, :], 1.0 / P, EPS, ALU.mult, ALU.add).then_inc(o_ms, 1)
                for h in range(4):
                    ve.wait_ge(o_pow, h + 1)
                    step(ve.reciprocal(rs[:, h, :], rs[:, h, :]))
                    step(ve.scalar_tensor_tensor(rs[:, h, :], oT[:, h, :], col("gla"), rs[:, h, :], ALU.mult, ALU.mult))
                    ve.tensor_tensor(mix[:, h, :], rs[:, h, :], gs[:, h, :], ALU.mult).then_inc(o_mix, 1)
                    g = h
                    ve.wait_ge(win_sum, g + 1)
                    ve.tensor_tensor(pT[:, g, :], ps[:, 4 + 2 * (g % 2), :],
                                     tab[:, TABLES["rcount"]].rearrange("p (g t) -> p g t", g=4)[:, g], ALU.mult
                                     ).then_inc(scaled, 1)
                    ve.wait_ge(scaled, g + 1)
                    ve.tensor_tensor(pT[:, g, :], pT[:, g, :], ps[:, 5 + 2 * (g % 2), :], ALU.subtract
                                     ).then_inc(pooled, 1)
                ve.wait_ge(o_mix, 4)
                for g in range(4):
                    ve.wait_ge(pool_mm, g + 1)
                    ve.tensor_scalar(mix[:, 4 + g, :], ps[:, g, :], col("pscale", g), None, ALU.mult).then_inc(pool_out, 1)
        gla.close()

        def three(pe, out, w_hi, w_lo, a_hi, a_lo, start, stop):
            pe.matmul(out, w_hi, a_hi, start=start, stop=False)
            pe.matmul(out, w_lo, a_hi, start=False, stop=False)
            return pe.matmul(out, w_hi, a_lo, start=False, stop=stop)

        def fast_project_out(name, act_in, first_block, gate, next_block, meanwhile=None):
            with ExitStack() as st:
                w_hi, w_lo = (sb(f"{name}_w{n}", [P, 2, 1024], F32R, on=st) for n in ("hi", "lo"))
                a_hi, a_lo = (sb(f"{name}_a{n}", [P, KT, T], F32R, on=st) for n in ("hi", "lo"))
                a_rounded, a_split, w_rounded, used, added = (
                    sem(f"{name}_{n}") for n in ("a_rounded", "a_split", "w_rounded", "used", "added"))
                with nc.Block() as block:
                    if meanwhile:
                        block.gpsimd(meanwhile)

                    @block.sync
                    def _(sp):
                        load_blocks(sp, next_block)

                    @block.tensor
                    def _(pe):
                        for n in range(KT):
                            pe.wait_ge(blocks_done, first_block + n + 1)
                            for k in range(KT):
                                c = slice(k * P, (k + 1) * P)
                                if n == 0:
                                    pe.wait_ge(a_split, k + 1)
                                m = three(pe, ps[:, n, :], w_hi[:, n % 2, c], w_lo[:, n % 2, c],
                                          a_hi[:, k, :], a_lo[:, k, :], k == 0, k == KT - 1)
                            m.then_inc(used, 1)

                    @block.scalar
                    def _(act):
                        def round_block(n):
                            b = first_block + n
                            act.wait_ge(block_in[b % SLOTS], 16 * (b // SLOTS + 1))
                            if n >= 2:
                                act.wait_ge(used, n - 1)
                            act.activation(w_hi[:, n % 2, :], ring[:, b % SLOTS, :], ACT.Copy).then_inc(w_rounded, 1)
                        round_block(0)
                        for k in range(KT):
                            act.activation(a_hi[:, k, :], act_in[:, k, :], ACT.Copy).then_inc(a_rounded, 1)
                        for n in range(1, KT):
                            round_block(n)

                    @block.vector
                    def _(ve):
                        def rest_of_block(n):
                            ve.wait_ge(w_rounded, n + 1)
                            ve.tensor_tensor(w_lo[:, n % 2, :], ring[:, (first_block + n) % SLOTS, :],
                                             w_hi[:, n % 2, :].bitcast(F32), ALU.subtract).then_inc(blocks_done, 1)
                        rest_of_block(0)
                        for k in range(KT):
                            ve.wait_ge(a_rounded, k + 1)
                            ve.tensor_tensor(a_lo[:, k, :], act_in[:, k, :], a_hi[:, k, :].bitcast(F32), ALU.subtract
                                             ).then_inc(a_split, 1)
                        rest_of_block(1)
                        for n in range(KT):
                            if n + 2 < KT:
                                rest_of_block(n + 2)
                            ve.wait_ge(used, n + 1)
                            if gate is None:
                                ve.tensor_tensor(res[:, n, :], ps[:, n, :], res[:, n, :], ALU.add).then_inc(added, 1)
                            else:
                                ve.scalar_tensor_tensor(res[:, n, :], ps[:, n, :], gate(n), res[:, n, :],
                                                        ALU.mult, ALU.add).then_inc(added, 1)

        def project_out(name, act_in, first_block, gate, next_block):
            added = sem(name + "_added")
            with nc.Block() as block:
                @block.sync
                def _(sp):
                    load_blocks(sp, next_block)

                @block.tensor
                def _(pe):
                    for n in range(KT):
                        dense_tile(pe, block_here(pe, first_block + n), act_in, ps[:, n, :])

                @block.vector
                def _(ve):
                    for n in range(KT):
                        ve.wait_ge(blocks_done, first_block + n + 1)
                        if gate is None:
                            ve.tensor_tensor(res[:, n, :], ps[:, n, :], res[:, n, :], ALU.add).then_inc(added, 1)
                        else:
                            ve.scalar_tensor_tensor(res[:, n, :], ps[:, n, :], gate(n), res[:, n, :],
                                                    ALU.mult, ALU.add).then_inc(added, 1)

        zeroed = ExitStack()
        zeros = sb("zeros", [P, D], on=zeroed)
        zero_set, y_cleared = sem("zero_set"), sem("y_cleared")

        def clear_results(pool):
            pool.memset(zeros[:, :], 0.0).then_inc(zero_set, 1)
            pool.wait_ge(zero_set, 1)
            pool.dma_start(y_dram[MINTILES * P:, :].rearrange("(n p) d -> p n d", p=P),
                           zeros[:, :].unsqueeze(1).to_broadcast([P, MAXTILES - MINTILES, D])).then_inc(y_cleared, 16)
        fast_project_out("mixout", mix, STREAM["out"].start, lambda n: mod[:, 16 + n, 0:1], STREAM["gdn"].start + SLOTS,
                    clear_results)
        norm("n2", res, hn, lambda k: gscale[:, 2, k:k + 1], lambda k: mod[:, 24 + k, 0:1])
        with nc.Block() as block:
            @block.gpsimd
            def _(pool):
                pool.wait_ge(y_cleared, 16)
        zeroed.close()

        retire()
        moe = ctx.enter_context(ExitStack())
        htok = mix[:, :, :].rearrange("p (t h) n -> p t (h n)", h=2)
        h_tr, h_kept = sem("h_tr"), [sem("h_kept_act"), sem("h_kept_dve")]
        with nc.Block() as block:
            @block.tensor
            def _(pe):
                for n in range(8):
                    t, half = n // 2, n % 2
                    for k in range(4):
                        m = pe.transpose(ps[:, n, k * P:(k + 1) * P], hn[:, 4 * half + k, t * P:(t + 1) * P], ident)
                    m.then_inc(h_tr, 1)

            @block.scalar
            def _(act):
                for n in range(0, 8, 2):
                    act.wait_ge(h_tr, n + 1)
                    act.activation(mix[:, n, :], ps[:, n, :], ACT.Copy).then_inc(h_kept[0], 1)

            @block.vector
            def _(ve):
                for n in range(1, 8, 2):
                    ve.wait_ge(h_tr, n + 1)
                    ve.tensor_copy(mix[:, n, :], ps[:, n, :]).then_inc(h_kept[1], 1)

            @block.sync
            def _(sp):
                for t in range(TT):
                    sp.wait_ge(h_kept[0], t + 1)
                    sp.wait_ge(h_kept[1], t + 1)
                    sp.dma_start(h2_dram[t * P:(t + 1) * P, :], htok[:, t, :]).then_inc(h_stored, 16)

        I32 = mybir.dt.int32
        w_up, w_down = sb("w_up", [P, 2, KT * 512], on=moe), sb("w_down", [P, 2, 2 * D], on=moe)
        lgt = sb("lgt", [P, TT, 36], on=moe)
        gt_ = sb("gt_", [P, 8, TT, 8], on=moe)
        prod = sb("prod", [P, 3, TT, 4, 8], on=moe)
        one = sb("one", [P, 8, TT, 1], on=moe)
        ex_ = sb("ex_", [P, 4, NEXP], on=moe)
        cmp_ = sb("cmp_", [1, MAXTILES, NEXP], on=moe)
        meta_f = sb("meta_f", [1, MAXTILES + 1], on=moe)
        meta = sb("meta", [1, MAXTILES + 1], I32, on=moe)
        slot_f = sb("slot_f", [P, 2, TT, 1], on=moe)
        slot_i = sb("slot_i", [P, 2, TT], I32, on=moe)
        tok_f = sb("tok_f", [MAXTILES, P], on=moe)
        tok_i = sb("tok_i", [P, MAXTILES], I32, on=moe)
        logits_done, r_step, r_exp, ranked = sem("logits_done"), sem("r_step"), sem("r_exp"), sem("ranked")
        slots_ready, tok_zero, tok_filled, tok_sent, tok_back, tok_tr, tok_ready = (
            sem(n) for n in ("slots_ready", "tok_zero", "tok_filled", "tok_sent", "tok_back", "tok_tr", "tok_ready"))
        onehot_ready = sem("onehot_ready")
        with nc.Block() as block:
            @block.tensor
            def _(pe):
                wr = sml[:, SMALL["router"]].rearrange("p (k n) -> p k n", k=KT)
                for t in range(TT):
                    for k in range(KT):
                        m = pe.matmul(ps[:, 0, t * 36:(t + 1) * 36], hn[:, k, t * P:(t + 1) * P], wr[:, k, :],
                                      start=k == 0, stop=k == KT - 1)
                m.then_inc(logits_done, 1)
                pe.wait_ge(onehot_ready, 1)
                chosen = prod[:, 2].rearrange("p t g e -> p t (g e)")
                for t in range(TT):
                    for b in range(t + 1):
                        pe.matmul(ps[:, 1, t * NEXP:(t + 1) * NEXP], tab[:, TABLES["strict"]] if b == t else ones,
                                  chosen[:, b, :], start=b == 0, stop=b == t)
                for t in range(TT):
                    m = pe.matmul(ps[:, 2, 0:NEXP], ones, chosen[:, t, :], start=t == 0, stop=t == TT - 1)
                m.then_inc(ranked, 1)
                pe.wait_ge(tok_back, 16)
                pe.transpose(ps[:, 3, 0:MAXTILES], tok_f[:, :], tab[0:MAXTILES, 0:MAXTILES]).then_inc(tok_tr, 1)

            @block.scalar
            def _(act):
                act.wait_ge(r_step, 3)
                act.activation(gt_[:, 1, :, 0:4], gt_[:, 0, :, 0:4], ACT.Exp).then_inc(r_exp, 1)
                act.wait_ge(r_step, 20)
                act.activation(one[:, 5], one[:, 4], ACT.Exp).then_inc(r_exp, 1)

            @block.gpsimd
            def _(pool):
                pool.memset(tok_f[:, :], 0.0).then_inc(tok_zero, 1)
                pool.wait_ge(tok_zero, 1)
                pool.dma_start(tok_dram.rearrange("(n p) a -> n (p a)", p=P), tok_f[:, :]).then_inc(tok_filled, 16)
                pool.wait_ge(tok_filled, 16)
                pool.wait_ge(slots_ready, 1)
                for n in range(2):
                    for t in range(TT):
                        pool.indirect_dma_start(
                            out=tok_dram, out_offset=bass.IndirectOffsetOnAxis(ap=slot_i[:, n, t:t + 1], axis=0),
                            in_=tab[:, TABLES.at["token"][0] + t:TABLES.at["token"][0] + t + 1], in_offset=None
                        ).then_inc(tok_sent, 16)
                pool.wait_ge(tok_sent, 2 * TT * 16)
                pool.dma_start(tok_f[:, :], tok_dram.rearrange("(n p) a -> n (p a)", p=P)).then_inc(tok_back, 16)

            @block.vector
            def _(ve):
                n = [0]

                def step(ins):
                    n[0] += 1
                    ins.then_inc(r_step, 1)
                    ve.wait_ge(r_step, n[0])

                def wide(x, width):
                    return x.to_broadcast([P, TT, width])
                rank = tab[:, TABLES["rank"]].unsqueeze(1)

                def first_of(eq, width, top, hot):
                    step(ve.tensor_tensor(hot, eq, rank[:, :, 0:width].to_broadcast([P, TT, width]), ALU.mult))
                    step(ve.tensor_reduce(top, hot, AX.X, ALU.max))
                    step(ve.tensor_tensor(hot, hot, wide(top, width), ALU.is_equal))
                ve.wait_ge(logits_done, 1)
                step(ve.tensor_copy(lgt[:, :, :], ps[:, 0, 0:144].rearrange("p (t n) -> p t n", t=TT)))
                group = lgt[:, :, 0:4]
                step(ve.tensor_reduce(one[:, 0], group, AX.X, ALU.max))
                step(ve.tensor_tensor(gt_[:, 0, :, 0:4], group, wide(one[:, 0], 4), ALU.subtract))
                ve.wait_ge(r_exp, 1)
                step(ve.tensor_reduce(one[:, 1], gt_[:, 1, :, 0:4], AX.X, ALU.add))
                step(ve.reciprocal(one[:, 1], one[:, 1]))
                step(ve.tensor_tensor(gt_[:, 2, :, 0:4], group, wide(one[:, 0], 4), ALU.is_equal))
                first_of(gt_[:, 2, :, 0:4], 4, one[:, 2], gt_[:, 3, :, 0:4])
                hot_g = gt_[:, 3, :, 0:4].unsqueeze(3).to_broadcast([P, TT, 4, 8])
                step(ve.tensor_tensor(prod[:, 0], lgt[:, :, 4:36].rearrange("p t (g e) -> p t g e", g=4),
                                      hot_g, ALU.mult))
                le, eq, h1, h2, rest = (gt_[:, n, :, :] for n in (4, 5, 6, 7, 0))
                step(ve.tensor_reduce(le.unsqueeze(3), prod[:, 0].rearrange("p t g e -> p t e g"), AX.X, ALU.add))
                step(ve.tensor_reduce(one[:, 2], le, AX.X, ALU.max))
                step(ve.tensor_tensor(eq, le, wide(one[:, 2], 8), ALU.is_equal))
                first_of(eq, 8, one[:, 3], h1)
                step(ve.scalar_tensor_tensor(rest, h1, MASKED_LOW, le, ALU.mult, ALU.add))
                step(ve.tensor_reduce(one[:, 3], rest, AX.X, ALU.max))
                step(ve.tensor_tensor(eq, rest, wide(one[:, 3], 8), ALU.is_equal))
                step(ve.tensor_tensor(one[:, 4], one[:, 3], one[:, 2], ALU.subtract))
                first_of(eq, 8, one[:, 7], h2)
                step(ve.tensor_tensor(prod[:, 0], hot_g, h1.unsqueeze(2).to_broadcast([P, TT, 4, 8]), ALU.mult))
                step(ve.tensor_tensor(prod[:, 1], hot_g, h2.unsqueeze(2).to_broadcast([P, TT, 4, 8]), ALU.mult))
                ve.tensor_tensor(prod[:, 2], prod[:, 0], prod[:, 1], ALU.add).then_inc(onehot_ready, 1)
                step(ve.memset(one[:, 6], 1.0))
                ve.wait_ge(r_exp, 2)
                step(ve.tensor_tensor(one[:, 6], one[:, 5], one[:, 6], ALU.add))
                step(ve.reciprocal(one[:, 6], one[:, 6]))
                step(ve.tensor_tensor(one[:, 6], one[:, 6], one[:, 1], ALU.mult))
                step(ve.tensor_tensor(one[:, 5], one[:, 5], one[:, 6], ALU.mult))
                ve.wait_ge(ranked, 1)
                count, ntile, upto_, first = (ex_[:, n, :] for n in range(4))
                step(ve.tensor_copy(count, ps[:, 2, 0:NEXP]))
                step(ve.tensor_scalar(ntile, count, 0.5, None, ALU.is_gt))
                for m in range(1, TT):
                    step(ve.scalar_tensor_tensor(ntile, count, m * P + 0.5, ntile, ALU.is_gt, ALU.add))
                step(ve.tensor_tensor_scan(upto_, ones[:, 0:NEXP], ntile, 0.0, ALU.mult, ALU.add))
                step(ve.tensor_tensor(first, upto_, ntile, ALU.subtract))
                step(ve.tensor_scalar(first, first, float(P), None, ALU.mult))
                slot = gt_[:, 0:4].rearrange("p a t e -> p (a t e)").rearrange("p (t e) -> p t e", t=TT)
                step(ve.tensor_tensor(slot, ps[:, 1, 0:TT * NEXP].rearrange("p (t e) -> p t e", t=TT),
                                      first.unsqueeze(1).to_broadcast([P, TT, NEXP]), ALU.add))
                for a in range(2):
                    picked = prod[:, a].rearrange("p t g e -> p t (g e)")
                    step(ve.tensor_tensor(picked, picked, slot, ALU.mult))
                    step(ve.tensor_reduce(slot_f[:, a], picked, AX.X, ALU.add))
                ve.tensor_copy(slot_i[:, :, :], slot_f[:, :, :, :].rearrange("p a t o -> p a (t o)")).then_inc(slots_ready, 1)
                number = tab[0:1, TABLES["tile"]]
                step(ve.tensor_tensor(cmp_[:, :, :], number.unsqueeze(2).to_broadcast([1, MAXTILES, NEXP]),
                                      ex_[0:1, 2, :].unsqueeze(1).to_broadcast([1, MAXTILES, NEXP]), ALU.is_ge))
                step(ve.tensor_reduce(meta_f[:, 0:MAXTILES].unsqueeze(2), cmp_[:, :, :], AX.X, ALU.add))
                step(ve.tensor_scalar(meta_f[:, 0:MAXTILES], meta_f[:, 0:MAXTILES], NEXP - 1.0, None, ALU.min))
                even = number.rearrange("p (a b) -> p a b", b=2)[:, :, 0]
                step(ve.tensor_scalar(cmp_[:, 0, 0:MAXTILES // 2], even, ex_[0:1, 2, NEXP - 1:NEXP], None, ALU.is_lt))
                step(ve.tensor_reduce(meta_f[:, MAXTILES:], cmp_[:, 0, 0:MAXTILES // 2], AX.X, ALU.add))
                step(ve.tensor_copy(meta[:, :], meta_f[:, :]))
                ve.wait_ge(tok_tr, 1)
                ve.tensor_copy(tok_i[:, :], ps[:, 3, 0:MAXTILES]).then_inc(tok_ready, 1)
                ve.wait_ge(tok_ready, 1)

        hg = sb("hg", [P, 2, D], on=moe)
        hgT = sb("hgT", [P, 2, KT, P], on=moe)
        sg = sb("sg", [P, 2, 256], on=moe)
        hid = sb("hid", [P, 2, 256], on=moe)
        hidT = sb("hidT", [P, 2, 2, P], on=moe)
        ytile = sb("ytile", [P, 2, D], on=moe)
        idx = sb("idx", [P, 2, 1], I32, on=moe)
        names = ("up_in", "down_in", "idx_set", "gathered", "turned", "copied_a", "copied_b", "up_done", "gate", "hid_done", "hid_tr",
                 "hid_copied", "down_done", "y_a", "y_b", "y_stored")
        M = {n: [sem(f"m_{n}{u}") for u in range(2)] for n in names}
        gathering = sem("gathering")
        dma_names = ("up_in", "down_in", "gathered", "y_stored")
        with nc.Block() as block:
            def pairs(eng):
                return eng.value_load(meta[0:1, MAXTILES:MAXTILES + 1], min_val=1, max_val=MAXTILES // 2)

            @block.sync
            def _(sp):
                with sp.Fori(0, pairs(sp)) as i:
                    tile = [flat(experts[bass.ds(sp.value_load(meta[0:1, bass.ds(i * 2 + u, 1)], min_val=0,
                                                               max_val=NEXP - 1), 1)].rearrange("a p n -> p a n"))
                            for u in range(2)]
                    for u in range(2):
                        sp.wait_ge(M["up_done"][u], i + 1)
                        sp.dma_start(w_up[:, u, :], tile[u][:, 0:KT * 512]).then_inc(M["up_in"][u], 16)
                    for u in range(2):
                        sp.wait_ge(M["down_done"][u], i + 1)
                        sp.dma_start(w_down[:, u, :], tile[u][:, KT * 512:]).then_inc(M["down_in"][u], 16)

            @block.gpsimd
            def _(pool):
                credit(pool, [v for n, v in M.items() if n not in dma_names])
                pool.wait_ge(h_stored, TT * 16)
                turns = pairs(pool)
                with pool.Fori(0, turns) as i:
                    for u in range(2):
                        pool.wait_ge(M["turned"][u], i + 1)
                        apart(pool)
                        pool.tensor_copy(idx[:, u, :], tok_i[:, bass.ds(i * 2 + u, 1)]).then_inc(M["idx_set"][u], 1)
                        pool.wait_ge(M["idx_set"][u], i + 2)
                        pool.sem_inc(gathering, 1)
                        pool.indirect_dma_start(
                            out=hg[:, u, :], out_offset=None, in_=h2_dram,
                            in_offset=bass.IndirectOffsetOnAxis(ap=idx[:, u, :], axis=0)).then_inc(M["gathered"][u], 16)
                for u in range(2):
                    pool.wait_ge(M["y_stored"][u], turns * 16 + 1)

            @block.tensor
            def _(pe):
                with pe.Fori(0, pairs(pe)) as i:
                    for u in range(2):
                        pe.wait_ge(M["gathered"][u], i * 16 + 16)
                        pe.wait_ge(M["y_a"][u], i + 1)
                        pe.wait_ge(M["y_b"][u], i + 1)
                        for k in range(KT):
                            m = pe.transpose(ps[:, 2 * u + k // 4, (k % 4) * P:(k % 4 + 1) * P],
                                             hg[:, u, k * P:(k + 1) * P], ident)
                        m.then_inc(M["turned"][u], 1)
                    for u in range(2):
                        pe.wait_ge(M["up_in"][u], i * 16 + 16)
                        pe.wait_ge(M["copied_a"][u], i + 2)
                        pe.wait_ge(M["copied_b"][u], i + 2)
                        pe.wait_ge(M["hid_done"][u], i + 1)
                        for k in range(KT):
                            m = pe.matmul(ps[:, 4 + u, :], hgT[:, u, k, :], w_up[:, u, k * 512:(k + 1) * 512],
                                          start=k == 0, stop=k == KT - 1)
                        m.then_inc(M["up_done"][u], 1)

                    def turn_hidden(u):
                        pe.wait_ge(M["hid_done"][u], i + 2)
                        pe.wait_ge(M["hid_copied"][u], i + 1)
                        for f in range(2):
                            m = pe.transpose(ps[:, 6 + u, f * P:(f + 1) * P], hid[:, u, f * P:(f + 1) * P], ident)
                        m.then_inc(M["hid_tr"][u], 1)

                    def down(u, half):
                        for f in range(2):
                            o = f * D + half * 512
                            m = pe.matmul(ps[:, 2 * u + half, :], hidT[:, u, f, :], w_down[:, u, o:o + 512],
                                          start=f == 0, stop=f == 1)
                        return m
                    turn_hidden(0)
                    pe.wait_ge(M["down_in"][0], i * 16 + 16)
                    pe.wait_ge(M["hid_copied"][0], i + 2)
                    down(0, 0)
                    turn_hidden(1)
                    down(0, 1).then_inc(M["down_done"][0], 1)
                    pe.wait_ge(M["down_in"][1], i * 16 + 16)
                    pe.wait_ge(M["hid_copied"][1], i + 2)
                    down(1, 0)
                    down(1, 1).then_inc(M["down_done"][1], 1)

            @block.scalar
            def _(act):
                with act.Fori(0, pairs(act)) as i:
                    for u in range(2):
                        act.wait_ge(M["turned"][u], i + 2)
                        act.activation(hgT[:, u, 0:4, :].rearrange("p k n -> p (k n)"), ps[:, 2 * u, :], ACT.Copy
                                       ).then_inc(M["copied_a"][u], 1)
                    for u in range(2):
                        act.wait_ge(M["up_done"][u], i + 2)
                        act.activation(sg[:, u, :], ps[:, 4 + u, 0:256], ACT.Silu).then_inc(M["gate"][u], 1)
                    for u in range(2):
                        act.wait_ge(M["down_done"][u], i + 2)
                        act.wait_ge(M["y_stored"][u], i * 16 + 1)
                        act.activation(ytile[:, u, 0:512], ps[:, 2 * u, :], ACT.Copy).then_inc(M["y_a"][u], 1)
                        act.wait_ge(M["y_a"][u], i + 2)
                        act.wait_ge(M["y_b"][u], i + 2)
                        act.dma_start(y_dram[bass.ds((i * 2 + u) * P, P), :], ytile[:, u, :]
                                      ).then_inc(M["y_stored"][u], 16)

            @block.vector
            def _(ve):
                for u in range(2):
                    ve.sem_inc(M["y_stored"][u], 1)
                with ve.Fori(0, pairs(ve)) as i:
                    for u in range(2):
                        ve.wait_ge(M["turned"][u], i + 2)
                        ve.tensor_copy(hgT[:, u, 4:8, :].rearrange("p k n -> p (k n)"), ps[:, 2 * u + 1, :]
                                       ).then_inc(M["copied_b"][u], 1)
                    for u in range(2):
                        ve.wait_ge(M["gate"][u], i + 2)
                        ve.tensor_tensor(hid[:, u, :], sg[:, u, :], ps[:, 4 + u, 256:512], ALU.mult
                                         ).then_inc(M["hid_done"][u], 1)
                    for u in range(2):
                        ve.wait_ge(M["hid_tr"][u], i + 2)
                        ve.tensor_copy(hidT[:, u, :, :].rearrange("p f n -> p (f n)"), ps[:, 6 + u, 0:256]
                                       ).then_inc(M["hid_copied"][u], 1)
                    for u in range(2):
                        ve.wait_ge(M["down_done"][u], i + 2)
                        ve.wait_ge(M["y_stored"][u], i * 16 + 1)
                        ve.tensor_copy(ytile[:, u, 512:1024], ps[:, 2 * u + 1, :]).then_inc(M["y_b"][u], 1)

        acc = mix[:, :, :].rearrange("p (t h) n -> p t h n", h=2)
        rows_back, weighed = [sem(f"rows_back{t}") for t in range(TT)], sem("weighed")
        yrow = w_up[:, :, :].rearrange("p a (t n) -> p a t n", t=TT)
        with nc.Block() as block:
            @block.gpsimd
            def _(pool):
                for t in range(TT):
                    for a in range(2):
                        pool.indirect_dma_start(
                            out=yrow[:, a, t, :], out_offset=None, in_=y_dram,
                            in_offset=bass.IndirectOffsetOnAxis(ap=slot_i[:, a, t:t + 1], axis=0)
                        ).then_inc(rows_back[t], 16)

            @block.vector
            def _(ve):
                for t in range(TT):
                    ve.wait_ge(rows_back[t], 32)
                    y1, y2 = yrow[:, 0, t, :], yrow[:, 1, t, :]
                    ve.tensor_scalar(y1, y1, one[:, 6, t, :], None, ALU.mult).then_inc(weighed, 1)
                    ve.wait_ge(weighed, 2 * t + 1)
                    ve.scalar_tensor_tensor(htok[:, t, :], y2, one[:, 5, t, :], y1, ALU.mult, ALU.add).then_inc(weighed, 1)
        y_done, y_added = sem("y_done"), sem("y_added")
        with nc.Block() as block:
            @block.tensor
            def _(pe):
                for k in range(KT):
                    for t in range(TT):
                        m = pe.transpose(ps[:, k, t * P:(t + 1) * P],
                                         acc[:, t, k // 4, (k % 4) * P:(k % 4 + 1) * P], ident)
                    m.then_inc(y_done, 1)

            @block.vector
            def _(ve):
                for k in range(KT):
                    ve.wait_ge(y_done, k + 1)
                    ve.scalar_tensor_tensor(res[:, k, :], ps[:, k, :], mod[:, 40 + k, 0:1], res[:, k, :],
                                            ALU.mult, ALU.add).then_inc(y_added, 1)
        moe.close()
        norm("fin", res, res, lambda k: col("final", k))

        retire()
        norm("gn", res, hn, lambda k: col("attn", k))
        V = mix
        gdn = ctx.enter_context(ExitStack())
        Q = sb("Q", [P, HEADS, T], on=gdn)
        K = sb("K", [P, HEADS, T], on=gdn)
        Z = sb("Z", [P, HEADS, T], on=gdn)
        gcols = sb("gcols", [P, 3, TT, HEADS], on=gdn)
        egl = sb("egl", [P, HEADS, TT], on=gdn)
        rows = tab[0:8, TABLES["rcount"]].rearrange("p (a t) -> p a t", a=4)
        ea = sb("ea", [8, 1], on=gdn)
        ab_done, ab_act, ab_dve, ab_tr, ab_cols = (sem(n) for n in ("ab_done", "ab_act", "ab_dve", "ab_tr", "ab_cols"))
        with nc.Block() as block:
            @block.tensor
            def _(pe):
                wab = sml[:, SMALL["wab"]].rearrange("p (k n) -> p k n", k=KT)
                for part in range(2):
                    for k in range(KT):
                        m = pe.matmul(ps[0:8, part, :], wab[:, k, 8 * part:8 * part + 8], hn[:, k, :],
                                      start=k == 0, stop=k == KT - 1)
                m.then_inc(ab_done, 1)
                pe.wait_ge(ab_dve, 6)
                for a in range(3):
                    for t in range(TT):
                        o = (a * TT + t) * 8
                        m = pe.transpose(ps[:, 2, o:o + 8], rows[:, a, t * P:(t + 1) * P], tab[0:8, 0:8])
                m.then_inc(ab_tr, 1)

            @block.scalar
            def _(act):
                n = [0]

                def step(ins):
                    n[0] += 1
                    ins.then_inc(ab_act, 1)
                    act.wait_ge(ab_act, n[0])
                act.wait_ge(ab_done, 1)
                step(act.activation(rows[:, 1, :], ps[0:8, 0, :], ACT.Sigmoid))
                step(act.activation(ea[:, :], ab8[:, 0:1], ACT.Exp))
                step(act.activation(rows[:, 3, :], ps[0:8, 1, :], ACT.Abs, bias=ab8[:, 1:2]))
                step(act.activation(rows[:, 3, :], rows[:, 3, :], ACT.Exp, scale=-1.0))
                step(act.activation(rows[:, 3, :], rows[:, 3, :], ACT.Ln, bias=1.0))
                act.wait_ge(ab_dve, 5)
                step(act.activation(rows[:, 3, :], rows[:, 0, :], ACT.Exp))

            @block.vector
            def _(ve):
                n = [0]

                def step(ins):
                    n[0] += 1
                    ins.then_inc(ab_dve, 1)
                    ve.wait_ge(ab_dve, n[0])
                ve.wait_ge(ab_act, 5)
                step(ve.tensor_scalar(rows[:, 0, :], ps[0:8, 1, :], ab8[:, 1:2], 0.0, ALU.add, ALU.max))
                step(ve.tensor_tensor(rows[:, 0, :], rows[:, 0, :], rows[:, 3, :], ALU.add))
                step(ve.tensor_scalar(rows[:, 3, :], rows[:, 0, :], ea[:, :], -1.0, ALU.mult, ALU.mult))
                step(ve.tensor_tensor_scan(rows[:, 0, :], tab[0:8, TABLES["resetd"]], rows[:, 3, :], 0.0,
                                           ALU.mult, ALU.add))
                step(ve.nop())
                ve.wait_ge(ab_act, 6)
                step(ve.tensor_tensor(rows[:, 2, :], rows[:, 1, :], rows[:, 3, :], ALU.mult))
                ve.wait_ge(ab_tr, 1)
                ve.tensor_copy(gcols[:, :, :, :].rearrange("p a t h -> p (a t h)"), ps[:, 2, 0:96]).then_inc(ab_cols, 1)

        st = gdn.enter_context(ExitStack())
        cin = sb("cin", [P, 2, 3, T + 3], on=st)
        cv = sb("cv", [P, 2, 3, T], on=st)
        sq = hctx[:, :, :].rearrange("p (u j b) t -> p u j (b t)", u=2, j=2)
        rs = sb("g_rs", [P, 2, 2, T], on=st)
        BG = STREAM["gdn"].start
        cin_zero, relay = sem("cin_zero"), sem("g_relay")
        (copied, gated_z, conv_step, conved, silued, squared, summed, mean_read, rooted, qk_step, qk_done) = (
            [sem(f"g_{n}{u}") for u in range(2)] for n in
            ("copied", "gated_z", "conv_step", "conved", "silued", "squared", "summed", "mean_read", "rooted",
             "qk_step", "qk_done"))
        with nc.Block() as block:
            @block.sync
            def _(sp):
                load_blocks(sp, STREAM["gdnout"].start + SLOTS)

            @block.gpsimd
            def _(pool):
                pool.memset(cin[:, :, :, 0:3], 0.0).then_inc(cin_zero, 1)

            def turns(eng, one_turn, last):
                one_turn(0, None)
                with eng.Fori(0, HEADS // 2 - 1) as i:
                    one_turn(i + 1, i)
                last(HEADS // 2 - 1)

            def block_of(u, j):
                return BG + (2 * u + j if j < 2 else 2 + 2 * u + j)

            def head(x, t, u):
                return flat(x[:, bass.ds(t * 2 + u, 1), :])

            @block.tensor
            def _(pe):
                def sums(u, before):
                    for j in range(2):
                        pe.wait_ge(squared[u], before * 2 + j + 1)
                        if j == 0:
                            pe.wait_ge(copied[u], before * 3 + 3)
                        else:
                            pe.wait_ge(gated_z[u], before + 1)
                        pe.matmul(ps[:, 4 * u + 2 + j, :], ones, sq[:, u, j, :], start=True, stop=True
                                  ).then_inc(summed[u], 1)

                def one_turn(t, before):
                    def tile(u, j):
                        if before is not None:
                            if j < 2:
                                pe.wait_ge(copied[u], before * 3 + j + 1)
                            else:
                                pe.wait_ge(mean_read[u], before * 2 + j - 1)
                        b = block_of(u, j)
                        w = block_here(pe, b) if before is None else block_here(pe, b, t)
                        dense_tile(pe, w, hn, ps[:, 4 * u + j, :])
                    for u in range(2):
                        tile(u, 0)
                        tile(u, 1)
                        if before is not None:
                            sums(u, before)
                    for u in range(2):
                        tile(u, 2)
                        tile(u, 3)
                turns(pe, one_turn, lambda before: [sums(u, before) for u in range(2)])

            @block.scalar
            def _(act):
                def roots(u, before):
                    for j in range(2):
                        act.wait_ge(mean_read[u], before * 2 + j + 1)
                        act.activation(rs[:, u, j, :], rs[:, u, j, :], ACT.Sqrt).then_inc(rooted[u], 1)

                def one_turn(t, before):
                    def copy(u, j):
                        act.wait_ge(blocks_done, t * 8 + block_of(u, j) + 1)
                        if before is not None:
                            act.wait_ge(conved[u], before * 3 + j + 1)
                        act.activation(cin[:, u, j, 3:], ps[:, 4 * u + j, :], ACT.Copy).then_inc(copied[u], 1)

                    def silu(u, j):
                        act.wait_ge(conved[u], t * 3 + j + 1)
                        act.sem_inc(relay, 1)
                        act.activation(head((Q, K, V)[j], t, u), cv[:, u, j, :], ACT.Silu).then_inc(silued[u], 1)
                    for u in range(2):
                        copy(u, 0)
                        copy(u, 1)
                        if before is not None:
                            roots(u, before)
                        for j in range(2):
                            silu(u, j)
                            act.wait_ge(silued[u], t * 3 + j + 1)
                            if before is not None:
                                act.wait_ge(summed[u], before * 2 + j + 1)
                            act.sem_inc(relay, 1)
                            act.activation(sq[:, u, j, :], head((Q, K)[j], t, u), ACT.Square).then_inc(squared[u], 1)
                    for u in range(2):
                        copy(u, 2)
                        act.wait_ge(blocks_done, t * 8 + block_of(u, 3) + 1)
                        act.sem_inc(relay, 1)
                        act.activation(head(Z, t, u), ps[:, 4 * u + 3, :], ACT.Silu).then_inc(gated_z[u], 1)
                        silu(u, 2)
                turns(act, one_turn, lambda before: [roots(u, before) for u in range(2)])

            @block.vector
            def _(ve):
                def normalise(u, before):
                    for j in range(2):
                        ve.wait_ge(summed[u], before * 2 + j + 1)
                        ve.tensor_scalar(rs[:, u, j, :], ps[:, 4 * u + 2 + j, :], EPS, None, ALU.add
                                         ).then_inc(mean_read[u], 1)
                    for j in range(2):
                        ve.wait_ge(rooted[u], before * 2 + j + 1)
                        ve.reciprocal(rs[:, u, j, :], rs[:, u, j, :]).then_inc(qk_step[u], 1)
                        ve.wait_ge(qk_step[u], before * 2 + j + 1)
                        x = head((Q, K)[j], before, u)
                        ve.scalar_tensor_tensor(x, x, (P ** -0.5, 1.0)[j], rs[:, u, j, :], ALU.mult, ALU.mult
                                                ).then_inc(qk_done[u], 1)

                def one_turn(t, before):
                    def convolve(u, j):
                        ve.wait_ge(copied[u], t * 3 + j + 1)
                        if before is not None:
                            ve.wait_ge(silued[u], before * 3 + j + 1)
                        for w in range(4):
                            tap = par[:, bass.ds((t * 2 + u) * 4 + PARAMS.at["conv"][0] + 32 * j + w, 1)]
                            if w == 0:
                                ins = ve.tensor_scalar(cv[:, u, j, :], cin[:, u, j, 0:T], tap, None, ALU.mult)
                            else:
                                ve.wait_ge(conv_step[u], t * 9 + 3 * j + w)
                                ins = ve.scalar_tensor_tensor(cv[:, u, j, :], cin[:, u, j, w:w + T], tap,
                                                              cv[:, u, j, :], ALU.mult, ALU.add)
                            ins.then_inc(conv_step[u] if w < 3 else conved[u], 1)
                    for u in range(2):
                        convolve(u, 0)
                        convolve(u, 1)
                        if before is not None:
                            normalise(u, before)
                    for u in range(2):
                        convolve(u, 2)
                ve.wait_ge(cin_zero, 1)
                turns(ve, one_turn, lambda before: [normalise(u, before) for u in range(2)])
        st.close()

        def tiles(x):
            return x.rearrange("p (n i) -> p n i", n=TT)

        def every_tile(mask):
            return mask.unsqueeze(1).to_broadcast([P, TT, P])
        KD = sb("KD", [P, HEADS, T], on=gdn)
        AT = hn
        st = gdn.enter_context(ExitStack())
        rowm = hctx[:, :, :].rearrange("p (u a b) t -> p u a (b t)", u=2, a=2)
        dm, aT_, bmT, mm_, tn, tT = (sb(f"inv_{n}", [P, 2, T], on=st) for n in ("dm", "aT", "bmT", "m", "t", "tT"))
        ks = sb("ks", [P, 2, T], on=st)
        vs = sml[:, 0:2 * T].rearrange("p (u t) -> p u t", u=2)
        names = ("staged", "rowed", "spread", "diff", "expd", "exprow", "paired", "dve", "qdec", "t_tr", "kv_tr",
                 "t_copy", "kv_ready", "masked", "m_done", "m_copy", "xy_done", "updated", "fin_done", "fin_kept")
        S = {n: [sem(f"i_{n}{u}") for u in range(2)] for n in names}
        with nc.Block() as block:
            @block.scalar
            def _(act):
                with act.Fori(0, HEADS // 2) as i:
                    heads = [bass.ds(i * 2 + u, 1) for u in range(2)]
                    for u in range(2):
                        act.wait_ge(S["fin_done"][u], i + 1)
                        apart(act)
                        act.activation(ks[:, u, :], flat(K[:, heads[u], :]), ACT.Copy).then_inc(S["staged"][u], 1)
                        act.activation(vs[:, u, :], flat(V[:, heads[u], :]), ACT.Copy).then_inc(S["staged"][u], 1)
                    for u in range(2):
                        act.wait_ge(S["diff"][u], i * 2 + 3)
                        act.activation(mm_[:, u, :], ps[:, 4 * u, :], ACT.Exp).then_inc(S["exprow"][u], 1)
                        act.activation(dm[:, u, :], dm[:, u, :], ACT.Exp).then_inc(S["expd"][u], 1)
                    for u in range(2):
                        act.wait_ge(S["t_tr"][u], i + 2)
                        act.activation(tn[:, u, :], ps[:, 4 * u + 2, :], ACT.Copy).then_inc(S["t_copy"][u], 1)
                    for lv in range(1, LEVELS + 1):
                        for u in range(2):
                            act.wait_ge(S["m_done"][u], i * LEVELS + lv + 1)
                            if lv == 1:
                                act.wait_ge(S["qdec"][u], i + 2)
                            act.activation(mm_[:, u, :], ps[:, 4 * u + 2, :], ACT.Copy).then_inc(S["m_copy"][u], 1)

            @block.gpsimd
            def _(pool):
                credit(pool, S.values())
                with pool.Fori(0, HEADS // 2) as i:
                    heads = [bass.ds(i * 2 + u, 1) for u in range(2)]
                    for u in range(2):
                        pool.wait_ge(S["exprow"][u], i + 2)
                        pool.wait_ge(S["paired"][u], i + 2)
                        apart(pool)
                        q = flat(Q[:, heads[u], :])
                        pool.tensor_tensor(q, q, mm_[:, u, :], ALU.mult).then_inc(S["qdec"][u], 1)
                    for lv in range(1, LEVELS + 1):
                        for u in range(2):
                            if lv == 1:
                                pool.wait_ge(S["dve"][u], i * 8 + 8 + 1)
                            pool.wait_ge(S["m_done"][u], i * LEVELS + lv - 1 + 1)
                            m0 = TABLES.at["level"][0] + lv * P
                            pool.tensor_tensor(tiles(bmT[:, u, :]), tiles(aT_[:, u, :]),
                                               every_tile(tab[:, m0:m0 + P]), ALU.mult).then_inc(S["masked"][u], 1)

            @block.vector
            def _(ve):
                with ve.Fori(0, HEADS // 2) as i:
                    heads = [bass.ds(i * 2 + u, 1) for u in range(2)]

                    def bycol(a, u):
                        return gcols[:, a, :, heads[u]].to_broadcast([P, TT, P])
                    for u in range(2):
                        for a in range(2):
                            ve.tensor_scalar(rowm[0:8, u, a, :], rows[:, a, :], tab[0:8, heads[u]], None,
                                             ALU.mult).then_inc(S["rowed"][u], 1)
                    for u in range(2):
                        ve.wait_ge(S["spread"][u], i + 2)
                        ve.tensor_tensor(tiles(dm[:, u, :]), tiles(ps[:, 4 * u, :]), bycol(0, u), ALU.subtract
                                         ).then_inc(S["diff"][u], 1)
                    for u in range(2):
                        ve.wait_ge(S["diff"][u], i * 2 + 2)
                        ve.tensor_scalar(dm[:, u, :], dm[:, u, :], 0.0, None, ALU.min).then_inc(S["diff"][u], 1)
                    for step in range(8):
                        for u in range(2):
                            d, at, t = tiles(dm[:, u, :]), tiles(aT_[:, u, :]), tiles(tT[:, u, :])
                            if step:
                                ve.wait_ge(S["dve"][u], i * 8 + step + 1)
                            if step == 0:
                                ve.wait_ge(S["expd"][u], i + 2)
                                ins = ve.tensor_tensor(d, d, every_tile(tab[:, TABLES["incl"]]), ALU.mult)
                            elif step == 1:
                                ve.wait_ge(S["paired"][u], i + 2)
                                ins = ve.tensor_tensor(flat(AT[:, heads[u], :]), ps[:, 4 * u + 3, :], dm[:, u, :], ALU.mult)
                            elif step == 2:
                                ins = ve.tensor_tensor(at, d, every_tile(tab[:, TABLES["strict"]]), ALU.mult)
                            elif step == 3:
                                ins = ve.tensor_tensor(aT_[:, u, :], ps[:, 4 * u + 1, :], aT_[:, u, :], ALU.mult)
                            elif step == 4:
                                ins = ve.tensor_tensor(aT_[:, u, :], ps[:, 4 * u + 2, :], aT_[:, u, :], ALU.mult)
                            elif step == 5:
                                m0 = TABLES.at["level"][0]
                                ins = ve.tensor_tensor(t, at, every_tile(tab[:, m0:m0 + P]), ALU.mult)
                            elif step == 6:
                                ins = ve.tensor_tensor(t, every_tile(ident), t, ALU.subtract)
                            else:
                                ve.wait_ge(S["exprow"][u], i + 2)
                                apart(ve)
                                ins = ve.tensor_copy(egl[:, heads[u], :].rearrange("p a n -> p n a"),
                                                     tiles(mm_[:, u, :])[:, :, P - 1:P])
                            ins.then_inc(S["dve"][u], 1)
                    for u in range(2):
                        ve.wait_ge(S["kv_tr"][u], i + 2)
                        ktok, vtok_ = tiles(ps[:, 4 * u, :]), tiles(ps[:, 4 * u + 1, :])
                        ve.tensor_tensor(flat(KD[:, heads[u], :]).rearrange("p (n i) -> p n i", n=TT), ktok,
                                         tiles(dm[:, u, :])[:, :, P - 1:P].to_broadcast([P, TT, P]), ALU.mult
                                         ).then_inc(S["kv_ready"][u], 1)
                        ve.tensor_tensor(tiles(ks[:, u, :]), ktok, bycol(2, u), ALU.mult).then_inc(S["kv_ready"][u], 1)
                        ve.tensor_tensor(tiles(vs[:, u, :]), vtok_, bycol(1, u), ALU.mult).then_inc(S["kv_ready"][u], 1)
                    for lv in range(1, LEVELS + 1):
                        for u in range(2):
                            ve.wait_ge(S["xy_done"][u], i * LEVELS + lv + 1)
                            ve.tensor_tensor(tT[:, u, :], tT[:, u, :], ps[:, 4 * u + 2, :], ALU.subtract
                                             ).then_inc(S["updated"][u], 1)
                            if lv < LEVELS:
                                ve.tensor_tensor(tn[:, u, :], tn[:, u, :], ps[:, 4 * u + 3, :], ALU.subtract
                                                 ).then_inc(S["updated"][u], 1)
                    for u in range(2):
                        ve.wait_ge(S["fin_done"][u], i + 2)
                        for n, keep in enumerate((V, K)):
                            ve.tensor_scalar(flat(keep[:, heads[u], :]), ps[:, 4 * u + n, :], 1.0, None, ALU.mult
                                             ).then_inc(S["fin_kept"][u], 1)

            @block.tensor
            def _(pe):
                def four(out, lhsT, rhs):
                    for n in range(TT):
                        c = slice(n * P, (n + 1) * P)
                        m = pe.matmul(out[:, c], lhsT[:, c], rhs[:, c], start=True, stop=True)
                    return m
                with pe.Fori(0, HEADS // 2) as i:
                    heads = [bass.ds(i * 2 + u, 1) for u in range(2)]
                    B = [[ps[:, 4 * u + n, :] for n in range(4)] for u in range(2)]
                    for u in range(2):
                        pe.wait_ge(S["rowed"][u], i * 2 + 2 + 1)
                        pe.wait_ge(S["fin_kept"][u], i * 2 + 1)
                        for a in range(2):
                            m = pe.matmul(B[u][a], tab[0:8, TABLES["ones"]], rowm[0:8, u, a, :], start=True, stop=True)
                        m.then_inc(S["spread"][u], 1)
                    for u in range(2):
                        pe.wait_ge(S["staged"][u], i * 2 + 2 + 1)
                        pe.wait_ge(S["updated"][u], i * (2 * LEVELS - 1) + 1)
                        four(B[u][2], ks[:, u, :], ks[:, u, :])
                        for n in range(TT):
                            q = Q[:, heads[u], n * P:(n + 1) * P]
                            m = pe.matmul(B[u][3][:, n * P:(n + 1) * P], ks[:, u, n * P:(n + 1) * P], flat(q),
                                          start=True, stop=True)
                        m.then_inc(S["paired"][u], 1)
                    for u in range(2):
                        pe.wait_ge(S["dve"][u], i * 8 + 7 + 1)
                        for n in range(TT):
                            c = slice(n * P, (n + 1) * P)
                            m = pe.transpose(B[u][2][:, c], tT[:, u, c], ident)
                        m.then_inc(S["t_tr"][u], 1)
                        pe.wait_ge(S["exprow"][u], i + 2)
                        for n in range(TT):
                            c = slice(n * P, (n + 1) * P)
                            pe.transpose(B[u][0][:, c], ks[:, u, c], ident)
                            m = pe.transpose(B[u][1][:, c], vs[:, u, c], ident)
                        m.then_inc(S["kv_tr"][u], 1)
                    for lv in range(1, LEVELS + 1):
                        for u in range(2):
                            pe.wait_ge(S["masked"][u], i * LEVELS + lv + 1)
                            pe.wait_ge(S["t_copy"][u], i + 2)
                            pe.wait_ge(S["updated"][u], i * (2 * LEVELS - 1) + 2 * (lv - 1) + 1)
                            four(B[u][2], bmT[:, u, :], tn[:, u, :]).then_inc(S["m_done"][u], 1)
                        for u in range(2):
                            pe.wait_ge(S["m_copy"][u], i * LEVELS + lv + 1)
                            if lv < LEVELS:
                                four(B[u][3], tT[:, u, :], mm_[:, u, :])
                            four(B[u][2], mm_[:, u, :], tT[:, u, :]).then_inc(S["xy_done"][u], 1)
                    for u in range(2):
                        pe.wait_ge(S["updated"][u], i * (2 * LEVELS - 1) + 2 * LEVELS - 1 + 1)
                        pe.wait_ge(S["kv_ready"][u], i * 3 + 3 + 1)
                        four(B[u][0], tT[:, u, :], vs[:, u, :])
                        four(B[u][1], ks[:, u, :], tT[:, u, :]).then_inc(S["fin_done"][u], 1)
        st.close()

        retire()
        st = gdn.enter_context(ExitStack())
        St = sb("St", [P, HEADS, P], on=st)
        vn = sb("vn", [P, HEADS, P], on=st)
        s_zero, ws_done, vn_done, so_done, sd_done, o_kept2 = (
            [sem(f"{n}{g}") for g in range(2)] for n in ("s_zero", "ws_done", "vn_done", "so_done", "sd_done", "o_kept2"))
        s_next = [sem(f"s_next{g}") for g in range(2)]
        with nc.Block() as block:
            @block.tensor
            def _(pe):
                for n in range(TT):
                    c = slice(n * P, (n + 1) * P)
                    for g in range(2):
                        pe.wait_ge(s_next[g], 2 * n + 1)
                        for h in range(4):
                            m = pe.matmul(ps[:, g, h * P:(h + 1) * P], K[:, 4 * g + h, c], St[:, 4 * g + h, :],
                                          start=True, stop=True)
                        m.then_inc(ws_done[g], 1)
                    for g in range(2):
                        pe.wait_ge(vn_done[g], n + 1)
                        if n:
                            pe.wait_ge(o_kept2[g], n)
                        for h in range(4):
                            out = ps[:, 2 + g, h * P:(h + 1) * P]
                            pe.matmul(out, St[:, 4 * g + h, :], Q[:, 4 * g + h, c], start=True, stop=False)
                            m = pe.matmul(out, vn[:, 4 * g + h, :], AT[:, 4 * g + h, c], start=False, stop=True)
                        m.then_inc(so_done[g], 1)
                        if n < TT - 1:
                            for h in range(4):
                                m = pe.matmul(ps[:, 4 + g, h * P:(h + 1) * P], KD[:, 4 * g + h, c],
                                              vn[:, 4 * g + h, :], start=True, stop=True)
                            m.then_inc(sd_done[g], 1)

            @block.vector
            def _(ve):
                for g in range(2):
                    ve.memset(St[:, 4 * g:4 * g + 4, :], 0.0).then_inc(s_next[g], 1)
                for n in range(TT):
                    for g in range(2):
                        hs = slice(4 * g, 4 * g + 4)
                        ve.wait_ge(ws_done[g], n + 1)
                        if n:
                            ve.wait_ge(sd_done[g], n)
                            ve.wait_ge(so_done[g], n)
                        ve.tensor_tensor(vn[:, hs, :], V[:, hs, n * P:(n + 1) * P],
                                         ps[:, g, :].rearrange("p (h e) -> p h e", h=4), ALU.subtract
                                         ).then_inc(vn_done[g], 1)
                    for g in range(2):
                        if n == TT - 1:
                            break
                        hs = slice(4 * g, 4 * g + 4)
                        ve.wait_ge(so_done[g], n + 1)
                        ve.tensor_tensor(St[:, hs, :], St[:, hs, :], egl[:, hs, n:n + 1].to_broadcast([P, 4, P]),
                                         ALU.mult).then_inc(s_next[g], 1)
                        ve.wait_ge(s_next[g], 2 * n + 2)
                        ve.wait_ge(sd_done[g], n + 1)
                        ve.tensor_tensor(St[:, hs, :], St[:, hs, :], ps[:, 4 + g, :].rearrange("p (h e) -> p h e", h=4),
                                         ALU.add).then_inc(s_next[g], 1)

            @block.scalar
            def _(act):
                for n in range(TT):
                    for g in range(2):
                        act.wait_ge(so_done[g], n + 1)
                        act.activation(Q[:, 4 * g:4 * g + 4, n * P:(n + 1) * P],
                                       ps[:, 2 + g, :].rearrange("p (h e) -> p h e", h=4), ACT.Copy
                                       ).then_inc(o_kept2[g], 1)
        st.close()

        on_sq, on_sum, on_ms, on_root, on_step, on_done = (
            sem(n) for n in ("on_sq", "on_sum", "on_ms", "on_root", "on_step", "on_done"))
        with nc.Block() as block:
            @block.scalar
            def _(act):
                for h in range(HEADS):
                    act.activation(hn[:, h, :], Q[:, h, :], ACT.Square).then_inc(on_sq, 1)
                for h in range(HEADS):
                    act.wait_ge(on_ms, h + 1)
                    act.activation(mix[:, h, :], mix[:, h, :], ACT.Sqrt).then_inc(on_root, 1)

            @block.tensor
            def _(pe):
                for h in range(HEADS):
                    pe.wait_ge(on_sq, h + 1)
                    pe.matmul(ps[:, h, :], ones, hn[:, h, :], start=True, stop=True).then_inc(on_sum, 1)

            @block.vector
            def _(ve):
                for h in range(HEADS):
                    ve.wait_ge(on_sum, h + 1)
                    ve.tensor_scalar(mix[:, h, :], ps[:, h, :], 1.0 / P, EPS, ALU.mult, ALU.add).then_inc(on_ms, 1)
                for h in range(HEADS):
                    ve.wait_ge(on_root, h + 1)
                    ve.reciprocal(mix[:, h, :], mix[:, h, :]).then_inc(on_step, 1)
                    ve.wait_ge(on_step, 2 * h + 1)
                    ve.scalar_tensor_tensor(mix[:, h, :], Q[:, h, :], col("ogain"), mix[:, h, :], ALU.mult, ALU.mult
                                            ).then_inc(on_step, 1)
                    ve.wait_ge(on_step, 2 * h + 2)
                    ve.tensor_tensor(Q[:, h, :], mix[:, h, :], Z[:, h, :], ALU.mult).then_inc(on_done, 1)
        project_out("gdnout", Q, STREAM["gdnout"].start, None, STREAM["gu0"].start + SLOTS)
        gdn.close()

        def feed_forward(layer):
            norm(f"fn{layer}", res, hn, lambda k: col("ffn", 8 * layer + k))
            with ExitStack() as st:
                act_ = sb(f"ff_act{layer}", [P, FT, T], on=st)
                sg = hctx[:, :, :].rearrange("p (a b) t -> p a (b t)", b=2)
                w_hi, w_lo = (sb(f"ff_w{n}{layer}", [P, 2, 1024], F32R, on=st) for n in ("hi", "lo"))
                a_hi, a_lo = (sb(f"ff_a{n}{layer}", [P, 2, T], F32R, on=st) for n in ("hi", "lo"))
                h_hi, h_lo = (sb(f"ff_h{n}{layer}", [P, KT, T], F32R, on=st) for n in ("hi", "lo"))
                B0 = STREAM[f"gu{layer}"].start
                B1 = STREAM[f"down{layer}"].start
                silu_done, act_ready, added, h_split, w_rounded, tile_done, a_rounded, a_split, row_done, h_rest = (
                    sem(f"ff_{n}{layer}") for n in ("silu", "act", "added", "h_split", "w_rounded", "tile_done",
                                                    "a_rounded", "a_split", "row_done", "h_rest"))
                turns, rest = FT // 4, FT % 4
                with nc.Block() as block:
                    @block.sync
                    def _(sp):
                        load_blocks(sp, B1 + FT + SLOTS)

                    @block.tensor
                    def _(pe):
                        def up(i, pairs, extra):
                            for j in range(2 * pairs):
                                pe.wait_ge(act_ready, i * 4 + extra + j // 2 + 1)
                                b = B0 + 2 * extra + j
                                pe.wait_ge(blocks_done, i * SLOTS + b + 1)
                                for k in range(KT):
                                    c = slice(k * P, (k + 1) * P)
                                    m = three(pe, ps[:, j, :], w_hi[:, j % 2, c], w_lo[:, j % 2, c],
                                              h_hi[:, k, :], h_lo[:, k, :], k == 0, k == KT - 1)
                                m.then_inc(tile_done, 1)
                        pe.wait_ge(h_rest, KT)
                        with pe.Fori(0, turns) as i:
                            up(i, 4, 0)
                        up(0, rest, 4 * turns)
                        pe.wait_ge(act_ready, 4 + FT)
                        for f in range(FT):
                            pe.wait_ge(blocks_done, B1 + f + 1)
                            pe.wait_ge(a_split, f + 1)
                            for n in range(KT):
                                c = slice(n * P, (n + 1) * P)
                                m = three(pe, ps[:, n, :], w_hi[:, f % 2, c], w_lo[:, f % 2, c],
                                          a_hi[:, f % 2, :], a_lo[:, f % 2, :], f == 0, f == FT - 1)
                            m.then_inc(row_done, 1)

                    def round_block(act, j, i=None):
                        b = B0 + j
                        s, v = b % SLOTS, 16 * (b // SLOTS + 1)
                        act.wait_ge(block_in[s], v if i is None else i * 16 + v)
                        if j >= 2 * FT + 2:
                            act.wait_ge(row_done, j - 2 * FT - 1)
                        elif i is not None or j >= 2:
                            act.wait_ge(tile_done, (0 if i is None else i * SLOTS) + j + 1)
                        act.activation(w_hi[:, j % 2, :], ring[:, s, :], ACT.Copy).then_inc(w_rounded, 1)

                    def rest_of_block(ve, j, i=None):
                        ve.wait_ge(w_rounded, (0 if i is None else i * SLOTS) + j + 1)
                        ve.tensor_tensor(w_lo[:, j % 2, :], ring[:, (B0 + j) % SLOTS, :], w_hi[:, j % 2, :].bitcast(F32),
                                         ALU.subtract).then_inc(blocks_done, 1)

                    def round_row(act, f):
                        if f >= 2:
                            act.wait_ge(row_done, f - 1)
                        act.wait_ge(act_ready, 4 + f + 1)
                        act.activation(a_hi[:, f % 2, :], act_[:, f, :], ACT.Copy).then_inc(a_rounded, 1)

                    def rest_of_row(ve, f):
                        ve.wait_ge(a_rounded, f + 1)
                        ve.tensor_tensor(a_lo[:, f % 2, :], act_[:, f, :], a_hi[:, f % 2, :].bitcast(F32),
                                         ALU.subtract).then_inc(a_split, 1)

                    @block.scalar
                    def _(act):
                        act.sem_inc(tile_done, 2)
                        for k in range(KT):
                            act.activation(h_hi[:, k, :], hn[:, k, :], ACT.Copy).then_inc(h_split, 1)
                        round_block(act, 0)
                        round_block(act, 1)

                        def gate(i, pairs, extra):
                            t = 0 if i is None else i
                            for p in range(pairs):
                                act.wait_ge(tile_done, t * 8 + 2 * extra + 2 * p + 1 + 2)
                                act.wait_ge(act_ready, t * 4 + extra + p + 1)
                                act.activation(sg[:, p, :], ps[:, 2 * p, :], ACT.Silu).then_inc(silu_done, 1)
                                for j in range(2):
                                    round_block(act, 2 * (extra + p) + 2 + j, i)
                        with act.Fori(0, turns) as i:
                            gate(i, 4, 0)
                        gate(None, rest, 4 * turns)
                        round_row(act, 0)
                        for f in range(FT):
                            if f + 1 < FT:
                                round_row(act, f + 1)
                            if f + 2 < FT:
                                round_block(act, 2 * FT + f + 2)

                    @block.vector
                    def _(ve):
                        ve.sem_inc(act_ready, 4)
                        for k in range(KT):
                            ve.wait_ge(h_split, k + 1)
                            ve.tensor_tensor(h_lo[:, k, :], hn[:, k, :], h_hi[:, k, :].bitcast(F32),
                                             ALU.subtract).then_inc(h_rest, 1)
                        rest_of_block(ve, 0)
                        rest_of_block(ve, 1)

                        def gated(i, pairs, extra):
                            t = 0 if i is None else i
                            for p in range(pairs):
                                rest_of_block(ve, 2 * (extra + p) + 2, i)
                                ve.wait_ge(silu_done, t * 4 + extra + p + 1)
                                ve.wait_ge(tile_done, t * 8 + 2 * extra + 2 * p + 2 + 2)
                                at = act_[:, extra + p, :] if i is None else flat(act_[:, bass.ds(i * 4 + p, 1), :])
                                ve.tensor_tensor(at, sg[:, p, :], ps[:, 2 * p + 1, :], ALU.mult).then_inc(act_ready, 1)
                                rest_of_block(ve, 2 * (extra + p) + 3, i)
                        with ve.Fori(0, turns) as i:
                            gated(i, 4, 0)
                        gated(None, rest, 4 * turns)
                        rest_of_row(ve, 0)
                        for f in range(FT):
                            if f + 1 < FT:
                                rest_of_row(ve, f + 1)
                            if f + 2 < FT:
                                rest_of_block(ve, 2 * FT + f + 2)
                        for n in range(KT):
                            ve.wait_ge(row_done, FT)
                            ve.tensor_tensor(res[:, n, :], ps[:, n, :], res[:, n, :], ALU.add).then_inc(added, 1)

        mixed.close()
        feed_forward(0)

        retire()
        sbt = ctx.enter_context(ExitStack())
        mix = sb("sbV", [P, KT, T], on=sbt)
        Q = sb("sbQ", [P, HEADS, T], on=sbt)
        K = sb("sbK", [P, HEADS, T], on=sbt)
        V = mix[:, :, :].rearrange("p (t a) (c d) -> p t (a c) d", a=2, d=P)
        st = sbt.enter_context(ExitStack())
        hk = mix
        norm("an", res, hn, lambda k: col("attn", 8 + k), also=(hk, lambda k: col("kvn", k)))
        sq = hctx[:, :, :].rearrange("p (j b) t -> p j (b t)", b=2)
        roots = [hn[:, n, :] for n in range(8)]
        w_hi, w_lo = (sb(f"sb_w{n}", [P, 2, 1024], F32R, on=st) for n in ("hi", "lo"))
        h_hi, h_lo = (sb(f"sb_h{n}", [P, KT, T], F32R, on=st) for n in ("hi", "lo"))
        (copied, squared, summed, mean_read, rooted, inverted, normed, v_kept, h_rounded, h_split, w_rounded,
         used) = (sem(f"sb_{n}") for n in ("copied", "squared", "summed", "mean_read", "rooted", "inverted", "normed",
                                           "v_kept", "h_rounded", "h_split", "w_rounded", "used"))
        B2 = STREAM["sbq"].start
        TILES, BLOCKS = 2 * HEADS, 2 * HEADS + KT
        sums_after = {5: range(0, 4), 9: range(4, 8), 13: range(8, 12), 15: range(12, 16)}
        with nc.Block() as block:
            @block.sync
            def _(sp):
                load_blocks(sp, STREAM["sbout"].start + SLOTS)

            @block.tensor
            def _(pe):
                def sums(g):
                    for j in range(4):
                        pe.wait_ge(copied, 4 * g + j + 1)
                        pe.wait_ge(squared, 4 * g + j + 1)
                        pe.matmul(ps[:, 4 * (g % 2) + j, :], ones, sq[:, j, :], start=True, stop=True
                                  ).then_inc(summed, 1)
                for n in range(TILES):
                    g, j = n // 4, n % 4
                    if j == 2 and g:
                        sums(g - 1)
                    if g >= 2:
                        pe.wait_ge(mean_read, 4 * (g - 2) + j + 1)
                    pe.wait_ge(blocks_done, B2 + n + 1)
                    for k in range(KT):
                        c = slice(k * P, (k + 1) * P)
                        pe.wait_ge(h_split, (0 if n < HEADS else KT) + k + 1)
                        m = three(pe, ps[:, n % 8, :], w_hi[:, n % 2, c], w_lo[:, n % 2, c],
                                  h_hi[:, k, :], h_lo[:, k, :], k == 0, k == KT - 1)
                    m.then_inc(used, 1)
                sums(TILES // 4 - 1)
                pe.wait_ge(mean_read, TILES)
                for k in range(KT):
                    pe.wait_ge(blocks_done, B2 + TILES + k + 1)
                    for n in range(8):
                        t, c = n // 2, slice((n % 2) * 512, (n % 2) * 512 + 512)
                        tokens = slice(t * P, (t + 1) * P)
                        m = three(pe, ps[:, n, :], h_hi[:, k, tokens], h_lo[:, k, tokens],
                                  w_hi[:, k % 2, c], w_lo[:, k % 2, c], k == 0, k == KT - 1)
                    m.then_inc(used, 1)

            @block.scalar
            def _(act):
                def round_all(src):
                    for k in range(KT):
                        act.activation(h_hi[:, k, :], src[:, k, :], ACT.Copy).then_inc(h_rounded, 1)

                def round_block(n):
                    s = (B2 + n) % SLOTS
                    act.wait_ge(block_in[s], 16 * ((B2 + n) // SLOTS + 1))
                    act.activation(w_hi[:, n % 2, :], ring[:, s, :], ACT.Copy).then_inc(w_rounded, 1)

                def root(n):
                    act.wait_ge(mean_read, n + 1)
                    act.activation(roots[n % 8], roots[n % 8], ACT.Sqrt).then_inc(rooted, 1)
                round_block(0)
                round_all(hn)
                round_block(1)
                for n in range(BLOCKS):
                    act.wait_ge(used, n + 1)
                    g, j = n // 4, n % 4
                    if n == HEADS - 1:
                        round_all(hk)
                    if n < TILES:
                        dst = (Q if g < 2 else K)[:, n % HEADS, :]
                        act.activation(dst, ps[:, n % 8, :], ACT.Copy).then_inc(copied, 1)
                    if n + 2 < BLOCKS:
                        round_block(n + 2)
                    if n < TILES:
                        if g:
                            act.wait_ge(summed, 4 * (g - 1) + j + 1)
                        act.activation(sq[:, j, :], ps[:, n % 8, :], ACT.Square).then_inc(squared, 1)
                    for m in sums_after.get(n, ()):
                        root(m)
                for n in range(0, 8, 2):
                    act.activation(mix[:, n, :], ps[:, n, :], ACT.Copy).then_inc(v_kept, 1)

            @block.vector
            def _(ve):
                def rest_of_all(src, before):
                    for k in range(KT):
                        ve.wait_ge(h_rounded, before + k + 1)
                        ve.tensor_tensor(h_lo[:, k, :], src[:, k, :], h_hi[:, k, :].bitcast(F32), ALU.subtract
                                         ).then_inc(h_split, 1)

                def rest_of_block(n):
                    ve.wait_ge(w_rounded, n + 1)
                    ve.tensor_tensor(w_lo[:, n % 2, :], ring[:, (B2 + n) % SLOTS, :], w_hi[:, n % 2, :].bitcast(F32),
                                     ALU.subtract).then_inc(blocks_done, 1)

                def normalise(n):
                    dst, gain = (Q, col("qgain")) if n < HEADS else (K, col("kgain"))
                    ve.wait_ge(rooted, n + 1)
                    ve.reciprocal(roots[n % 8], roots[n % 8]).then_inc(inverted, 1)
                    ve.wait_ge(inverted, n + 1)
                    d = dst[:, n % HEADS, :]
                    ve.scalar_tensor_tensor(d, d, gain, roots[n % 8], ALU.mult, ALU.mult).then_inc(normed, 1)
                rest_of_block(0)
                rest_of_all(hn, 0)
                rest_of_block(1)
                for n in range(BLOCKS):
                    g, j = n // 4, n % 4
                    if n == HEADS - 1:
                        rest_of_all(hk, KT)
                    if n + 2 < BLOCKS:
                        rest_of_block(n + 2)
                    for m in sums_after.get(n, ()):
                        ve.wait_ge(summed, m + 1)
                        if m >= HEADS:
                            ve.wait_ge(normed, m - HEADS + 1)
                        ve.tensor_scalar(roots[m % 8], ps[:, m % 8, :], 1.0 / P, EPS, ALU.mult, ALU.add
                                         ).then_inc(mean_read, 1)
                    if 6 <= n < TILES + 6:
                        normalise(n - 6)
                ve.wait_ge(used, BLOCKS)
                for n in range(1, 8, 2):
                    ve.tensor_copy(mix[:, n, :], ps[:, n, :]).then_inc(v_kept, 1)
        st.close()

        WIDTH = [T - a * P for a in range(TT)]
        OFF = [sum(WIDTH[:a]) for a in range(TT)]
        PACKED = sum(WIDTH)
        scale = float(P) ** -0.5
        st = sbt.enter_context(ExitStack())
        ks = sb("a_ks", [P, 2, T], on=st)
        vs = sb("a_vs", [P, 2, TT, P], on=st)
        lo, sp_, ln = (sb(f"a_{n}", [P, 2, PACKED], on=st) for n in ("lo", "sp", "ln"))
        names = ("staged", "z_done", "abs_done", "ln_done", "z_read", "summed", "fail_ready", "rest_done", "log_a",
                 "exp_done", "att_ready", "o_done", "o_kept")
        A = {n: [sem(f"a_{n}{u}") for u in range(2)] for n in names}
        with nc.Block() as block:
            @block.scalar
            def _(act):
                with act.Fori(0, HEADS // 2) as i:
                    heads = [bass.ds(i * 2 + u, 1) for u in range(2)]
                    for u in range(2):
                        act.wait_ge(A["o_done"][u], i + 1)
                        apart(act)
                        act.activation(ks[:, u, :], flat(K[:, heads[u], :]), ACT.Copy).then_inc(A["staged"][u], 1)
                        act.activation(vs[:, u, :, :], V[:, :, heads[u], :].rearrange("p t a d -> p t (a d)"), ACT.Copy
                                       ).then_inc(A["staged"][u], 1)
                    for u in range(2):
                        act.wait_ge(A["z_done"][u], i + 2)
                        for a in range(TT):
                            act.activation(ln[:, u, OFF[a]:OFF[a] + WIDTH[a]], ps[:, 4 * u + a, 0:WIDTH[a]], ACT.Abs,
                                           scale=scale).then_inc(A["abs_done"][u], 1)
                    for u in range(2):
                        act.wait_ge(A["abs_done"][u], i * 4 + 4 + 1)
                        act.activation(ln[:, u, :], ln[:, u, :], ACT.Exp, scale=-1.0).then_inc(A["ln_done"][u], 1)
                        act.wait_ge(A["ln_done"][u], i * 2 + 2)
                        act.activation(ln[:, u, :], ln[:, u, :], ACT.Ln, bias=1.0).then_inc(A["ln_done"][u], 1)
                    for u in range(2):
                        act.wait_ge(A["log_a"][u], i * 4 + 4 + 1)
                        act.activation(lo[:, u, :], lo[:, u, :], ACT.Exp).then_inc(A["exp_done"][u], 1)
                    for u in range(2):
                        act.wait_ge(A["o_done"][u], i + 2)
                        apart(act)
                        act.activation(flat(Q[:, heads[u], :]), ps[:, 4 * u, :], ACT.Copy).then_inc(A["o_kept"][u], 1)

            @block.gpsimd
            def _(pool):
                credit(pool, A.values())
                with pool.Fori(0, HEADS // 2) as i:
                    for u in range(2):
                        pool.wait_ge(A["summed"][u], i * 2 + 2 + 1)
                        for a in range(TT):
                            d = sp_[:, u, OFF[a]:OFF[a] + P]
                            pool.tensor_tensor(d, d, tab[:, TABLES["strict"]], ALU.mult).then_inc(A["fail_ready"][u], 1)
                    for u in range(2):
                        pool.wait_ge(A["exp_done"][u], i + 2)
                        for a in range(TT):
                            d = lo[:, u, OFF[a]:OFF[a] + P]
                            pool.tensor_tensor(d, d, tab[:, TABLES["strict"]], ALU.mult).then_inc(A["att_ready"][u], 1)

            @block.vector
            def _(ve):
                with ve.Fori(0, HEADS // 2) as i:
                    for u in range(2):
                        ve.wait_ge(A["o_done"][u], i + 1)
                        for a in range(TT):
                            c = slice(OFF[a], OFF[a] + WIDTH[a])
                            z = ps[:, 4 * u + a, 0:WIDTH[a]]
                            ve.wait_ge(A["abs_done"][u], i * 4 + a + 2)
                            ve.tensor_scalar(lo[:, u, c], z, scale, 0.0, ALU.mult, ALU.min).then_inc(A["z_read"][u], 1)
                            ve.tensor_scalar(sp_[:, u, c], z, scale, 0.0, ALU.mult, ALU.max).then_inc(A["z_read"][u], 1)
                    for u in range(2):
                        ve.wait_ge(A["z_read"][u], i * 8 + 8 + 1)
                        ve.wait_ge(A["ln_done"][u], i * 2 + 2 + 1)
                        ve.tensor_tensor(sp_[:, u, :], sp_[:, u, :], ln[:, u, :], ALU.add).then_inc(A["summed"][u], 1)
                        ve.tensor_tensor(lo[:, u, :], lo[:, u, :], ln[:, u, :], ALU.subtract).then_inc(A["summed"][u], 1)
                    for u in range(2):
                        ve.wait_ge(A["summed"][u], i * 2 + 2 + 1)
                        ve.wait_ge(A["rest_done"][u], i + 2)
                        for a in range(TT):
                            c = slice(OFF[a], OFF[a] + WIDTH[a])
                            ve.tensor_tensor(lo[:, u, c], lo[:, u, c], ps[:, 4 * u + a, 0:WIDTH[a]], ALU.subtract
                                             ).then_inc(A["log_a"][u], 1)

            @block.tensor
            def _(pe):
                with pe.Fori(0, HEADS // 2) as i:
                    heads = [bass.ds(i * 2 + u, 1) for u in range(2)]
                    for u in range(2):
                        pe.wait_ge(A["staged"][u], i * 2 + 2 + 1)
                        pe.wait_ge(A["o_kept"][u], i + 1)
                        for a in range(TT):
                            m = pe.matmul(ps[:, 4 * u + a, 0:WIDTH[a]], ks[:, u, a * P:(a + 1) * P],
                                          flat(Q[:, heads[u], a * P:T]), start=True, stop=True)
                        m.then_inc(A["z_done"][u], 1)
                    for u in range(2):
                        pe.wait_ge(A["fail_ready"][u], i * 4 + 4 + 1)
                        for a in range(TT):
                            for b in range(a, TT):
                                m = pe.matmul(ps[:, 4 * u + a, (b - a) * P:WIDTH[a]],
                                              tab[:, TABLES["after"]] if a == b else ones,
                                              sp_[:, u, OFF[b]:OFF[b] + WIDTH[b]], start=a == b, stop=a == b,
                                              skip_group_check=a != b)
                        m.then_inc(A["rest_done"][u], 1)
                    for u in range(2):
                        pe.wait_ge(A["att_ready"][u], i * 4 + 4 + 1)
                        for a in range(TT):
                            m = pe.matmul(ps[:, 4 * u, a * P:T], vs[:, u, a, :], lo[:, u, OFF[a]:OFF[a] + WIDTH[a]],
                                          start=a == 0, stop=a == 0, skip_group_check=a != 0)
                        m.then_inc(A["o_done"][u], 1)
        st.close()
        fast_project_out("sbout", Q, STREAM["sbout"].start, None, STREAM["gu1"].start + SLOTS)
        sbt.close()
        feed_forward(1)
        stored = sem("stored")
        with nc.Block() as block:
            @block.sync
            def _(sp):
                sp.dma_start(outT.rearrange("(k p) t -> p k t", p=P), res[:, :, :]).then_inc(stored, 16)
                sp.wait_ge(stored, 16)

def kernel(**inputs):
    import concourse.bacc as bacc
    from concourse.bass_utils import run_bass_kernel_spmd

    a = {k: np.asarray(v) for k, v in inputs.items()}

    def by_tile(w):
        return w.reshape(KT, P, -1, P).transpose(2, 1, 0, 3).reshape(-1, P, 1024)

    def by_row(w):
        return w.reshape(-1, P, 1024)

    def pairs(w):
        return w.reshape(4, 2, P, 512).transpose(0, 2, 1, 3).reshape(4, P, 1024)

    def column(v):
        return v.reshape(-1, P).T

    w_in, gdn = a["w_in"][0], a["gdn_w_in_2"][0]
    ei = a["w_expert_in"][0].reshape(NEXP, KT, P, 512).transpose(0, 2, 1, 3).reshape(NEXP, P, -1)
    eo = a["w_expert_out"][0].reshape(NEXP, 2, P, D).transpose(0, 2, 1, 3).reshape(NEXP, P, -1)
    gt = by_tile(gdn[:, :4096]).reshape(2, 2, 4, 2, P, 1024).transpose(2, 0, 3, 1, 4, 5)
    gu = [by_tile(w).reshape(2, FT, P, 1024).transpose(1, 0, 2, 3).reshape(-1, P, 1024) for w in a["ffn_w_gu_2"]]
    ada = a["w_ada"][0].reshape(KT, P, 6, D).transpose(2, 0, 1, 3).reshape(-1, P, D)
    stream = np.concatenate([
        ada[:16], by_tile(w_in[:, 256:512]), pairs(w_in[:, 512:1024]), by_tile(w_in[:, 0:256]),
        by_tile(w_in[:, 1024:1536]), pairs(w_in[:, 1568:2080]), ada[16:], by_tile(a["w_out"][0]),
        gt.reshape(-1, P, 1024),
        by_tile(a["gdn_w_out_2"][0]), gu[0], by_row(a["ffn_w_down_2"][0]), by_tile(a["sb_w_q_2"][0]),
        by_tile(a["w_kv_2"][:, :D]), by_row(a["w_kv_2"][:, D:]), by_tile(a["sb_w_out_2"][0]), gu[1],
        by_row(a["ffn_w_down_2"][1])])
    small = np.concatenate([
        w_in[:, 1536:1568].reshape(KT, P, 32).transpose(1, 0, 2).reshape(P, -1),
        gdn[:, 4096:4112].reshape(KT, P, 16).transpose(1, 0, 2).reshape(P, -1),
        np.concatenate([a["w_router_group"][0], a["w_router_expert"][0]], axis=1).reshape(KT, P, 36)
        .transpose(1, 0, 2).reshape(P, -1),
        a["w_pool"][0].transpose(1, 0, 2).reshape(P, -1)], axis=1)
    params = np.concatenate([
        column(a["b_ada"][0]), column(a["norm1_g"][0]), column(a["norm2_g"][0]), column(a["final_norm_g"]),
        column(a["attn_norm_2"].reshape(-1)), column(a["ffn_norm_2"].reshape(-1)), column(a["kv_norm_2"]),
        column(a["gla_norm_g"][0]), column(a["pool_scale"][0]), column(a["b_decay"][0].reshape(-1)),
        a["gdn_conv_w_2"][0].reshape(4, 24, P).transpose(2, 1, 0).reshape(P, 96), column(a["gdn_o_gain_2"][0]),
        column(a["k_gain_2"]), column(a["sb_q_gain_2"][0]),
        np.stack([a["c"][0], a["c_ctx"]], axis=1).reshape(KT, P, 2).transpose(1, 0, 2).reshape(P, 16)], axis=1)
    arrays = {
        "xT": a["x"][0].T, "ctxT": a["ctx"][0].T, "stream": stream,
        "experts": np.concatenate([ei, eo], axis=2), "small": small, "params": params,
        "heads8": np.stack([a["gdn_a_log_2"][0], a["gdn_dt_bias_2"][0]], axis=1), "wdec": a["w_decay"][0],
        "table": tables(), "windows": window_blocks()[0]}
    arrays = {k: np.ascontiguousarray(v) for k, v in arrays.items()}
    nc = bacc.Bacc("TRN2", target_bir_lowering=False, num_devices=1)
    aps = [nc.dram_tensor(k, v.shape, F32, kind="ExternalInput").ap() for k, v in arrays.items()]
    out = nc.dram_tensor("outT", (D, T), F32, kind="ExternalOutput").ap()
    program(nc, *aps, out)
    r = run_bass_kernel_spmd(nc, [arrays], core_ids=[0])
    return np.ascontiguousarray(r.results[0]["outT"].T)[None]
```
